# Optimizing a Trainium2 kernel written in Bass

```python
import jax, jax.numpy as jnp
from jax import lax
import numpy as np

D_MODEL = 1024
BATCH = 1
SEQ = 128
DEPTH = 2
DEC_BATCH = 1
DEC_SEQ = 512
PAST_LEN = 128

GRID_W = 64
N_MIXERS = 2
N_MLA = (DEPTH + 1) // 2
N_CONV = DEPTH // 2
N_HEADS = 8
Q_LORA = 512
KV_LORA = 256
QK_NOPE = 128
QK_ROPE = 64
QK_DIM = QK_NOPE + QK_ROPE
V_DIM = 128
ROPE_THETA = 10000.0
CONV_WIDTH = 31
CONV_PAD = (CONV_WIDTH - 1) // 2
D_FF = ((8 * D_MODEL // 3 + 255) // 256) * 256
Q_BLOCK = 128
EPS = 1e-6

kernel_name = "hybrid_mla_conformer_diffusion_step"

def rms_norm(x, g):
    xf = x.astype(jnp.float32)
    y = xf * lax.rsqrt(jnp.mean(xf * xf, axis=-1, keepdims=True) + EPS)
    return (y * g.astype(jnp.float32)).astype(x.dtype)

def layer_norm(x, g, b):
    xf = x.astype(jnp.float32)
    mu = jnp.mean(xf, axis=-1, keepdims=True)
    var = jnp.mean(jnp.square(xf - mu), axis=-1, keepdims=True)
    y = (xf - mu) * lax.rsqrt(var + EPS)
    return (y * g.astype(jnp.float32) + b.astype(jnp.float32)).astype(x.dtype)

def modulation(cond, w_mod, b_mod):
    m = jax.nn.silu(cond) @ w_mod + b_mod
    return jnp.split(m[..., None, :], 6, axis=-1)

def axial_rope_tables(T):
    rows = T // GRID_W
    t = jnp.arange(T)
    row = jnp.repeat(jnp.arange(rows), GRID_W).astype(jnp.float32)
    col = (t % GRID_W).astype(jnp.float32)
    ax = QK_ROPE // 2
    inv = 1.0 / (ROPE_THETA ** (jnp.arange(0, ax, 2, dtype=jnp.float32) / ax))
    ar = row[:, None] * inv[None, :]
    ac = col[:, None] * inv[None, :]
    cos = jnp.concatenate([jnp.cos(ar), jnp.cos(ar), jnp.cos(ac), jnp.cos(ac)], axis=-1)
    sin = jnp.concatenate([jnp.sin(ar), jnp.sin(ar), jnp.sin(ac), jnp.sin(ac)], axis=-1)
    return cos, sin

def apply_rope(x, cos, sin):
    nope, pe = x[..., :QK_NOPE], x[..., QK_NOPE:].astype(jnp.float32)
    r1, r2, c1, c2 = jnp.split(pe, 4, axis=-1)
    rot = jnp.concatenate([-r2, r1, -c2, c1], axis=-1)
    pe = pe * cos[None, :, None, :] + rot * sin[None, :, None, :]
    return jnp.concatenate([nope, pe.astype(x.dtype)], axis=-1)

def mla_compress(h, w_dq, q_norm, w_uq, w_dkv, kv_norm, q_hn):
    B, T, _ = h.shape
    cq = rms_norm(h @ w_dq, q_norm)
    q = rms_norm((cq @ w_uq).reshape(B, T, N_HEADS, QK_DIM), q_hn)
    kv = h @ w_dkv
    ckv = rms_norm(kv[..., :KV_LORA], kv_norm)
    kpe = kv[..., KV_LORA:]
    return q, ckv, kpe

def mla_expand(ckv, kpe, w_ukv, k_hn):
    B, T, _ = ckv.shape
    kvu = (ckv @ w_ukv).reshape(B, T, N_HEADS, QK_NOPE + V_DIM)
    k_nope, v = kvu[..., :QK_NOPE], kvu[..., QK_NOPE:]
    k_pe = jnp.broadcast_to(kpe[:, :, None, :], (B, T, N_HEADS, QK_ROPE))
    k = rms_norm(jnp.concatenate([k_nope, k_pe], axis=-1), k_hn)
    return k, v

def block_attention(q, k, v):
    B, T, H, Dk = q.shape
    nb = T // Q_BLOCK
    qb = q.reshape(B, nb, Q_BLOCK, H, Dk).transpose(1, 0, 2, 3, 4)
    scale = Dk ** -0.5

    def one_block(qblk):
        s = jnp.einsum('bqhd,bkhd->bhqk', qblk, k).astype(jnp.float32) * scale
        p = jax.nn.softmax(s, axis=-1).astype(v.dtype)
        return jnp.einsum('bhqk,bkhd->bqhd', p, v)

    o = lax.map(one_block, qb)
    return o.transpose(1, 0, 2, 3, 4).reshape(B, T, H * V_DIM)

def conformer_conv(h, w_pw1, b_pw1, w_dw, b_dw, ln_g, ln_b, w_pw2, b_pw2):
    a = h @ w_pw1 + b_pw1
    g = a[..., :D_MODEL] * jax.nn.sigmoid(a[..., D_MODEL:])
    y = lax.conv_general_dilated(
        g, w_dw[:, None, :].astype(g.dtype), window_strides=(1,),
        padding=[(CONV_PAD, CONV_PAD)], dimension_numbers=('NWC', 'WIO', 'NWC'),
        feature_group_count=D_MODEL) + b_dw
    y = jax.nn.silu(layer_norm(y, ln_g, ln_b))
    return y @ w_pw2 + b_pw2

def swiglu(h, w_gate, w_up, w_down):
    return (jax.nn.silu(h @ w_gate) * (h @ w_up)) @ w_down

def setup_inputs(seed: int = 0) -> dict:
    key = jax.random.key(seed)
    ks = iter(jax.random.split(key, 64))
    f32 = jnp.float32

    def w(shape, fan_in, mult=1.0):
        return jax.random.normal(next(ks), shape, f32) * (mult * fan_in ** -0.5)

    def gain(shape):
        return 1.0 + 0.02 * jax.random.normal(next(ks), shape, f32)

    def bias(shape):
        return 0.01 * jax.random.normal(next(ks), shape, f32)

    D = D_MODEL
    return {
        "x_prompt": jax.random.normal(next(ks), (BATCH, SEQ, D), f32),
        "x_sample": jax.random.normal(next(ks), (DEC_BATCH, DEC_SEQ, D), f32),
        "cache_ckv": jax.random.normal(next(ks), (DEC_BATCH, N_MLA, PAST_LEN, KV_LORA), f32),
        "cache_kpe": jax.random.normal(next(ks), (DEC_BATCH, N_MLA, PAST_LEN, QK_ROPE), f32),
        "c": jax.random.normal(next(ks), (DEC_BATCH, D), f32),
        "c_ctx": jax.random.normal(next(ks), (D,), f32),
        "w_mod": w((DEPTH, D, 6 * D), D, 0.5),
        "b_mod": bias((DEPTH, 6 * D)),
        "norm_mix": gain((DEPTH, D)),
        "norm_ffn": gain((DEPTH, D)),
        "mla_w_dq": w((N_MLA, D, Q_LORA), D),
        "mla_q_norm": gain((N_MLA, Q_LORA)),
        "mla_w_uq": w((N_MLA, Q_LORA, N_HEADS * QK_DIM), Q_LORA),
        "mla_w_dkv": w((N_MLA, D, KV_LORA + QK_ROPE), D),
        "mla_kv_norm": gain((N_MLA, KV_LORA)),
        "mla_w_ukv": w((N_MLA, KV_LORA, N_HEADS * (QK_NOPE + V_DIM)), KV_LORA),
        "mla_q_hnorm": gain((N_MLA, QK_DIM)),
        "mla_k_hnorm": gain((N_MLA, QK_DIM)),
        "mla_w_o": w((N_MLA, N_HEADS * V_DIM, D), N_HEADS * V_DIM),
        "conv_w_pw1": w((N_CONV, D, 2 * D), D),
        "conv_b_pw1": bias((N_CONV, 2 * D)),
        "conv_w_dw": w((N_CONV, CONV_WIDTH, D), CONV_WIDTH),
        "conv_b_dw": bias((N_CONV, D)),
        "conv_ln_g": gain((N_CONV, D)),
        "conv_ln_b": bias((N_CONV, D)),
        "conv_w_pw2": w((N_CONV, D, D), D),
        "conv_b_pw2": bias((N_CONV, D)),
        "ffn_w_gate": w((DEPTH, D, D_FF), D),
        "ffn_w_up": w((DEPTH, D, D_FF), D),
        "ffn_w_down": w((DEPTH, D_FF, D), D_FF),
    }

def reference(x_prompt, x_sample, cache_ckv, cache_kpe, c, c_ctx,
              w_mod, b_mod, norm_mix, norm_ffn,
              mla_w_dq, mla_q_norm, mla_w_uq, mla_w_dkv, mla_kv_norm, mla_w_ukv,
              mla_q_hnorm, mla_k_hnorm, mla_w_o,
              conv_w_pw1, conv_b_pw1, conv_w_dw, conv_b_dw, conv_ln_g, conv_ln_b,
              conv_w_pw2, conv_b_pw2,
              ffn_w_gate, ffn_w_up, ffn_w_down):
    xp = x_prompt
    xs = x_sample
    cos, sin = axial_rope_tables(xs.shape[1])
    new_ckv, new_kpe = [], []

    for l in range(DEPTH):
        sh1_c, sc1_c, g1_c, sh2_c, sc2_c, g2_c = modulation(c_ctx, w_mod[l], b_mod[l])
        sh1_s, sc1_s, g1_s, sh2_s, sc2_s, g2_s = modulation(c, w_mod[l], b_mod[l])
        hp = rms_norm(xp, norm_mix[l]) * (1.0 + sc1_c) + sh1_c
        hs = rms_norm(xs, norm_mix[l]) * (1.0 + sc1_s) + sh1_s
        j = l // N_MIXERS

        if l % N_MIXERS == 0:
            args = (mla_w_dq[j], mla_q_norm[j], mla_w_uq[j], mla_w_dkv[j],
                    mla_kv_norm[j], mla_q_hnorm[j])
            qp, ckv_p, kpe_p = mla_compress(hp, *args)
            kp, vp = mla_expand(ckv_p, kpe_p, mla_w_ukv[j], mla_k_hnorm[j])
            op = block_attention(qp, kp, vp) @ mla_w_o[j]
            new_ckv.append(ckv_p)
            new_kpe.append(kpe_p)
            qs, ckv_s, kpe_s = mla_compress(hs, *args)
            qs = apply_rope(qs, cos, sin)
            ks_, vs_ = mla_expand(ckv_s, kpe_s, mla_w_ukv[j], mla_k_hnorm[j])
            ks_ = apply_rope(ks_, cos, sin)
            kc, vc = mla_expand(cache_ckv[:, j], cache_kpe[:, j], mla_w_ukv[j], mla_k_hnorm[j])
            os_ = block_attention(qs, jnp.concatenate([kc, ks_], axis=1),
                                  jnp.concatenate([vc, vs_], axis=1)) @ mla_w_o[j]
        else:
            cargs = (conv_w_pw1[j], conv_b_pw1[j], conv_w_dw[j], conv_b_dw[j],
                     conv_ln_g[j], conv_ln_b[j], conv_w_pw2[j], conv_b_pw2[j])
            op = conformer_conv(hp, *cargs)
            os_ = conformer_conv(hs, *cargs)

        xp = xp + g1_c * op
        xs = xs + g1_s * os_

        hp = rms_norm(xp, norm_ffn[l]) * (1.0 + sc2_c) + sh2_c
        hs = rms_norm(xs, norm_ffn[l]) * (1.0 + sc2_s) + sh2_s
        xp = xp + g2_c * swiglu(hp, ffn_w_gate[l], ffn_w_up[l], ffn_w_down[l])
        xs = xs + g2_s * swiglu(hs, ffn_w_gate[l], ffn_w_up[l], ffn_w_down[l])

    state_ckv = jnp.stack(new_ckv, axis=1)
    state_kpe = jnp.stack(new_kpe, axis=1)
    return (xp, xs, state_ckv, state_kpe)


_drawn_inputs = setup_inputs


def setup_inputs(seed=0):
    import zlib

    import numpy as np

    out = dict(_drawn_inputs(seed))
    spreads = {}
    factors = {'cache_ckv': 6.065,
     'cache_kpe': 8.0,
     'b_mod': 4.171,
     'norm_mix': 2.968,
     'norm_ffn': 6.611,
     'mla_q_norm': 8.0,
     'mla_kv_norm': 2.949,
     'mla_q_hnorm': 8.0,
     'mla_k_hnorm': 8.0,
     'conv_b_pw1': 64.0,
     'conv_b_dw': 52.423,
     'conv_ln_g': 64.0,
     'conv_ln_b': 64.0,
     'conv_b_pw2': 64.0}
    for name, (base, spread) in spreads.items():
        noise = np.random.default_rng([zlib.crc32(name.encode()), seed]).standard_normal(out[name].shape)
        drawn = base * np.exp(spread * noise) if base else spread * noise
        out[name] = __import__('jax').numpy.asarray(drawn.astype(out[name].dtype))
    for name, factor in factors.items():
        out[name] = (out[name] * factor).astype(out[name].dtype)
    return out
```

```python
from contextlib import ExitStack

import numpy as np

import concourse.bass as bass
from concourse import mybir

P = 128
F32 = mybir.dt.float32
F32R = mybir.dt.float32r
I32 = mybir.dt.int32
ALU = mybir.AluOpType
ACT = mybir.ActivationFunctionType

CTX, LAT = 128, 512
TOK = CTX + LAT
PAST = 128
KEYS = CTX + PAST + LAT
D = 1024
KT = D // P
HALF = TOK // 2
HEADS, NOPE, ROPE, VD = 8, 128, 64, 128
QK = NOPE + ROPE
QL, KVL = 512, 256
QLT, KVT = QL // P, KVL // P
FF = 2816
FT = FF // P
TAPS, PAD = 31, 15
GRID_W = 64
THETA = 10000.0
EPS = 1e-6
RUN = CTX + PAD + LAT
GPW = RUN + 2 * PAD
QT = TOK // P
NKT = KEYS // P
DOWN_K = (8, 8, 6)
HID_SLOTS = 10
UNIT = 2048

SEGS = ((0, CTX, 0), (CTX, TOK, 1))
PSEGS = ((0, 0, CTX, 0, 0), (0, CTX, HALF, CTX, 1), (1, 0, HALF, HALF, 1))

V1 = {"b_mod": 0, "norm_mix": 96, "norm_ffn": 112}
V2, NV2 = {}, 0
for _n, _w in (("q_norm", 4), ("kv_norm", 2), ("b_pw1", 16), ("b_dw", 8), ("ln_g", 8), ("ln_b", 8),
               ("b_pw2", 8), ("c", 8), ("c_ctx", 8), ("gq", 1), ("gk", 1), ("gq_pe", 1), ("gk_pe", 1)):
    V2[_n] = NV2
    NV2 += _w


def rope_tables():
    t = np.arange(LAT)
    ax = ROPE // 2
    inv = (1.0 / (THETA ** (np.arange(0, ax, 2, dtype=np.float32) / np.float32(ax)))).astype(np.float32)
    ar = (t // GRID_W).astype(np.float32)[:, None] * inv[None, :]
    ac = (t % GRID_W).astype(np.float32)[:, None] * inv[None, :]
    cos = np.concatenate([np.cos(ar), np.cos(ar), np.cos(ac), np.cos(ac)], axis=1).T
    sin = np.concatenate([np.sin(ar), np.sin(ar), np.sin(ac), np.sin(ac)], axis=1).T
    rot = np.zeros((P, P), np.float32)
    q = ROPE // 4
    for b in range(0, P, ROPE // 2):
        for i in range(q):
            rot[b + q + i, b + i] = -1.0
            rot[b + i, b + q + i] = 1.0
    return (np.concatenate([cos, cos]).astype(np.float32), np.concatenate([sin, sin]).astype(np.float32), rot)


MT = 24
FIRST_BG = 5
N_HALF = 2 * (12 - FIRST_BG)
BG_STEPS = 12
BG_SLOTS = 6


def half_pair(j):
    return min((KT * j + KT - 1) // BG_STEPS + 1, FT // 2)


def tile_order():
    o = ["vec"] + [("x", k) for k in range(KT)]
    norm = lambda n: [("stat", n), ("rb", n)]
    o += [("stat", "mix0"), "taps", "cache", ("rb", "mix0"), ("mod", 0), ("mod", 1)]
    o += [("dq", m) for m in range(QLT)] + [("dkv", m) for m in range(KVT + 1)]
    o += norm("cq") + norm("ck") + ["kpstat", "kprot", "ctxout"]
    even = lambda h, *n: [(x, h) for x in n] if h % 2 == 0 else []
    qk = lambda h: [("qn", h), *even(h, "pe"), ("kn", h), *even(h, "rot"), ("hstat", h)]
    o += qk(0) + [("v", 0), ("rk", 0)]
    for h in range(HEADS):
        o += [("s", h, t) for t in range(QT)]
        if h + 1 < HEADS:
            o += qk(h + 1)
        o += [("mt", 3 * h)] + [("pt", h, t) for t in range(QT)] + [("mt", 3 * h + 1)] + [("o", h, g) for g in range(3)]
        if h + 1 < HEADS:
            o += [("v", h + 1)]
        o += [("mt", 3 * h + 2)]
        if h + 1 < HEADS:
            o += [("rk", h + 1)]
    o += [("wo", m) for m in range(KT)]

    def ffn(l):
        r = norm(f"ffn{l}")
        for kind, a, _ in ffn_steps():
            if kind == "pair":
                r += [("gate", l, a), ("gate", l, a + 1)]
                r += [("mh", j) for j in range(N_HALF) if l == 0 and half_pair(j) == a // 2]
                r += [("up", l, a), ("up", l, a + 1)]
            else:
                r += [("down", l, a, m) for m in range(KT)]
        r += [("mh", j) for j in range(N_HALF) if l == 0 and half_pair(j) == FT // 2]
        return r

    o += ffn(0) + norm("mix1")
    for i in range(KT):
        o += [("a", i), ("b", i)]
    o += ["mu"] + norm("ln") + [("pw2", m) for m in range(KT)] + ffn(1)
    o += [("y", t) for t in range(QT)]
    return {n: i for i, n in enumerate(o)}


def ffn_steps():
    steps, f = [], 0
    for c, n in enumerate(DOWN_K):
        end = sum(DOWN_K[:c + 1])
        while f < min(end + 2, FT):
            steps.append(("pair", f, 0))
            f += 2
        steps.append(("down", c, end - n))
    return steps


def program(nc, x_prompt, x_sample, cache_ckv, cache_kpe, c, c_ctx, w_mod, b_mod, norm_mix, norm_ffn,
            w_dq, q_norm, w_uq, w_dkv, kv_norm, w_ukv, q_hn, k_hn, w_o, w_pw1, b_pw1, w_dw, b_dw,
            ln_g, ln_b, w_pw2, b_pw2, w_gate, w_up, w_down, y_prompt, y_sample, new_ckv, new_kpe):
    T = tile_order()
    cos_np, sin_np, rot_np = rope_tables()
    consts = {"eye": np.eye(P, dtype=np.float32), "rot": rot_np, "cos": cos_np, "sin": sin_np}
    const = {n: nc.inline_tensor(a, name=f"const_{n}").ap() for n, a in consts.items()}

    ctx = ExitStack()
    with ctx:
        base = (nc.sbuf_base + 63) // 64 * 64
        top = [base]

        def region(nbytes):
            at = top[0]
            top[0] += nbytes
            return at

        def sb(name, shape, at, dt=F32):
            return nc.alloc_sbuf_tensor_at(name, shape, dt, offset=at)

        R_X, R_HH, R_HL = region(KT * TOK * 4), region(KT * TOK * 4), region(KT * TOK * 4)
        R_HID = region(2 * HID_SLOTS * TOK * 4)
        R_RAW, R_WH, R_WL = region(2 * UNIT * 4), region(2 * UNIT * 4), region(2 * UNIT * 4)
        R_MOD = region(2 * 1024 * 4)
        R_T = [region(TOK * 4) for _ in range(8)]
        R_P, R_PE = region(4 * TOK * 4 + CTX * 4), region(2 * TOK * 4)

        X = sb("X", [P, KT, TOK], R_X)
        HH = sb("HH", [P, KT, TOK], R_HH, F32R)
        HL = sb("HL", [P, KT, TOK], R_HL, F32R)
        HIDH = sb("HIDH", [P, HID_SLOTS, TOK], R_HID, F32R)
        HIDL = sb("HIDL", [P, HID_SLOTS, TOK], R_HID + HID_SLOTS * TOK * 4, F32R)
        RAW = sb("RAW", [P, 2, UNIT], R_RAW)
        WH = sb("WH", [P, 2, UNIT], R_WH, F32R)
        WL = sb("WL", [P, 2, UNIT], R_WL, F32R)
        MODS = sb("MODS", [P, 10, KT, P], R_HH)
        MODA = [[sb(f"MODA{i}{s}", [P, KT // 2, P], (R_WH, R_WL)[i] + (s * UNIT + 1536) * 4) for s in range(2)] for i in range(2)]
        BGW = [sb(f"BGW{i}", [P, 512], R_MOD + 2048 * i if i < 4 else R_P + 8192 + 2048 * (i - 4)) for i in range(BG_SLOTS)]
        BGACC = [sb(f"BGACC{i}", [P, 2, 512], R_P + 4096 * i) for i in range(2)]
        SQ = [sb(f"SQ{i}", [P, TOK], R_T[i]) for i in range(2)]
        TMP = [sb(f"TMP{i}", [P, TOK], R_T[2 + i]) for i in range(2)]
        ACTV = [sb(f"ACTV{i}", [P, TOK], R_T[4 + i]) for i in range(2)]
        SCALED = [TMP[0], TMP[1], SQ[0]]
        SUM = sb("SUM", [P, TOK], R_T[6])
        RSTD = sb("RSTD", [P, TOK], R_T[7])
        XROWS = sb("XROWS", [P, QT, D], R_HID)
        CROWS = sb("CROWS", [P, KVL + P], R_P)
        TAPROWS = sb("TAPROWS", [TAPS, D], R_P + 2048)
        CQH = sb("CQH", [P, QLT, TOK], R_HID, F32R)
        CQL = sb("CQL", [P, QLT, TOK], R_HID + 10240, F32R)
        CKH = sb("CKH", [P, KVT, KEYS], R_HID + 20480, F32R)
        CKL = sb("CKL", [P, KVT, KEYS], R_HID + 26624, F32R)
        KPH = sb("KPH", [P, KEYS], R_HID + 32768, F32R)
        KPL = sb("KPL", [P, KEYS], R_HID + 35840, F32R)
        CQRAW = sb("CQRAW", [P, QLT, TOK], R_HID + 38912)
        VH = sb("VH", [P, NKT, VD], R_HID + 38912, F32R)
        VL = sb("VL", [P, NKT, VD], R_HID + 41984, F32R)
        KNH = sb("KNH", [P, KEYS], R_HID + 45056, F32R)
        KNL = sb("KNL", [P, KEYS], R_HID + 48128, F32R)
        CKRAW = sb("CKRAW", [P, KVT, TOK], R_P)
        KPSQ = sb("KPSQ", [P, KEYS], R_P + 5120)
        ROPET = sb("ROPET", [P, LAT], R_P + 8192)
        KPRAW = sb("KPRAW", [P, KEYS], R_PE)
        ROPEQ = sb("ROPEQ", [P, LAT], R_T[6] + KEYS * 4)
        RK = sb("RK", [P, KEYS], R_T[6])
        KSQ = sb("KSQ", [P, KEYS], R_T[0])
        QNH = sb("QNH", [P, TOK], R_T[4], F32R)
        QNL = sb("QNL", [P, TOK], R_T[5], F32R)
        QPH = sb("QPH", [P, TOK], R_PE, F32R)
        QPL = sb("QPL", [P, TOK], R_PE + TOK * 4, F32R)
        PROB = sb("PROB", [P, 4, TOK], R_P)
        PROBC = sb("PROBC", [P, CTX], R_P + 4 * TOK * 4)
        O = sb("O", [P, HEADS, TOK], R_HH)
        PTH = sb("PTH", [P, 2, 5, 256], R_HL, F32R)
        PTL = sb("PTL", [P, 2, 5, 256], R_HL + 10240, F32R)
        OH = sb("OH", [P, HEADS, TOK], R_HID, F32R)
        OL = sb("OL", [P, HEADS, TOK], R_HL, F32R)
        COS = sb("COS", [P, LAT], R_MOD)
        SIN = sb("SIN", [P, LAT], R_MOD + LAT * 4)
        QSQ, PEG = TMP[1], TMP[0]
        PESQ = sb("PESQ", [P, TOK], R_MOD + 5376)
        CKOUT = sb("CKOUT", [P, KVL + ROPE], R_MOD + 4096)
        CKN = sb("CKN", [P, KVT, CTX], R_T[0] + 3072)
        PTCH = sb("PTCH", [P, CTX], R_T[0] + 4096, F32R)
        PTCL = sb("PTCL", [P, CTX], R_T[0] + 4608, F32R)
        DIAGN = sb("DIAGN", [P, QT, P], R_T[4])
        DIAGK = [sb(f"DIAGK{t}", [P, P], R_RAW + 1536 * 4 + (t // 4) * UNIT * 4 + (t % 4) * P * 4) for t in range(NKT)]
        ROWS = sb("ROWS", [P, P], R_PE + 3072)
        ROWS2 = sb("ROWS2", [NV2, P], R_PE + 3584)
        GP = [sb(f"GP{i}", [P, GPW], R_HID + 20480 + 2752 * i) for i in range(2)]
        YACC = [sb(f"YACC{i}", [P, RUN], R_HID + 26624 + 2688 * i) for i in range(2)]
        Y = sb("Y", [P, KT, TOK], R_HID)
        YROW = [sb(f"YROW{t}", [P, D], R_HID + 4096 * t) for t in range(QT)]

        def small(name, shape, dt=F32):
            n = 4
            for s in shape[1:]:
                n *= s
            at = region((n + 31) // 32 * 32)
            return sb(name, shape, at, dt)

        EYE = small("EYE", [P, P])
        ROT = small("ROT", [P, P])
        ONES = small("ONES", [P, P])
        VT1 = small("VT1", [P, P])
        VT2 = small("VT2", [P, NV2])
        WTAP = small("WTAP", [P, KT, TAPS])
        SC = small("SC", [P, KT, 2])
        MODV = small("MODV", [P, 2, 2, 48])
        GAIN = small("GAIN", [P, 2, 2, 2, KT])
        GB = small("GB", [P, 2, KT])
        GQK = small("GQK", [P, 1])
        RS = small("RS", [P, 4, 12])
        RSI = small("RSI", [P, 12], I32)
        KPSS = small("KPSS", [P, NKT])
        RQ = [small(f"RQ{i}", [P, QT]) for i in range(2)]
        EPSC = small("EPSC", [P, 1])
        HST = small("HST", [P, 12])
        MAX8 = small("MAX8", [P, QT])
        NB8 = small("NB8", [P, QT])
        SUM8 = small("SUM8", [P, QT])
        REC8 = small("REC8", [P, QT])
        assert top[0] <= nc.sbuf_usable_end

        PS = ctx.enter_context(nc.psum_tensor("PS", [P, 8, 512], F32))

        sems = {}

        def sem(name):
            if name not in sems:
                sems[name] = ctx.enter_context(nc.semaphore(name))
            return sems[name]

        mm_done = sem("mm_done")
        tile_read = [sem(f"tile_read{i}") for i in range(4)]
        raw_landed = [sem(f"raw_landed{i}") for i in range(2)]
        hi_done, lo_done = sem("hi_done"), sem("lo_done")
        mods_landed = [sem(f"mods_landed{i}") for i in range(10)]
        moda_landed = [sem(f"moda_landed{i}") for i in range(2)]
        bgw_landed = [sem(f"bgw_landed{i}") for i in range(BG_SLOTS)]
        modw_used = sem("modw_used")

        def tile2(name):
            s = T[name] % 4
            return PS[:, 2 * s:2 * s + 2, :]

        def free_of(name):
            return tile_read[T[name] % 4]

        def filled(eng, name):
            eng.wait_ge(mm_done, T[name] + 1)

        def was_read(eng, name):
            eng.wait_ge(free_of(name), T[name] // 4 + 1)

        def mod_tile_used(eng, i):
            chunk, j = divmod(i, KT)
            if j == KT - 1:
                filled(eng, ("mod", chunk))
            else:
                eng.wait_ge(modw_used, (KT - 1) * chunk + j + 1)

        def row2(ap):
            return ap.rearrange("p (b t) -> p b t", b=2)

        def cols(w, c0, n=256):
            return w[:, c0:c0 + n].rearrange("(k p) n -> p k n", p=P)

        units = []

        def full(kt, w, c0):
            return (kt * 256, [(lambda r, kt=kt: r[:, 0:kt * 256].rearrange("p (k n) -> p k n", k=kt), cols(w, c0))])

        for m in range(0, QLT, 2):
            units.append((("dq", m), *full(KT, w_dq[0], m * P)))
        units.append((("dkv", 0), *full(KT, w_dkv[0], 0)))
        dup = [(lambda r, i=i: r[:, 0:KT * P].rearrange("p (k n) -> p k n", k=KT)[:, :, i * ROPE:(i + 1) * ROPE],
                cols(w_dkv[0], KVL, ROPE)) for i in range(2)]
        units.append((("dkv", 2), KT * P, dup))
        for h in range(HEADS):
            v = lambda r, a, k, n: r[:, a:a + k * n].rearrange("p (k n) -> p k n", k=k)
            d = [(lambda r, v=v: v(r, 0, QLT, NOPE), cols(w_uq[0], h * QK, NOPE)),
                 (lambda r, v=v: v(r, 512, KVT, 256), cols(w_ukv[0], h * 256))]
            if h % 2 == 0:
                d += [(lambda r, v=v, i=i: v(r, 1024, QLT, P)[:, :, i * ROPE:(i + 1) * ROPE],
                       cols(w_uq[0], (h + i) * QK + NOPE, ROPE)) for i in range(2)]
            units.append((("head", h), 1536 if h % 2 == 0 else 1024, d))
        for m in range(0, KT, 2):
            units.append((("wo", m), *full(KT, w_o[0], m * P)))

        def ffn_units(l):
            for kind, a, f0 in ffn_steps():
                if kind == "pair":
                    units.append((("gate", l, a), *full(KT, w_gate[l], a * P)))
                    units.append((("up", l, a), *full(KT, w_up[l], a * P)))
                else:
                    n = DOWN_K[a]
                    for m in range(0, KT, 2):
                        units.append((("down", l, a, m), *full(n, w_down[l][f0 * P:(f0 + n) * P], m * P)))

        ffn_units(0)
        for i in range(KT):
            g = [(lambda r, j=j: r.rearrange("p (k n) -> p k n", k=KT)[:, :, j * P:(j + 1) * P],
                  cols(w_pw1[0], j * D + i * P, P)) for j in range(2)]
            units.append((("glu", i), UNIT, g))
        for m in range(0, KT, 2):
            units.append((("pw2", m), *full(KT, w_pw2[0], m * P)))
        ffn_units(1)
        U = {u[0]: i for i, u in enumerate(units)}
        landed = []
        count = [0, 0]
        for i, u in enumerate(units):
            count[i % 2] += 16 * len(u[2])
            landed.append(count[i % 2])

        LAST = {"dq": lambda n: ("dq", n[1] + 1), "dkv": lambda n: ("dkv", min(n[1] + 1, KVT)),
                "head": lambda n: ("v", n[1]), "wo": lambda n: ("wo", n[1] + 1),
                "gate": lambda n: ("gate", n[1], n[2] + 1), "up": lambda n: ("up", n[1], n[2] + 1),
                "down": lambda n: ("down", n[1], n[2], n[3] + 1), "glu": lambda n: ("b", n[1]),
                "pw2": lambda n: ("pw2", n[1] + 1)}
        unit_last = [LAST[u[0][0]](u[0]) for u in units]

        NORMS, DIAGS, nsum, ndiag = {}, {}, 0, 0
        for n, adds in (("mix0", KT), ("cq", QLT), ("ck", KVT), ("ffn0", KT), ("mix1", KT), ("mu", KT), ("ln", KT), ("ffn1", KT)):
            nsum += adds - 1
            NORMS[n] = nsum
        for n in ["mix0", "cq", "ck"] + [("rk", h) for h in range(HEADS)] + ["ffn0", "mix1", "ln", "ffn1"]:
            DIAGS[n] = ndiag
            ndiag += NKT if isinstance(n, tuple) else QT
        SQ_BASE, nsq = {}, 0
        for n, tiles in (("mix0", KT), ("cq", QLT), ("ck", KVT), ("ffn0", KT), ("mix1", KT), ("ln", KT), ("ffn1", KT)):
            SQ_BASE[n] = nsq
            nsq += tiles
        APPLY = {"mix0": 0, "ffn0": 1, "mix1": 2, "ln": 3, "ffn1": 4}

        n_vec, n_late = [0], [0]

        block = ctx.enter_context(nc.Block())

        @block.sync
        def _(sp):
            def vec(dst, src):
                sp.dma_start(dst, src).then_inc(sem("vec_landed"), 16)
                n_vec[0] += 16

            def late(dst, src):
                sp.dma_start(dst, src).then_inc(sem("late_landed"), 16)
                n_late[0] += 16

            rows = lambda a: a.rearrange("(r p) -> r p", p=P)
            flat = lambda a: a.rearrange("l n -> (l n)")
            vec(EYE[:], const["eye"])
            vec(ROWS[0:96, :], rows(flat(b_mod)))
            vec(ROWS[96:112, :], rows(flat(norm_mix)))
            vec(ROWS[112:128, :], rows(flat(norm_ffn)))
            for n, a in (("q_norm", q_norm), ("kv_norm", kv_norm), ("b_pw1", b_pw1), ("b_dw", b_dw),
                         ("ln_g", ln_g), ("ln_b", ln_b), ("b_pw2", b_pw2), ("c", c)):
                r = rows(flat(a))
                vec(ROWS2[V2[n]:V2[n] + r.shape[0], :], r)
            vec(ROWS2[V2["c_ctx"]:V2["c_ctx"] + KT, :], rows(c_ctx))
            for n, a in (("gq", q_hn), ("gk", k_hn)):
                vec(ROWS2[V2[n]:V2[n] + 1, :], a[0:1, 0:NOPE])
                for i in range(2):
                    vec(ROWS2[V2[n + "_pe"]:V2[n + "_pe"] + 1, i * ROPE:(i + 1) * ROPE], a[0:1, NOPE:QK])
            late(ROT[:], const["rot"])
            late(TAPROWS[:], w_dw[0])
            late(CROWS[:, 0:KVL], cache_ckv[0, 0])
            for i in range(2):
                late(CROWS[:, KVL + i * ROPE:KVL + (i + 1) * ROPE], cache_kpe[0, 0])

            for i, (name, _, pieces) in enumerate(units):
                if name == ("head", 0):
                    sp.dma_start(COS[:], const["cos"]).then_inc(sem("rope_landed"), 16)
                    sp.dma_start(SIN[:], const["sin"]).then_inc(sem("rope_landed"), 16)
                if name == ("wo", 0):
                    filled(sp, ("rk", HEADS - 1))
                if i >= 2:
                    sp.wait_ge(lo_done, i - 1)
                for view, src in pieces:
                    sp.dma_start(view(RAW[:, i % 2, :]), src).then_inc(raw_landed[i % 2], 16)
                if name == ("head", 2):
                    was_read(sp, "ctxout")
                    sp.dma_start(new_ckv[0, 0], CKOUT[:, 0:KVL]).then_inc(sem("stored"), 16)
                    sp.dma_start(new_kpe[0, 0], CKOUT[:, KVL:]).then_inc(sem("stored"), 16)
            for t in range(QT):
                was_read(sp, ("y", t))
                dst = y_prompt[0] if t == 0 else y_sample[0, (t - 1) * P:t * P, :]
                sp.dma_start(dst, YROW[t][:]).then_inc(sem("y_stored"), 16)
            sp.wait_ge(sem("stored"), 32)
            sp.wait_ge(sem("y_stored"), 16 * QT)

        @block.gpsimd
        def _(pool):
            for i in range(2 * KT):
                if i >= 10:
                    mod_tile_used(pool, i - 10)
                pool.dma_start(MODS[:, i % 10], cols(w_mod[0], i * P, P)).then_inc(mods_landed[i % 10], 16)
            filled(pool, ("dkv", 1))
            for i in range(MT):
                if i >= 2:
                    filled(pool, ("mt", i - 2))
                src = cols(w_mod[0], 2 * D + i * P, P)
                for s in range(2):
                    pool.dma_start(MODA[i % 2][s][:], src[:, s * KT // 2:(s + 1) * KT // 2]).then_inc(moda_landed[i % 2], 16)
            filled(pool, ("o", HEADS - 1, 2))
            pool.wait_ge(sem("stored"), 32)
            for i in range(N_HALF * KT):
                j, k = divmod(i, KT)
                if i >= BG_SLOTS:
                    pool.wait_ge(sem("bgw_used"), i - BG_SLOTS + 1)
                l, c0 = divmod(FIRST_BG * D + j * 512, 6 * D)
                pool.dma_start(BGW[i % BG_SLOTS][:], w_mod[l, k * P:(k + 1) * P, c0:c0 + 512]).then_inc(bgw_landed[i % BG_SLOTS], 16)

        @block.tensor
        def _(pe):
            mm = nc.tensor.matmul
            n_mod = [0]
            n_unit = [0]

            def begin(name):
                n = T[name]
                if n >= 4:
                    pe.wait_ge(tile_read[n % 4], n // 4)
                return tile2(name)

            def split3(outs, wh, wl, xs, first, last):
                for o, (xh, xl) in zip(outs, xs):
                    mm(o, wh, xh, start=first, stop=False)
                for o, (xh, xl) in zip(outs, xs):
                    mm(o, wh, xl, start=False, stop=False)
                ins = None
                for o, (xh, xl) in zip(outs, xs):
                    ins = mm(o, wl, xh, start=False, stop=last)
                return ins

            def halves(ps, n=HALF):
                return [ps[:, 0, 0:n], ps[:, 1, 0:n]]

            def unit_begin(name):
                assert U[name] == n_unit[0], name
                pe.wait_ge(lo_done, n_unit[0] + 1)
                s = n_unit[0] % 2
                n_unit[0] += 1
                return WH[:, s, :], WL[:, s, :]

            def product(name, w, a, kt, step, xh, xl, n=HALF, wait=None):
                ps = begin(name)
                o = halves(ps, n)
                for k in range(kt):
                    if wait is not None:
                        wait(k)
                    wa = a + k * step
                    ins = split3(o, w[0][:, wa:wa + P], w[1][:, wa:wa + P],
                                 [(xh[:, k, i * n:(i + 1) * n], xl[:, k, i * n:(i + 1) * n]) for i in range(2)],
                                 k == 0, k == kt - 1)
                return ins

            def modulation(chunk):
                ps = begin(("mod", chunk))
                for j in range(KT):
                    i = n_mod[0]
                    pe.wait_ge(mods_landed[i % 10], 16 * (i // 10 + 1))
                    for k in range(KT):
                        ins = mm(ps[:, 0, 2 * j:2 * j + 2], MODS[:, i % 10, k, :], SC[:, k, :], start=(k == 0), stop=(k == KT - 1))
                    ins.then_inc(modw_used if j < KT - 1 else mm_done, 1)
                    n_mod[0] += 1

            def mod_tile(i):
                ps = begin(("mt", i))
                pe.wait_ge(moda_landed[i % 2], 32 * (i // 2 + 1))
                for k in range(KT):
                    ins = mm(ps[:, 0, 0:2], MODA[i % 2][k // 4][:, k % 4, :], SC[:, k, :], start=(k == 0), stop=(k == KT - 1))
                ins.then_inc(mm_done, 1)

            def mod_half(j):
                ps = begin(("mh", j))
                pe.wait_ge(sem("bgw_used"), KT * (j + 1))
                for c in range(4):
                    for s in range(2):
                        ins = mm(ps[:, 0, 2 * c + s:2 * c + s + 1], BGACC[j % 2][:, s, c * P:(c + 1) * P], ONES[:, 0:1],
                                 start=True, stop=True)
                ins.then_inc(mm_done, 1)

            def stat(n):
                ps = begin(("stat", n))
                pe.wait_ge(sem("sq_added"), NORMS[n])
                for t in range(QT):
                    ins = mm(ps[:, 0, t:t + 1], SUM[:, t * P:(t + 1) * P], ONES[:, 0:1], start=True, stop=True)
                ins.then_inc(mm_done, 1)

            def spread(name, diags, first):
                ps = begin(name)
                for t, d in enumerate(diags):
                    pe.wait_ge(sem("diag_ready"), first + t + 1)
                    ins = mm(ps[:, t // 3, (t % 3) * P:(t % 3 + 1) * P], ONES[:], d, start=True, stop=True)
                ins.then_inc(mm_done, 1)

            diagn = [DIAGN[:, t, :] for t in range(QT)]

            pe.wait_ge(sem("vec_landed"), n_vec[0])
            pe.wait_ge(sem("ones_set"), 1)
            tr = nc.tensor.transpose
            ps = begin("vec")
            tr(ps[:, 0, 0:P], ROWS[:], EYE[:])
            tr(ps[:, 0, P:P + NV2], ROWS2[:], EYE[0:NV2, 0:NV2]).then_inc(mm_done, 1)
            pe.wait_ge(sem("x_landed"), 32)
            for k in range(KT):
                ps = begin(("x", k))
                for t in range(QT):
                    ins = tr(ps[:, t // 3, (t % 3) * P:(t % 3 + 1) * P], XROWS[:, t, k * P:(k + 1) * P], EYE[:])
                ins.then_inc(mm_done, 1)
            stat("mix0")
            pe.wait_ge(sem("late_landed"), n_late[0])
            ps = begin("taps")
            for k in range(KT):
                ins = tr(ps[:, 0, k * TAPS:(k + 1) * TAPS], TAPROWS[:, k * P:(k + 1) * P], EYE[0:TAPS, 0:TAPS])
            ins.then_inc(mm_done, 1)
            ps = begin("cache")
            for j in range(KVT + 1):
                ins = tr(ps[:, 0, j * P:(j + 1) * P], CROWS[:, j * P:(j + 1) * P], EYE[:])
            ins.then_inc(mm_done, 1)
            spread(("rb", "mix0"), diagn, DIAGS["mix0"])
            pe.wait_ge(sem("sc_ready"), 2)
            for ch in range(2):
                modulation(ch)

            h_wait = lambda n: (lambda k: pe.wait_ge(sem("h_ready"), KT * n + k + 1))
            for m in range(0, QLT, 2):
                w = unit_begin(("dq", m))
                for j in range(2):
                    ins = product(("dq", m + j), w, j * P, KT, 256, HH, HL, wait=h_wait(APPLY["mix0"]) if m + j == 0 else None)
                    ins.then_inc(mm_done, 1)
            w = unit_begin(("dkv", 0))
            for j in range(2):
                product(("dkv", j), w, j * P, KT, 256, HH, HL).then_inc(mm_done, 1)
            w = unit_begin(("dkv", 2))
            product(("dkv", 2), w, 0, KT, P, HH, HL).then_inc(mm_done, 1)
            for n in ("cq", "ck"):
                stat(n)
                spread(("rb", n), diagn, DIAGS[n])
            ps = begin("kpstat")
            pe.wait_ge(sem("kpsq_ready"), 1)
            for t in range(NKT):
                ins = mm(ps[:, 0, t:t + 1], KPSQ[0:ROPE, t * P:(t + 1) * P], ONES[0:ROPE, 0:1], start=True, stop=True)
            ins.then_inc(mm_done, 1)
            ps = begin("kprot")
            pe.wait_ge(sem("kpg_ready"), 1)
            mm(ps[:, 0, :], ROT[:], KPSQ[:, KEYS - LAT:KEYS], start=True, stop=True).then_inc(mm_done, 1)
            ps = begin("ctxout")
            pe.wait_ge(sem("ckn_ready"), KVT)
            for j in range(KVT):
                tr(ps[:, 0, j * P:(j + 1) * P], CKN[:, j, :], EYE[:])
            tr(ps[:, 0, KVL:KVL + ROPE], KPRAW[0:ROPE, 0:CTX], EYE[0:ROPE, 0:ROPE]).then_inc(mm_done, 1)

            def qk(h):
                w = unit_begin(("head", h))
                if h == 0:
                    pe.wait_ge(sem("cq_ready"), QLT)
                    pe.wait_ge(sem("ck_ready"), KVT)
                    pe.wait_ge(sem("kp_ready"), 1)
                product(("qn", h), w, 0, QLT, P, CQH, CQL).then_inc(mm_done, 1)
                if h % 2 == 0:
                    product(("pe", h), w, 1024, QLT, P, CQH, CQL).then_inc(mm_done, 1)
                product(("kn", h), w, 512, KVT, 256, CKH, CKL, n=KEYS // 2).then_inc(mm_done, 1)
                if h % 2 == 0:
                    ps = begin(("rot", h))
                    was_read(pe, ("pe", h))
                    mm(ps[:, 0, :], ROT[:], PEG[:, CTX:TOK], start=True, stop=True).then_inc(mm_done, 1)
                ps = begin(("hstat", h))
                was_read(pe, ("qn", h))
                if h % 2 == 0:
                    was_read(pe, ("pe", h))
                lo, hi = (0, ROPE) if h % 2 == 0 else (ROPE, P)
                for t in range(QT):
                    mm(ps[:, 0, t:t + 1], QSQ[:, t * P:(t + 1) * P], ONES[:, 0:1], start=True, stop=False)
                    mm(ps[:, 0, t:t + 1], PESQ[lo:hi, t * P:(t + 1) * P], ONES[lo:hi, 0:1], start=False, stop=True)
                was_read(pe, ("kn", h))
                for t in range(NKT):
                    ins = mm(ps[:, 0, QT + t:QT + t + 1], KSQ[:, t * P:(t + 1) * P], ONES[:, 0:1], start=True, stop=True)
                ins.then_inc(mm_done, 1)

            def key_spread(h):
                spread(("rk", h), [d[:] for d in DIAGK], DIAGS[("rk", h)])

            def values(h):
                s = U[("head", h)] % 2
                ps = begin(("v", h))
                for t in range(NKT):
                    o = ps[:, t // 3, (t % 3) * P:(t % 3 + 1) * P]
                    for k in range(KVT):
                        wa = 512 + k * 256 + P
                        ks = slice(t * P, (t + 1) * P)
                        mm(o, CKH[:, k, ks], WH[:, s, wa:wa + P], start=(k == 0), stop=False)
                        mm(o, CKH[:, k, ks], WL[:, s, wa:wa + P], start=False, stop=False)
                        ins = mm(o, CKL[:, k, ks], WH[:, s, wa:wa + P], start=False, stop=(k == KVT - 1))
                ins.then_inc(mm_done, 1)

            def scores(h, t):
                ps = begin(("s", h, t))
                lo, hi = (0, ROPE) if h % 2 == 0 else (ROPE, P)
                q = slice(t * P, (t + 1) * P)
                if t == 0:
                    outs, keys = [ps[:, 0, 0:CTX]], [slice(0, CTX)]
                else:
                    outs, keys = halves(ps), [slice(CTX, CTX + 320), slice(CTX + 320, KEYS)]
                split3(outs, QNH[:, q], QNL[:, q], [(KNH[:, k], KNL[:, k]) for k in keys], True, False)
                ins = split3(outs, QPH[lo:hi, q], QPL[lo:hi, q], [(KPH[lo:hi, k], KPL[lo:hi, k]) for k in keys], False, True)
                ins.then_inc(mm_done, 1)

            def turn(h, t):
                ps = begin(("pt", h, t))
                pe.wait_ge(sem("prob_ready"), QT * h + t + 1)
                if t == 0:
                    ins = tr(ps[:, 0, 0:P], PROBC[:], EYE[:])
                else:
                    for k in range(5):
                        ins = tr(ps[:, k // 3, (k % 3) * P:(k % 3 + 1) * P], PROB[:, t - 1, k * P:(k + 1) * P], EYE[:])
                ins.then_inc(mm_done, 1)

            def weighted(h, g):
                ps = begin(("o", h, g))
                if g == 0:
                    was_read(pe, ("pt", h, 0))
                    split3([ps[:, 0, 0:P]], VH[:, 0, :], VL[:, 0, :], [(PTCH[:], PTCL[:])], True, True).then_inc(mm_done, 1)
                    return
                was_read(pe, ("pt", h, 2 * g - 1))
                was_read(pe, ("pt", h, 2 * g))
                for k in range(5):
                    ins = split3([ps[:, 0, 0:256]], VH[:, k + 1, :], VL[:, k + 1, :],
                                 [(PTH[:, g - 1, k, :], PTL[:, g - 1, k, :])], k == 0, k == 4)
                ins.then_inc(mm_done, 1)

            def head_ready(h):
                was_read(pe, ("qn", h))
                was_read(pe, ("kn", h))
                pe.wait_ge(sem("qp_ready"), h // 2 + 1)

            qk(0)
            values(0)
            key_spread(0)
            for h in range(HEADS):
                head_ready(h)
                for t in range(QT):
                    scores(h, t)
                if h + 1 < HEADS:
                    qk(h + 1)
                mod_tile(3 * h)
                for t in range(QT):
                    turn(h, t)
                mod_tile(3 * h + 1)
                was_read(pe, ("v", h))
                for g in range(3):
                    weighted(h, g)
                if h + 1 < HEADS:
                    values(h + 1)
                mod_tile(3 * h + 2)
                if h + 1 < HEADS:
                    key_spread(h + 1)

            for m in range(0, KT, 2):
                w = unit_begin(("wo", m))
                for j in range(2):
                    product(("wo", m + j), w, j * P, KT, 256, OH, OL,
                            wait=(lambda k: pe.wait_ge(sem("o_split"), k + 1)) if m + j == 0 else None).then_inc(mm_done, 1)

            def mod_halves(l, pair):
                for j in range(N_HALF):
                    if l == 0 and half_pair(j) == pair:
                        mod_half(j)

            def ffn(l):
                n = f"ffn{l}"
                stat(n)
                spread(("rb", n), diagn, DIAGS[n])
                for kind, a, f0 in ffn_steps():
                    if kind == "pair":
                        for g in ("gate", "up"):
                            if g == "up":
                                mod_halves(l, a // 2)
                            w = unit_begin((g, l, a))
                            for j in range(2):
                                product((g, l, a + j), w, j * P, KT, 256, HH, HL,
                                        wait=h_wait(APPLY[f"ffn{l}"]) if g == "gate" and a + j == 0 else None).then_inc(mm_done, 1)
                    else:
                        pe.wait_ge(sem("hid_ready"), FT * l + f0 + DOWN_K[a])
                        for m in range(0, KT, 2):
                            w = unit_begin(("down", l, a, m))
                            for j in range(2):
                                ps = begin(("down", l, a, m + j))
                                for k in range(DOWN_K[a]):
                                    hs = (f0 + k) % HID_SLOTS
                                    wa = k * 256 + j * P
                                    ins = split3(halves(ps), w[0][:, wa:wa + P], w[1][:, wa:wa + P],
                                                 [(HIDH[:, hs, i * HALF:(i + 1) * HALF], HIDL[:, hs, i * HALF:(i + 1) * HALF])
                                                  for i in range(2)], k == 0, k == DOWN_K[a] - 1)
                                ins.then_inc(mm_done, 1)

            ffn(0)
            mod_halves(0, FT // 2)
            stat("mix1")
            spread(("rb", "mix1"), diagn, DIAGS["mix1"])
            for i in range(KT):
                w = unit_begin(("glu", i))
                for j, n in enumerate(("a", "b")):
                    product((n, i), w, j * P, KT, 256, HH, HL, wait=h_wait(APPLY["mix1"]) if i + j == 0 else None).then_inc(mm_done, 1)
            ps = begin("mu")
            pe.wait_ge(sem("sq_added"), NORMS["mu"])
            for i in range(2):
                ins = mm(ps[:, i, 0:HALF], ONES[:], SUM[:, i * HALF:(i + 1) * HALF], start=True, stop=True)
            ins.then_inc(mm_done, 1)
            stat("ln")
            spread(("rb", "ln"), diagn, DIAGS["ln"])
            for m in range(0, KT, 2):
                w = unit_begin(("pw2", m))
                for j in range(2):
                    product(("pw2", m + j), w, j * P, KT, 256, HH, HL,
                            wait=h_wait(APPLY["ln"]) if m + j == 0 else None).then_inc(mm_done, 1)
            ffn(1)
            was_read(pe, ("down", 1, len(DOWN_K) - 1, KT - 2))
            was_read(pe, ("down", 1, len(DOWN_K) - 1, KT - 1))
            for t in range(QT):
                ps = begin(("y", t))
                for k in range(KT):
                    ins = tr(ps[:, k // 4, (k % 4) * P:(k % 4 + 1) * P], X[:, k, t * P:(t + 1) * P], EYE[:])
                ins.then_inc(mm_done, 1)

        @block.scalar
        def _(act):
            A = nc.scalar.activation
            n_hi = [0]
            n_sq = [0]

            def round_units(upto):
                while n_hi[0] <= min(upto, len(units) - 1):
                    u = n_hi[0]
                    act.wait_ge(raw_landed[u % 2], landed[u])
                    if u >= 2:
                        filled(act, unit_last[u - 2])
                    n = units[u][1]
                    A(WH[:, u % 2, 0:n], RAW[:, u % 2, 0:n], ACT.Copy).then_inc(hi_done, 1)
                    n_hi[0] += 1

            def square(norm, m, src, tiles=KT):
                before = NORMS[norm] - (tiles - 1)
                need = before + (max(m - 2, 1) if m >= 2 else 0)
                if need:
                    act.wait_ge(sem("sq_added"), need)
                dst = SQ[m % 2][:] if len(src.shape) == 2 else row2(SQ[m % 2][:])
                A(dst, src, ACT.Square).then_inc(sem("sq_made"), 1)

            def spread_copy(name, dst, n):
                filled(act, name)
                ps = tile2(name)
                A(dst[:, 0:3 * P], ps[:, 0, 0:3 * P], ACT.Copy)
                A(dst[:, 3 * P:n * P], ps[:, 1, 0:(n - 3) * P], ACT.Copy).then_inc(free_of(name), 1)

            def apply(norm, l, half):
                for k in range(KT):
                    act.wait_ge(sem("t_ready"), KT * APPLY[norm] + k + 1)
                    for a, b, s in SEGS:
                        ins = A(HH[:, k, a:b], SCALED[k % 3][:, a:b], ACT.Identity,
                                bias=MODV[:, l, s, 24 * half + k:24 * half + k + 1])
                    ins.then_inc(sem("part_hi"), 1)

            act.dma_start(XROWS[:, 0, :], x_prompt[0]).then_inc(sem("x_landed"), 16)
            act.dma_start(XROWS[:, 1:QT, :], x_sample[0].rearrange("(t p) d -> p t d", p=P)).then_inc(sem("x_landed"), 16)
            filled(act, "vec")
            was_read(act, "vec")
            A(SC[:, :, 0], VT2[:, V2["c_ctx"]:V2["c_ctx"] + KT], ACT.Silu).then_inc(sem("sc_ready"), 1)
            A(SC[:, :, 1], VT2[:, V2["c"]:V2["c"] + KT], ACT.Silu).then_inc(sem("sc_ready"), 1)
            for k in range(KT):
                was_read(act, ("x", k))
                square("mix0", k, X[:, k, :])
            round_units(1)
            filled(act, "cache")
            ps = tile2("cache")
            A(CKH[:, :, CTX:CTX + PAST], ps[:, 0, 0:KVL].rearrange("p (j t) -> p j t", j=KVT), ACT.Copy).then_inc(sem("cache_hi"), 1)
            spread_copy(("rb", "mix0"), RSTD, QT)
            apply("mix0", 0, 0)
            for m in range(QLT):
                if m % 2 == 0:
                    round_units(U[("dq", m)] + 1)
                filled(act, ("dq", m))
                square("cq", m, tile2(("dq", m))[:, :, 0:HALF], QLT)
                A(row2(CQRAW[:, m, :]), tile2(("dq", m))[:, :, 0:HALF], ACT.Copy).then_inc(free_of(("dq", m)), 1)
            round_units(U[("dkv", 0)] + 1)
            for m in range(KVT):
                filled(act, ("dkv", m))
                square("ck", m, tile2(("dkv", m))[:, :, 0:HALF], KVT)
                A(row2(CKRAW[:, m, :]), tile2(("dkv", m))[:, :, 0:HALF], ACT.Copy).then_inc(free_of(("dkv", m)), 1)
            round_units(U[("dkv", 2)] + 1)
            n = ("dkv", KVT)
            filled(act, n)
            for bank, a, b, t, s in PSEGS:
                to = t if s == 0 else t + PAST
                ins = A(KPRAW[:, to:to + b - a], tile2(n)[:, bank, a:b], ACT.Copy)
            ins.then_inc(free_of(n), 1)
            was_read(act, n)
            was_read(act, "cache")
            A(KPSQ[:], KPRAW[:], ACT.Square).then_inc(sem("kpsq_ready"), 1)
            spread_copy(("rb", "cq"), RSTD, QT)
            for m in range(QLT):
                act.wait_ge(sem("cq_t"), m + 1)
                A(CQH[:, m, :], TMP[m % 2][:], ACT.Copy).then_inc(sem("cq_hi"), 1)
            spread_copy(("rb", "ck"), RSTD, QT)
            for m in range(KVT):
                act.wait_ge(sem("ck_t"), m + 1)
                A(CKH[:, m, 0:CTX], TMP[m % 2][:, 0:CTX], ACT.Copy)
                A(CKH[:, m, CTX + PAST:KEYS], TMP[m % 2][:, CTX:TOK], ACT.Copy).then_inc(sem("ck_hi"), 1)
            act.wait_ge(sem("kp_rotated"), 1)
            A(KPH[:], KPSQ[:], ACT.Copy).then_inc(sem("kp_hi"), 1)
            filled(act, "ctxout")
            A(CKOUT[:], tile2("ctxout")[:, 0, 0:KVL + ROPE], ACT.Copy).then_inc(free_of("ctxout"), 1)

            def qk(h):
                round_units(U[("head", min(h + 1, HEADS - 1))])
                n = ("qn", h)
                filled(act, n)
                A(row2(QSQ[:]), tile2(n)[:, :, 0:HALF], ACT.Square)
                A(row2(QNH[:]), tile2(n)[:, :, 0:HALF], ACT.Copy, scale=GQK[:, 0:1]).then_inc(sem("qn_hi"), 1)
                if h % 2 == 0:
                    n = ("pe", h)
                    filled(act, n)
                    A(row2(PESQ[:]), tile2(n)[:, :, 0:HALF], ACT.Square).then_inc(sem("pe_sq"), 1)
                n = ("kn", h)
                filled(act, n)
                k2 = lambda r: r.rearrange("p (b t) -> p b t", b=2)
                A(k2(KSQ[:]), tile2(n)[:, :, 0:KEYS // 2], ACT.Square)
                A(k2(KNH[:]), tile2(n)[:, :, 0:KEYS // 2], ACT.Copy).then_inc(sem("kn_hi"), 1)
                if h % 2 == 0:
                    act.wait_ge(sem("q_rotated"), h // 2 + 1)
                    A(QPH[:], PEG[:], ACT.Copy).then_inc(sem("qp_hi"), 1)

            def values(h):
                n = ("v", h)
                filled(act, n)
                A(VH[:].rearrange("p (b j) v -> p b (j v)", b=2), tile2(n)[:, :, 0:3 * P], ACT.Copy).then_inc(sem("v_hi"), 1)

            qk(0)
            values(0)
            spread_copy(("rk", 0), RK, NKT)
            for h in range(HEADS):
                for t in range(QT):
                    p = PROBC[:] if t == 0 else PROB[:, t - 1, :]
                    act.wait_ge(sem("nb_ready"), QT * h + t + 1)
                    A(p, p, ACT.Exp, bias=NB8[:, t:t + 1], scale=RQ[h % 2][:, t:t + 1],
                      accum_out=SUM8[:, t:t + 1]).then_inc(sem("exp_done"), 1)
                if h + 1 < HEADS:
                    qk(h + 1)
                for t in range(QT):
                    n = ("pt", h, t)
                    filled(act, n)
                    if t == 0:
                        A(PTCH[:], tile2(n)[:, 0, 0:P], ACT.Copy).then_inc(sem("pt_hi"), 1)
                    else:
                        g, c0 = (t - 1) // 2, (t - 1) % 2 * P
                        for bank, k0, k1 in ((0, 0, 3), (1, 3, 5)):
                            ins = A(PTH[:, g, k0:k1, c0:c0 + P],
                                    tile2(n)[:, bank, 0:(k1 - k0) * P].rearrange("p (k q) -> p k q", q=P), ACT.Copy)
                        ins.then_inc(sem("pt_hi"), 1)
                for g in range(3):
                    n = ("o", h, g)
                    filled(act, n)
                    a, b = ((0, CTX), (CTX, CTX + 256), (CTX + 256, TOK))[g]
                    A(O[:, h, a:b], tile2(n)[:, 0, 0:b - a], ACT.Copy).then_inc(free_of(n), 1)
                if h + 1 < HEADS:
                    values(h + 1)
                    spread_copy(("rk", h + 1), RK, NKT)
            filled(act, ("mt", MT - 1))
            round_units(U[("wo", 0)])
            for k in range(HEADS):
                was_read(act, ("o", HEADS - 1, 2))
                A(OH[:, k, :], O[:, k, :], ACT.Copy).then_inc(sem("o_hi"), 1)

            for m in range(KT):
                if m % 2 == 0:
                    round_units(U[("wo", m)] + 1)
                was_read(act, ("wo", m))
                square("ffn0", m, X[:, m, :])

            def ffn(l):
                n = f"ffn{l}"
                spread_copy(("rb", n), RSTD, QT)
                apply(n, l, 1)
                nf = 0
                for kind, a, f0 in ffn_steps():
                    if kind == "pair":
                        round_units(U[("gate", l, a)] + 1)
                        for j in range(2):
                            n = ("gate", l, a + j)
                            filled(act, n)
                            if a >= 2:
                                was_read(act, ("up", l, a + j - 2))
                            A(row2(ACTV[j][:]), tile2(n)[:, :, 0:HALF], ACT.Silu).then_inc(free_of(n), 1)
                        round_units(U[("up", l, a)] + 1)
                        for j in range(2):
                            was_read(act, ("up", l, a + j))
                            A(HIDH[:, (a + j) % HID_SLOTS, :], TMP[j][:], ACT.Copy).then_inc(sem("hid_hi"), 1)
                    else:
                        for m in range(KT):
                            if m % 2 == 0:
                                round_units(U[("down", l, a, m)] + 1)
                            if l == 0 and a == len(DOWN_K) - 1:
                                was_read(act, ("down", l, a, m))
                                square("mix1", m, X[:, m, :])

            ffn(0)
            spread_copy(("rb", "mix1"), RSTD, QT)
            apply("mix1", 1, 0)
            for i in range(KT):
                round_units(U[("glu", i)] + 1)
                n = ("b", i)
                filled(act, n)
                if i >= 2:
                    was_read(act, ("a", i - 2))
                c0 = V2["b_pw1"] + KT + i
                A(row2(ACTV[i % 2][:]), tile2(n)[:, :, 0:HALF], ACT.Sigmoid, bias=VT2[:, c0:c0 + 1]).then_inc(free_of(n), 1)
            for i in range(KT):
                act.wait_ge(sem("y_centred"), i + 1)
                square("ln", i, Y[:, i, :])
            spread_copy(("rb", "ln"), RSTD, QT)
            for k in range(KT):
                act.wait_ge(sem("t_ready"), KT * APPLY["ln"] + k + 1)
                if k >= 2:
                    act.wait_ge(sem("h_ready"), KT * APPLY["ln"] + k - 1)
                c0 = V2["ln_b"] + k
                A(ACTV[k % 2][:], SCALED[k % 3][:], ACT.Silu, bias=VT2[:, c0:c0 + 1]).then_inc(sem("swish"), 1)
                act.wait_ge(sem("swish"), k + 1)
                A(HH[:, k, :], ACTV[k % 2][:], ACT.Copy).then_inc(sem("part_hi"), 1)
            for m in range(KT):
                if m % 2 == 0:
                    round_units(U[("pw2", m)] + 1)
                was_read(act, ("pw2", m))
                square("ffn1", m, X[:, m, :])
            ffn(1)
            for t in range(QT):
                n = ("y", t)
                filled(act, n)
                A(YROW[t][:, 0:512], tile2(n)[:, 0, :], ACT.Copy).then_inc(sem("y_half"), 1)

        @block.vector
        def _(dve):
            V = nc.vector
            n_lo, n_add, n_chain, n_t, n_part, n_bg = [0], [0], [0], [0], [0], [0]

            def link(ins):
                n_chain[0] += 1
                ins.then_inc(sem("dve_chain"), 1)
                dve.wait_ge(sem("dve_chain"), n_chain[0])

            def split_units(upto):
                while n_lo[0] <= min(upto, len(units) - 1):
                    u = n_lo[0]
                    dve.wait_ge(hi_done, u + 1)
                    n = units[u][1]
                    V.tensor_tensor(WL[:, u % 2, 0:n], RAW[:, u % 2, 0:n], WH[:, u % 2, 0:n].bitcast(F32),
                                    ALU.subtract).then_inc(lo_done, 1)
                    n_lo[0] += 1

            def add_sum(m, a, b):
                if n_add[0] and m > 1:
                    dve.wait_ge(sem("sq_added"), n_add[0])
                V.tensor_tensor(SUM[:], a if m == 1 else SUM[:], b, ALU.add).then_inc(sem("sq_added"), 1)
                n_add[0] += 1

            def add_square(norm, m, tiles=KT):
                base = SQ_BASE[norm]
                dve.wait_ge(sem("sq_made"), base + m + 1)
                if m >= 1:
                    add_sum(m, SQ[0][:], SQ[m % 2][:])

            def rsqrt(n):
                link(V.tensor_scalar(RSI[:, 0:n], RS[:, 0, 0:n].bitcast(I32), 1, None, ALU.arith_shift_right))
                link(V.tensor_scalar(RS[:, 1, 0:n].bitcast(I32), RSI[:, 0:n], -1.0, 1597463007.0, ALU.mult, ALU.add))
                for _ in range(3):
                    link(V.tensor_tensor(RS[:, 2, 0:n], RS[:, 1, 0:n], RS[:, 1, 0:n], ALU.mult))
                    link(V.scalar_tensor_tensor(out=RS[:, 3, 0:n], in0=RS[:, 2, 0:n], scalar=-0.5, in1=RS[:, 0, 0:n],
                                                op0=ALU.mult, op1=ALU.mult))
                    link(V.scalar_tensor_tensor(out=RS[:, 1, 0:n], in0=RS[:, 3, 0:n], scalar=1.5, in1=RS[:, 1, 0:n],
                                                op0=ALU.add, op1=ALU.mult))

            def norm(n, dim):
                filled(dve, ("stat", n))
                s = ("stat", n)
                V.tensor_scalar(RS[:, 0, 0:QT], tile2(s)[:, 0, 0:QT], 1.0 / dim, EPS, ALU.mult, ALU.add).then_inc(free_of(s), 1)
                was_read(dve, s)
                rsqrt(QT)
                for t in range(QT):
                    V.tensor_scalar(DIAGN[:, t, :], EYE[:], RS[:, 1, t:t + 1], None, ALU.mult).then_inc(sem("diag_ready"), 1)

            def mod_read_chunk(n, ch, t0, tiles):
                l, j = divmod(ch, 6)
                filled(dve, n)
                src = tile2(n)[:, 0, 0:2 * tiles].rearrange("p (k s) -> p k s", s=2)
                at = 8 * j + t0
                b = VT1[:, V1["b_mod"] + 48 * l + at:V1["b_mod"] + 48 * l + at + tiles]
                for s in range(2):
                    ins = V.tensor_tensor(MODV[:, l, s, at:at + tiles], src[:, :, s], b, ALU.add)
                ins.then_inc(free_of(n), 1)
                if j in (1, 4) and t0 + tiles == KT:
                    was_read(dve, n)
                    g0 = V1["norm_mix" if j == 1 else "norm_ffn"] + KT * l
                    for s in range(2):
                        ins = V.scalar_tensor_tensor(out=GAIN[:, l, j // 4, s, :], in0=MODV[:, l, s, 8 * j:8 * j + 8], scalar=1.0,
                                                     in1=VT1[:, g0:g0 + KT], op0=ALU.add, op1=ALU.mult)
                    link(ins)

            def background(steps):
                for _ in range(steps):
                    i = n_bg[0]
                    if i == N_HALF * KT:
                        return
                    n_bg[0] += 1
                    j, k = divmod(i, KT)
                    if k == 0 and j >= 2:
                        filled(dve, ("mh", j - 2))
                    dve.wait_ge(bgw_landed[i % BG_SLOTS], 16 * (i // BG_SLOTS + 1))
                    if k:
                        dve.wait_ge(sem("bgw_used"), i)
                    for s in range(2):
                        acc, w, c = BGACC[j % 2][:, s, :], BGW[i % BG_SLOTS][:], SC[:, k, s:s + 1]
                        if k == 0:
                            ins = V.tensor_scalar(acc, w, c, None, ALU.mult)
                        else:
                            ins = V.scalar_tensor_tensor(out=acc, in0=w, scalar=c, in1=acc, op0=ALU.mult, op1=ALU.add)
                    ins.then_inc(sem("bgw_used"), 1)

            def mod_halves(pair):
                for j in range(N_HALF):
                    if half_pair(j) == pair:
                        mod_read_chunk(("mh", j), FIRST_BG + j // 2, 4 * (j % 2), 4)

            def apply(norm_name, l, half):
                was_read(dve, ("rb", norm_name))

                def scale(k):
                    if k >= 3:
                        dve.wait_ge(sem("h_ready"), KT * APPLY[norm_name] + k - 2)
                    for a, b, s in SEGS:
                        ins = V.scalar_tensor_tensor(out=SCALED[k % 3][:, a:b], in0=X[:, k, a:b], scalar=GAIN[:, l, half, s, k:k + 1],
                                                     in1=RSTD[:, a:b], op0=ALU.mult, op1=ALU.mult)
                    ins.then_inc(sem("t_ready"), 1)
                    n_t[0] += 1

                scale(0)
                for k in range(KT):
                    if k + 1 < KT:
                        scale(k + 1)
                    n_part[0] += 1
                    dve.wait_ge(sem("t_ready"), n_t[0] - (k + 1 < KT))
                    dve.wait_ge(sem("part_hi"), n_part[0])
                    for a, b, s in SEGS:
                        ins = V.scalar_tensor_tensor(out=HL[:, k, a:b], in0=SCALED[k % 3][:, a:b],
                                                     scalar=MODV[:, l, s, 24 * half + k:24 * half + k + 1],
                                                     in1=HH[:, k, a:b].bitcast(F32), op0=ALU.add, op1=ALU.subtract)
                    ins.then_inc(sem("h_ready"), 1)

            def residual(n, m, l, which):
                filled(dve, n)
                for bank, a, b, t, s in PSEGS:
                    g = MODV[:, l, s, 8 * which + m:8 * which + m + 1]
                    ins = V.scalar_tensor_tensor(out=X[:, m, t:t + b - a], in0=tile2(n)[:, bank, a:b], scalar=g,
                                                 in1=X[:, m, t:t + b - a], op0=ALU.mult, op1=ALU.add)
                ins.then_inc(free_of(n), 1)

            V.memset(ONES[:], 1.0).then_inc(sem("ones_set"), 1)
            filled(dve, "vec")
            ps = tile2("vec")
            V.tensor_copy(VT1[:], ps[:, 0, 0:P])
            V.tensor_copy(VT2[:], ps[:, 0, P:P + NV2]).then_inc(free_of("vec"), 1)
            was_read(dve, "vec")
            link(V.tensor_tensor(GQK[:], VT2[:, V2["gq"]:V2["gq"] + 1], VT2[:, V2["gk"]:V2["gk"] + 1], ALU.mult))
            for k in range(KT):
                n = ("x", k)
                filled(dve, n)
                V.tensor_copy(X[:, k, 0:3 * P], tile2(n)[:, 0, 0:3 * P])
                V.tensor_copy(X[:, k, 3 * P:TOK], tile2(n)[:, 1, 0:2 * P]).then_inc(free_of(n), 1)
                if k >= 1:
                    add_square("mix0", k - 1)
            add_square("mix0", KT - 1)
            norm("mix0", D)
            filled(dve, "taps")
            V.tensor_copy(WTAP[:].rearrange("p k t -> p (k t)"), tile2("taps")[:, 0, 0:KT * TAPS]).then_inc(free_of("taps"), 1)
            filled(dve, "cache")
            dve.wait_ge(sem("cache_hi"), 1)
            ps = tile2("cache")
            V.tensor_tensor(CKL[:, :, CTX:CTX + PAST], ps[:, 0, 0:KVL].rearrange("p (j t) -> p j t", j=KVT),
                            CKH[:, :, CTX:CTX + PAST].bitcast(F32), ALU.subtract)
            V.tensor_copy(KPRAW[:, CTX:CTX + PAST], ps[:, 0, KVL:KVL + P]).then_inc(free_of("cache"), 1)
            split_units(1)
            for ch in range(2):
                mod_read_chunk(("mod", ch), ch, 0, KT)
            apply("mix0", 0, 0)
            for m in range(QLT):
                if m % 2 == 0:
                    split_units(U[("dq", m)] + 1)
                add_square("cq", m, QLT)
            split_units(U[("dkv", 0)] + 1)
            for m in range(KVT):
                if m == 1:
                    filled(dve, ("stat", "cq"))
                if m == 0:
                    norm("cq", QL)
                add_square("ck", m, KVT)
            split_units(U[("dkv", 2)] + 1)
            was_read(dve, ("rb", "cq"))
            for m in range(QLT):
                g = VT2[:, V2["q_norm"] + m:V2["q_norm"] + m + 1]
                V.scalar_tensor_tensor(out=TMP[m % 2][:], in0=CQRAW[:, m, :], scalar=g, in1=RSTD[:],
                                       op0=ALU.mult, op1=ALU.mult).then_inc(sem("cq_t"), 1)
                dve.wait_ge(sem("cq_t"), m + 1)
                dve.wait_ge(sem("cq_hi"), m + 1)
                V.tensor_tensor(CQL[:, m, :], TMP[m % 2][:], CQH[:, m, :].bitcast(F32), ALU.subtract).then_inc(sem("cq_ready"), 1)
            norm("ck", KVL)
            was_read(dve, ("rb", "ck"))
            for m in range(KVT):
                g = VT2[:, V2["kv_norm"] + m:V2["kv_norm"] + m + 1]
                V.scalar_tensor_tensor(out=TMP[m % 2][:], in0=CKRAW[:, m, :], scalar=g, in1=RSTD[:],
                                       op0=ALU.mult, op1=ALU.mult).then_inc(sem("ck_t"), 1)
                dve.wait_ge(sem("ck_t"), m + 1)
                V.tensor_copy(CKN[:, m, :], TMP[m % 2][:, 0:CTX]).then_inc(sem("ckn_ready"), 1)
                dve.wait_ge(sem("ck_hi"), m + 1)
                V.tensor_tensor(CKL[:, m, 0:CTX], TMP[m % 2][:, 0:CTX], CKH[:, m, 0:CTX].bitcast(F32), ALU.subtract)
                V.tensor_tensor(CKL[:, m, CTX + PAST:KEYS], TMP[m % 2][:, CTX:TOK], CKH[:, m, CTX + PAST:KEYS].bitcast(F32),
                                ALU.subtract).then_inc(sem("ck_ready"), 1)
            filled(dve, "kpstat")
            V.tensor_copy(KPSS[:], tile2("kpstat")[:, 0, 0:NKT]).then_inc(free_of("kpstat"), 1)
            was_read(dve, "kpstat")
            V.tensor_scalar(KPSQ[:], KPRAW[:], VT2[:, V2["gk_pe"]:V2["gk_pe"] + 1], None, ALU.mult).then_inc(sem("kpg_ready"), 1)
            dve.wait_ge(sem("kpg_ready"), 1)
            dve.wait_ge(sem("rope_landed"), 32)
            filled(dve, "kprot")
            V.tensor_tensor(ROPET[:], tile2("kprot")[:, 0, :], SIN[:], ALU.mult).then_inc(free_of("kprot"), 1)
            was_read(dve, "kprot")
            late = KPSQ[:, KEYS - LAT:KEYS]
            link(V.tensor_tensor(late, late, COS[:], ALU.mult))
            V.tensor_tensor(late, late, ROPET[:], ALU.add).then_inc(sem("kp_rotated"), 1)
            dve.wait_ge(sem("kp_rotated"), 1)
            dve.wait_ge(sem("kp_hi"), 1)
            V.tensor_tensor(KPL[:], KPSQ[:], KPH[:].bitcast(F32), ALU.subtract).then_inc(sem("kp_ready"), 1)

            def qk(h):
                split_units(U[("head", min(h + 1, HEADS - 1))])
                n = ("qn", h)
                dve.wait_ge(sem("qn_hi"), h + 1)
                V.scalar_tensor_tensor(out=row2(QNL[:]), in0=tile2(n)[:, :, 0:HALF], scalar=GQK[:, 0:1],
                                       in1=row2(QNH[:]).bitcast(F32), op0=ALU.mult, op1=ALU.subtract).then_inc(free_of(n), 1)
                if h % 2 == 0:
                    n = ("pe", h)
                    dve.wait_ge(sem("pe_sq"), h // 2 + 1)
                    V.tensor_scalar(row2(PEG[:]), tile2(n)[:, :, 0:HALF], VT2[:, V2["gq_pe"]:V2["gq_pe"] + 1], None,
                                    ALU.mult).then_inc(free_of(n), 1)
                n = ("kn", h)
                dve.wait_ge(sem("kn_hi"), h + 1)
                k2 = lambda r: r.rearrange("p (b t) -> p b t", b=2)
                V.tensor_tensor(k2(KNL[:]), tile2(n)[:, :, 0:KEYS // 2], k2(KNH[:]).bitcast(F32),
                                ALU.subtract).then_inc(free_of(n), 1)
                if h % 2 == 0:
                    n = ("rot", h)
                    filled(dve, n)
                    V.tensor_tensor(ROPEQ[:], tile2(n)[:, 0, :], SIN[:], ALU.mult).then_inc(free_of(n), 1)
                    was_read(dve, n)
                    was_read(dve, ("pe", h))
                    link(V.tensor_tensor(PEG[:, CTX:TOK], PEG[:, CTX:TOK], COS[:], ALU.mult))
                    V.tensor_tensor(PEG[:, CTX:TOK], PEG[:, CTX:TOK], ROPEQ[:], ALU.add).then_inc(sem("q_rotated"), 1)
                    dve.wait_ge(sem("q_rotated"), h // 2 + 1)
                    dve.wait_ge(sem("qp_hi"), h // 2 + 1)
                    V.tensor_tensor(QPL[:], PEG[:], QPH[:].bitcast(F32), ALU.subtract).then_inc(sem("qp_ready"), 1)
                n = ("hstat", h)
                filled(dve, n)
                V.tensor_copy(HST[:, 0:QT], tile2(n)[:, 0, 0:QT])
                V.tensor_tensor(HST[:, QT:QT + NKT], tile2(n)[:, 0, QT:QT + NKT], KPSS[:], ALU.add).then_inc(free_of(n), 1)
                was_read(dve, n)
                link(V.tensor_scalar(RS[:, 0, 0:QT + NKT], HST[:, 0:QT + NKT], 1.0 / QK, EPS, ALU.mult, ALU.add))
                rsqrt(QT + NKT)
                link(V.tensor_scalar(RQ[h % 2][:], RS[:, 1, 0:QT], QK ** -0.5, None, ALU.mult))
                for t in range(NKT):
                    V.tensor_scalar(DIAGK[t][:], EYE[:], RS[:, 1, QT + t:QT + t + 1], None, ALU.mult).then_inc(sem("diag_ready"), 1)

            def values(h):
                n = ("v", h)
                dve.wait_ge(sem("v_hi"), h + 1)
                v2 = lambda r: r.rearrange("p (b j) v -> p b (j v)", b=2)
                V.tensor_tensor(v2(VL[:]), tile2(n)[:, :, 0:3 * P], v2(VH[:]).bitcast(F32), ALU.subtract).then_inc(free_of(n), 1)

            def mod_tile(i):
                mod_read_chunk(("mt", i), 2 + i // KT, i % KT, 1)

            qk(0)
            values(0)
            for h in range(HEADS):
                was_read(dve, ("rk", h))

                def peak(t):
                    n = ("s", h, t)
                    filled(dve, n)
                    if t == 0:
                        o, i0, i1 = PROBC[:], tile2(n)[:, 0, 0:CTX], RK[:, 0:CTX]
                    else:
                        o, i0, i1 = row2(PROB[:, t - 1, :]), tile2(n)[:, :, 0:HALF], row2(RK[:, CTX:KEYS])
                    V.tensor_tensor_reduce(out=o, in0=i0, in1=i1, scale=1.0, scalar=-3.0e38, op0=ALU.mult, op1=ALU.max,
                                           accum_out=MAX8[:, t:t + 1]).then_inc(free_of(n), 1)
                    was_read(dve, n)
                    V.scalar_tensor_tensor(out=NB8[:, t:t + 1], in0=MAX8[:, t:t + 1], scalar=-1.0, in1=RQ[h % 2][:, t:t + 1],
                                           op0=ALU.mult, op1=ALU.mult).then_inc(sem("nb_ready"), 1)

                def normalise(t):
                    dve.wait_ge(sem("exp_done"), QT * h + t + 1)
                    link(V.reciprocal(REC8[:, t:t + 1], SUM8[:, t:t + 1]))
                    p = PROBC[:] if t == 0 else PROB[:, t - 1, :]
                    V.tensor_scalar(p, p, REC8[:, t:t + 1], None, ALU.mult).then_inc(sem("prob_ready"), 1)

                for t in range(QT):
                    peak(t)
                    if t:
                        normalise(t - 1)
                normalise(QT - 1)
                if h + 1 < HEADS:
                    qk(h + 1)
                mod_tile(3 * h)
                for t in range(QT):
                    n = ("pt", h, t)
                    dve.wait_ge(sem("pt_hi"), QT * h + t + 1)
                    if t == 0:
                        V.tensor_tensor(PTCL[:], tile2(n)[:, 0, 0:P], PTCH[:].bitcast(F32), ALU.subtract).then_inc(free_of(n), 1)
                    else:
                        g, c0 = (t - 1) // 2, (t - 1) % 2 * P
                        for bank, k0, k1 in ((0, 0, 3), (1, 3, 5)):
                            ins = V.tensor_tensor(PTL[:, g, k0:k1, c0:c0 + P],
                                                  tile2(n)[:, bank, 0:(k1 - k0) * P].rearrange("p (k q) -> p k q", q=P),
                                                  PTH[:, g, k0:k1, c0:c0 + P].bitcast(F32), ALU.subtract)
                        ins.then_inc(free_of(n), 1)
                mod_tile(3 * h + 1)
                if h + 1 < HEADS:
                    values(h + 1)
                mod_tile(3 * h + 2)
            split_units(U[("wo", 0)])
            for k in range(HEADS):
                dve.wait_ge(sem("o_hi"), k + 1)
                V.tensor_tensor(OL[:, k, :], O[:, k, :], OH[:, k, :].bitcast(F32), ALU.subtract).then_inc(sem("o_split"), 1)
            def residuals(name, l, which, norm_name):
                for m in range(KT):
                    if m % 2 == 0:
                        split_units(U[name(m)] + 1)
                    residual(name(m), m, l, which)
                    if norm_name and m:
                        add_square(norm_name, m - 1)
                if norm_name:
                    add_square(norm_name, KT - 1)

            residuals(lambda m: ("wo", m), 0, 2, "ffn0")

            def ffn(l):
                n = f"ffn{l}"
                norm(n, D)
                apply(n, l, 1)
                for kind, a, f0 in ffn_steps():
                    if kind == "pair":
                        split_units(U[("gate", l, a)] + 1)
                        if l == 0:
                            background(BG_STEPS // 2)
                        split_units(U[("up", l, a)] + 1)
                        if l == 0:
                            mod_halves(a // 2)
                        for j in range(2):
                            n = ("up", l, a + j)
                            was_read(dve, ("gate", l, a + j))
                            filled(dve, n)
                            V.tensor_tensor(row2(TMP[j][:]), tile2(n)[:, :, 0:HALF], row2(ACTV[j][:]), ALU.mult).then_inc(free_of(n), 1)
                        for j in range(2):
                            was_read(dve, ("up", l, a + j))
                            dve.wait_ge(sem("hid_hi"), FT * l + a + j + 1)
                            V.tensor_tensor(HIDL[:, (a + j) % HID_SLOTS, :], TMP[j][:], HIDH[:, (a + j) % HID_SLOTS, :].bitcast(F32),
                                            ALU.subtract).then_inc(sem("hid_ready"), 1)
                        if l == 0:
                            background(BG_STEPS - BG_STEPS // 2)
                    else:
                        residuals(lambda m: ("down", l, a, m), l, 5, "mix1" if l == 0 and a == len(DOWN_K) - 1 else None)

            ffn(0)
            mod_halves(FT // 2)
            norm("mix1", D)
            for i in range(2):
                link(V.memset(GP[i][:], 0.0))
            apply("mix1", 1, 0)
            for i in range(KT):
                split_units(U[("glu", i)] + 1)
                was_read(dve, ("b", i))
                n = ("a", i)
                filled(dve, n)
                for bank, a, b, t, s in PSEGS:
                    to = t + PAD if s == 0 else t + 2 * PAD
                    ins = V.scalar_tensor_tensor(out=GP[i % 2][:, to:to + b - a], in0=tile2(n)[:, bank, a:b],
                                                 scalar=VT2[:, V2["b_pw1"] + i:V2["b_pw1"] + i + 1],
                                                 in1=ACTV[i % 2][:, t:t + b - a], op0=ALU.add, op1=ALU.mult)
                ins.then_inc(free_of(n), 1)
                was_read(dve, n)
                acc = YACC[i % 2]
                link(V.tensor_scalar(acc[:], GP[i % 2][:, 0:RUN], WTAP[:, i, 0:1], VT2[:, V2["b_dw"] + i:V2["b_dw"] + i + 1],
                                     ALU.mult, ALU.add))
                for j in range(1, TAPS - 1):
                    link(V.scalar_tensor_tensor(out=acc[:], in0=GP[i % 2][:, j:j + RUN], scalar=WTAP[:, i, j:j + 1],
                                                in1=acc[:], op0=ALU.mult, op1=ALU.add))
                j = TAPS - 1
                for a, b, s in SEGS:
                    at = a + s * PAD
                    ins = V.scalar_tensor_tensor(out=Y[:, i, a:b], in0=GP[i % 2][:, at + j:at + j + b - a], scalar=WTAP[:, i, j:j + 1],
                                                 in1=acc[:, at:at + b - a], op0=ALU.mult, op1=ALU.add)
                link(ins)
                if i == 1:
                    add_sum(1, Y[:, 0, :], Y[:, 1, :])
                elif i:
                    add_sum(i, None, Y[:, i, :])
            for s in range(2):
                link(V.tensor_tensor(GB[:, s, :], MODV[:, 1, s, 16:24], VT2[:, V2["b_pw2"]:V2["b_pw2"] + KT], ALU.mult))
            filled(dve, "mu")
            for i in range(KT):
                V.scalar_tensor_tensor(out=row2(Y[:, i, :]), in0=tile2("mu")[:, :, 0:HALF], scalar=-1.0 / D,
                                       in1=row2(Y[:, i, :]), op0=ALU.mult, op1=ALU.add).then_inc(sem("y_centred"), 1)
                if i:
                    add_square("ln", i - 1)
            add_square("ln", KT - 1)
            V.tensor_copy(EPSC[:], tile2("mu")[:, 0, 0:1]).then_inc(free_of("mu"), 1)
            norm("ln", D)
            was_read(dve, ("rb", "ln"))

            def ln_scale(k):
                V.scalar_tensor_tensor(out=SCALED[k % 3][:], in0=Y[:, k, :], scalar=VT2[:, V2["ln_g"] + k:V2["ln_g"] + k + 1],
                                       in1=RSTD[:], op0=ALU.mult, op1=ALU.mult).then_inc(sem("t_ready"), 1)

            ln_scale(0)
            for k in range(KT):
                if k + 1 < KT:
                    if k >= 2:
                        dve.wait_ge(sem("swish"), k - 1)
                    ln_scale(k + 1)
                n_part[0] += 1
                dve.wait_ge(sem("part_hi"), n_part[0])
                V.tensor_tensor(HL[:, k, :], ACTV[k % 2][:], HH[:, k, :].bitcast(F32), ALU.subtract).then_inc(sem("h_ready"), 1)
            n_t[0] += KT
            for k in range(KT):
                for a, b, s in SEGS:
                    ins = V.tensor_scalar(X[:, k, a:b], X[:, k, a:b], GB[:, s, k:k + 1], None, ALU.add)
                link(ins)
            residuals(lambda m: ("pw2", m), 1, 2, "ffn1")
            ffn(1)
            for t in range(QT):
                n = ("y", t)
                filled(dve, n)
                dve.wait_ge(sem("y_half"), t + 1)
                V.tensor_copy(YROW[t][:, 512:1024], tile2(n)[:, 1, :]).then_inc(free_of(n), 1)


_INS = ["x_prompt", "x_sample", "cache_ckv", "cache_kpe", "c", "c_ctx", "w_mod", "b_mod", "norm_mix", "norm_ffn",
        "mla_w_dq", "mla_q_norm", "mla_w_uq", "mla_w_dkv", "mla_kv_norm", "mla_w_ukv", "mla_q_hnorm", "mla_k_hnorm",
        "mla_w_o", "conv_w_pw1", "conv_b_pw1", "conv_w_dw", "conv_b_dw", "conv_ln_g", "conv_ln_b", "conv_w_pw2",
        "conv_b_pw2", "ffn_w_gate", "ffn_w_up", "ffn_w_down"]
_OUTS = [((1, CTX, D), "float32"), ((1, LAT, D), "float32"), ((1, 1, CTX, KVL), "float32"), ((1, 1, CTX, ROPE), "float32")]


def kernel(**inputs):
    import concourse.bacc as bacc
    from concourse.bass_utils import run_bass_kernel_spmd

    nc = bacc.Bacc("TRN2", target_bir_lowering=False, num_devices=1)
    arrays, args = {}, []
    for name in _INS:
        a = np.ascontiguousarray(inputs[name])
        arrays[f"in_{name}"] = a
        args.append(nc.dram_tensor(f"in_{name}", a.shape, mybir.dt.from_np(a.dtype), kind="ExternalInput").ap())
    for i, (shape, dtype) in enumerate(_OUTS):
        args.append(nc.dram_tensor(f"out_{i}", shape, mybir.dt.from_np(np.dtype(dtype)), kind="ExternalOutput").ap())
    program(nc, *args)
    r = run_bass_kernel_spmd(nc, [arrays], core_ids=[0])
    return tuple(r.results[0][f"out_{i}"] for i in range(len(_OUTS)))
```

```python
from contextlib import ExitStack

import numpy as np

import concourse.bass as bass
from concourse import mybir

P = 128
F32 = mybir.dt.float32
F32R = mybir.dt.float32r
I32 = mybir.dt.int32
ALU = mybir.AluOpType
ACT = mybir.ActivationFunctionType

CTX, LAT = 128, 512
TOK = CTX + LAT
PAST = 128
KEYS = CTX + PAST + LAT
D = 1024
KT = D // P
HALF = TOK // 2
HEADS, NOPE, ROPE, VD = 8, 128, 64, 128
QK = NOPE + ROPE
QL, KVL = 512, 256
QLT, KVT = QL // P, KVL // P
FF = 2816
FT = FF // P
TAPS, PAD = 31, 15
GRID_W = 64
THETA = 10000.0
EPS = 1e-6
RUN = CTX + PAD + LAT
GPW = RUN + 2 * PAD + 3
PE_TAPS = 11
CHALF = (RUN + 1) // 2
DIAG_SLOTS = 15
QT = TOK // P
NKT = KEYS // P
DOWN_K = (8, 8, 6)
HID_SLOTS = 10
UNIT = 2048

SEGS = ((0, CTX, 0), (CTX, TOK, 1))
PSEGS = ((0, 0, CTX, 0, 0), (0, CTX, HALF, CTX, 1), (1, 0, HALF, HALF, 1))

CSEGS = ((0, 0, CTX, 0), (0, CTX + PAD, CHALF, CTX), (1, 0, RUN - CHALF, CHALF - PAD))

V1 = {"b_mod": 0, "norm_mix": 96, "norm_ffn": 112}
V2, NV2 = {}, 0
for _n, _w in (("q_norm", 4), ("kv_norm", 2), ("b_pw1", 16), ("b_dw", 8), ("ln_g", 8), ("ln_b", 8),
               ("b_pw2", 8), ("c", 8), ("c_ctx", 8), ("gq", 1), ("gk", 1), ("gq_pe", 1), ("gk_pe", 1)):
    V2[_n] = NV2
    NV2 += _w


def rope_tables():
    t = np.arange(LAT)
    ax = ROPE // 2
    inv = (1.0 / (THETA ** (np.arange(0, ax, 2, dtype=np.float32) / np.float32(ax)))).astype(np.float32)
    ar = (t // GRID_W).astype(np.float32)[:, None] * inv[None, :]
    ac = (t % GRID_W).astype(np.float32)[:, None] * inv[None, :]
    cos = np.concatenate([np.cos(ar), np.cos(ar), np.cos(ac), np.cos(ac)], axis=1).T
    sin = np.concatenate([np.sin(ar), np.sin(ar), np.sin(ac), np.sin(ac)], axis=1).T
    rot = np.zeros((P, P), np.float32)
    q = ROPE // 4
    for b in range(0, P, ROPE // 2):
        for i in range(q):
            rot[b + q + i, b + i] = -1.0
            rot[b + i, b + q + i] = 1.0
    return (np.concatenate([cos, cos]).astype(np.float32), np.concatenate([sin, sin]).astype(np.float32), rot)


N_ROWS = 6
ROW_SLOTS = 4
FIRST_BG = 5
N_HALF = 2 * (12 - FIRST_BG)
BG_STEPS = 12
BG_SLOTS = 6


def half_pair(j):
    return min((KT * j + KT - 1) // BG_STEPS + 1, FT // 2)


def tile_order():
    o = [("x", k) for k in range(KT)] + ["vec"]
    norm = lambda n: [("stat", n), ("rb", n)]
    o += [("stat", "mix0"), "taps", "cache", ("rb", "mix0"), ("mrow", 0), ("mrow", 1), "mods"]
    o += [("dq", m) for m in range(QLT)] + [("dkv", m) for m in range(KVT + 1)]
    o += norm("cq") + norm("ck") + ["kpstat", "kprot", "ctxout"]
    even = lambda h, n: [(n, h)] if h % 2 == 0 else []
    o += [("qn", 0), ("pe", 0), ("kn", 0), ("rot", 0), ("hstat", 0), ("v", 0), ("rk", 0)]
    for h in range(HEADS):
        o += [("s", h, t) for t in range(QT)]
        more = h + 1 < HEADS
        if more:
            o += [("qn", h + 1), *even(h + 1, "pe")]
        o += [("pt", h, t) for t in range(QT)]
        if more:
            o += [("kn", h + 1), *even(h + 1, "rot"), ("hstat", h + 1)]
        ma, mb = ([("ma", h)], [("mb", h)]) if h < N_ROWS else ([], [])
        o += ma + [("o", h, g) for g in range(3)] + mb
        if more:
            o += [("v", h + 1), ("rk", h + 1)]
    o += [("wo", m) for m in range(KT)]

    def ffn(l):
        r = norm(f"ffn{l}")
        for kind, a, _ in ffn_steps():
            if kind == "pair":
                mh = [("mh", j) for j in range(N_HALF) if l == 0 and half_pair(j) == a // 2]
                r += [("gate", l, a), ("gate", l, a + 1)] + mh[:1] + [("up", l, a)] + mh[1:] + [("up", l, a + 1)]
            else:
                r += [("down", l, a, m) for m in range(KT)]
        r += [("mh", j) for j in range(N_HALF) if l == 0 and half_pair(j) == FT // 2]
        return r

    o += ffn(0) + norm("mix1")
    for i in range(KT):
        o += [("a", i), ("b", i)] + ([("cv", i - 1)] if i else [])
    o += [("cv", KT - 1)]
    o += ["mu"] + norm("ln") + [("pw2", m) for m in range(KT)] + ffn(1)
    o += [("y", t) for t in range(QT)]
    return {n: i for i, n in enumerate(o)}


def ffn_steps():
    steps, f = [], 0
    for c, n in enumerate(DOWN_K):
        end = sum(DOWN_K[:c + 1])
        while f < min(end + 2, FT):
            steps.append(("pair", f, 0))
            f += 2
        steps.append(("down", c, end - n))
    return steps


def program(nc, x_prompt, x_sample, cache_ckv, cache_kpe, c, c_ctx, w_mod, b_mod, norm_mix, norm_ffn,
            w_dq, q_norm, w_uq, w_dkv, kv_norm, w_ukv, q_hn, k_hn, w_o, w_pw1, b_pw1, w_dw, b_dw,
            ln_g, ln_b, w_pw2, b_pw2, w_gate, w_up, w_down, y_prompt, y_sample, new_ckv, new_kpe):
    T = tile_order()
    cos_np, sin_np, rot_np = rope_tables()
    consts = {"eye": np.eye(P, dtype=np.float32), "rot": rot_np, "cos": cos_np, "sin": sin_np}
    const = {n: nc.inline_tensor(a, name=f"const_{n}").ap() for n, a in consts.items()}

    ctx = ExitStack()
    with ctx:
        base = (nc.sbuf_base + 63) // 64 * 64
        top = [base]

        def region(nbytes):
            at = top[0]
            top[0] += nbytes
            return at

        def sb(name, shape, at, dt=F32):
            return nc.alloc_sbuf_tensor_at(name, shape, dt, offset=at)

        R_X, R_HH, R_HL = region(KT * TOK * 4), region(KT * TOK * 4), region(KT * TOK * 4)
        R_HID = region(2 * HID_SLOTS * TOK * 4)
        R_RAW, R_WH, R_WL = region(2 * UNIT * 4), region(2 * UNIT * 4), region(2 * UNIT * 4)
        R_MOD = region(2 * 1024 * 4)
        R_T = [region(TOK * 4) for _ in range(8)]
        R_P, R_PE = region(4 * TOK * 4 + CTX * 4), region(2 * TOK * 4)

        X = sb("X", [P, KT, TOK], R_X)
        HH = sb("HH", [P, KT, TOK], R_HH, F32R)
        HL = sb("HL", [P, KT, TOK], R_HL, F32R)
        HIDH = sb("HIDH", [P, HID_SLOTS, TOK], R_HID, F32R)
        HIDL = sb("HIDL", [P, HID_SLOTS, TOK], R_HID + HID_SLOTS * TOK * 4, F32R)
        RAW = sb("RAW", [P, 2, UNIT], R_RAW)
        WH = sb("WH", [P, 2, UNIT], R_WH, F32R)
        WL = sb("WL", [P, 2, UNIT], R_WL, F32R)
        MODS = sb("MODS", [P, 5, 2 * D], R_HH)
        MROW = sb("MROW", [2, 2 * D], R_MOD)
        MODA = [sb(f"MODA{i}", [P, 512], (R_WH, R_WL)[i // 2] + (i % 2 * UNIT + 1536) * 4) for i in range(ROW_SLOTS)]
        MROWA = sb("MROWA", [2, 512], R_HH + 7 * TOK * 4)
        BGW = [sb(f"BGW{i}", [P, 512], R_MOD + 2048 * i if i < 4 else R_P + 8192 + 2048 * (i - 4)) for i in range(BG_SLOTS)]
        BGACC = [sb(f"BGACC{i}", [P, 2, 512], R_P + 4096 * i) for i in range(2)]
        SQ = [sb(f"SQ{i}", [P, TOK], R_T[i]) for i in range(2)]
        TMP = [sb(f"TMP{i}", [P, TOK], R_T[2 + i]) for i in range(2)]
        ACTV = [sb(f"ACTV{i}", [P, TOK], R_T[4 + i]) for i in range(2)]
        SCALED = [TMP[0], TMP[1], SQ[0]]
        SUM = sb("SUM", [P, TOK], R_T[6])
        RSTD = sb("RSTD", [P, TOK], R_T[7])
        XROWS = sb("XROWS", [P, QT, D], R_HID)
        CROWS = sb("CROWS", [P, KVL + P], R_P)
        TAPROWS = sb("TAPROWS", [TAPS, D], R_P + 2048)
        CQH = sb("CQH", [P, QLT, TOK], R_HID, F32R)
        CQL = sb("CQL", [P, QLT, TOK], R_HID + 10240, F32R)
        CKH = sb("CKH", [P, KVT, KEYS], R_HID + 20480, F32R)
        CKL = sb("CKL", [P, KVT, KEYS], R_HID + 26624, F32R)
        KPH = sb("KPH", [P, KEYS], R_HID + 32768, F32R)
        KPL = sb("KPL", [P, KEYS], R_HID + 35840, F32R)
        CQRAW = sb("CQRAW", [P, QLT, TOK], R_HID + 38912)
        VH = sb("VH", [P, NKT, VD], R_HID + 38912, F32R)
        VL = sb("VL", [P, NKT, VD], R_HID + 41984, F32R)
        KNH = sb("KNH", [P, KEYS], R_HID + 45056, F32R)
        KNL = sb("KNL", [P, KEYS], R_HID + 48128, F32R)
        CKRAW = sb("CKRAW", [P, KVT, TOK], R_P)
        KPSQ = sb("KPSQ", [P, KEYS], R_P + 5120)
        ROPET = sb("ROPET", [P, LAT], R_P + 8192)
        KPRAW = sb("KPRAW", [P, KEYS], R_PE)
        ROPEQ = sb("ROPEQ", [P, LAT], R_T[6] + KEYS * 4)
        RK = sb("RK", [P, KEYS], R_T[6])
        KSQ = sb("KSQ", [P, KEYS], R_T[0])
        QNH = sb("QNH", [P, TOK], R_T[4], F32R)
        QNL = sb("QNL", [P, TOK], R_T[5], F32R)
        QPH = sb("QPH", [P, TOK], R_PE, F32R)
        QPL = sb("QPL", [P, TOK], R_PE + TOK * 4, F32R)
        PROB = sb("PROB", [P, 4, TOK], R_P)
        PROBC = sb("PROBC", [P, CTX], R_P + 4 * TOK * 4)
        O = sb("O", [P, HEADS, TOK], R_HH)
        PTH = sb("PTH", [P, 2, 5, 256], R_HL, F32R)
        PTL = sb("PTL", [P, 2, 5, 256], R_HL + 10240, F32R)
        OH = sb("OH", [P, HEADS, TOK], R_HID, F32R)
        OL = sb("OL", [P, HEADS, TOK], R_HL, F32R)
        COS = sb("COS", [P, LAT], R_MOD)
        SIN = sb("SIN", [P, LAT], R_MOD + LAT * 4)
        QSQ, PEG = TMP[1], TMP[0]
        PESQ = sb("PESQ", [P, TOK], R_MOD + 5376)
        CKOUT = sb("CKOUT", [P, KVL + ROPE], R_MOD + 4096)
        CKN = sb("CKN", [P, KVT, CTX], R_T[0] + 3072)
        PTCH = sb("PTCH", [P, CTX], R_T[0] + 4096, F32R)
        PTCL = sb("PTCL", [P, CTX], R_T[0] + 4608, F32R)
        DIAGN = sb("DIAGN", [P, QT, P], R_T[4])
        DIAGK = [sb(f"DIAGK{t}", [P, P], R_RAW + 1536 * 4 + (t // 4) * UNIT * 4 + (t % 4) * P * 4) for t in range(NKT)]
        ROWS = sb("ROWS", [P, P], R_PE + 3072)
        ROWS2 = sb("ROWS2", [NV2, P], R_PE + 3584)
        GP = [sb(f"GP{i}", [P, GPW], R_HID + 20480 + 2752 * i) for i in range(2)]
        GPH = [sb(f"GPH{i}", [P, GPW], R_HID + 25984 + 2752 * i, F32R) for i in range(2)]
        GPL = [sb(f"GPL{i}", [P, GPW], R_HID + 31488 + 2752 * i, F32R) for i in range(2)]
        YACC = [sb(f"YACC{i}", [P, RUN], R_HID + 36992 + 2688 * i) for i in range(2)]
        WTH = sb("WTH", [P, KT, TAPS], R_HID + 42368, F32R)
        WTL = sb("WTL", [P, KT, TAPS], R_HID + 43392)
        TDH = sb("TDH", [P, DIAG_SLOTS, P], R_P, F32R)
        TDL = sb("TDL", [P, DIAG_SLOTS, P], R_P + DIAG_SLOTS * P * 4, F32R)
        Y = sb("Y", [P, KT, TOK], R_HID)
        YROW = [sb(f"YROW{t}", [P, D], R_HID + 4096 * t) for t in range(QT)]

        def small(name, shape, dt=F32):
            n = 4
            for s in shape[1:]:
                n *= s
            at = region((n + 31) // 32 * 32)
            return sb(name, shape, at, dt)

        EYE = small("EYE", [P, P])
        ROT = small("ROT", [P, P])
        ONES = small("ONES", [P, P])
        VT1 = small("VT1", [P, P])
        VT2 = small("VT2", [P, NV2])
        WTAP = small("WTAP", [P, KT, TAPS])
        SC = small("SC", [P, KT, 2])
        MODV = small("MODV", [P, 2, 2, 48])
        GAIN = small("GAIN", [P, 2, 2, 2, KT])
        GB = small("GB", [P, 2, KT])
        GQK = small("GQK", [P, 1])
        RS = small("RS", [P, 4, 12])
        RSI = small("RSI", [P, 12], I32)
        KPSS = small("KPSS", [P, NKT])
        RQ = [small(f"RQ{i}", [P, QT]) for i in range(2)]
        EPSC = small("EPSC", [P, 1])
        HST = small("HST", [P, 12])
        MAX8 = small("MAX8", [P, QT])
        NB8 = small("NB8", [P, QT])
        SUM8 = small("SUM8", [P, QT])
        REC8 = small("REC8", [P, QT])
        assert top[0] <= nc.sbuf_usable_end

        PS = ctx.enter_context(nc.psum_tensor("PS", [P, 8, 512], F32))

        sems = {}

        def sem(name):
            if name not in sems:
                sems[name] = ctx.enter_context(nc.semaphore(name))
            return sems[name]

        mm_done = sem("mm_done")
        tile_read = [sem(f"tile_read{i}") for i in range(4)]
        raw_landed = [sem(f"raw_landed{i}") for i in range(2)]
        hi_done, lo_done = sem("hi_done"), sem("lo_done")
        mods_landed = [sem(f"mods_landed{i}") for i in range(5)]
        moda_landed = [sem(f"moda_landed{i}") for i in range(ROW_SLOTS)]
        bgw_landed = [sem(f"bgw_landed{i}") for i in range(BG_SLOTS)]

        def tile2(name):
            s = T[name] % 4
            return PS[:, 2 * s:2 * s + 2, :]

        def free_of(name):
            return tile_read[T[name] % 4]

        def filled(eng, name):
            eng.wait_ge(mm_done, T[name] + 1)

        def was_read(eng, name):
            eng.wait_ge(free_of(name), T[name] // 4 + 1)

        def tap_done(eng, n):
            i, j = divmod(n, PE_TAPS)
            if j == PE_TAPS - 1:
                filled(eng, ("cv", i))
            else:
                eng.wait_ge(sem("tap_used"), (PE_TAPS - 1) * i + j + 1)

        def row_used(eng, i):
            j, k = divmod(i, KT)
            if k == KT - 1:
                filled(eng, ("ma", j))
            else:
                eng.wait_ge(sem("rows_used"), (KT - 1) * j + k + 1)

        def row2(ap):
            return ap.rearrange("p (b t) -> p b t", b=2)

        def cols(w, c0, n=256):
            return w[:, c0:c0 + n].rearrange("(k p) n -> p k n", p=P)

        units = []

        def full(kt, w, c0):
            return (kt * 256, [(lambda r, kt=kt: r[:, 0:kt * 256].rearrange("p (k n) -> p k n", k=kt), cols(w, c0))])

        for m in range(0, QLT, 2):
            units.append((("dq", m), *full(KT, w_dq[0], m * P)))
        units.append((("dkv", 0), *full(KT, w_dkv[0], 0)))
        dup = [(lambda r, i=i: r[:, 0:KT * P].rearrange("p (k n) -> p k n", k=KT)[:, :, i * ROPE:(i + 1) * ROPE],
                cols(w_dkv[0], KVL, ROPE)) for i in range(2)]
        units.append((("dkv", 2), KT * P, dup))
        for h in range(HEADS):
            v = lambda r, a, k, n: r[:, a:a + k * n].rearrange("p (k n) -> p k n", k=k)
            d = [(lambda r, v=v: v(r, 0, QLT, NOPE), cols(w_uq[0], h * QK, NOPE)),
                 (lambda r, v=v: v(r, 512, KVT, 256), cols(w_ukv[0], h * 256))]
            if h % 2 == 0:
                d += [(lambda r, v=v, i=i: v(r, 1024, QLT, P)[:, :, i * ROPE:(i + 1) * ROPE],
                       cols(w_uq[0], (h + i) * QK + NOPE, ROPE)) for i in range(2)]
            units.append((("head", h), 1536 if h % 2 == 0 else 1024, d))
        for m in range(0, KT, 2):
            units.append((("wo", m), *full(KT, w_o[0], m * P)))

        def ffn_units(l):
            for kind, a, f0 in ffn_steps():
                if kind == "pair":
                    units.append((("gate", l, a), *full(KT, w_gate[l], a * P)))
                    units.append((("up", l, a), *full(KT, w_up[l], a * P)))
                else:
                    n = DOWN_K[a]
                    for m in range(0, KT, 2):
                        units.append((("down", l, a, m), *full(n, w_down[l][f0 * P:(f0 + n) * P], m * P)))

        ffn_units(0)
        for i in range(KT):
            g = [(lambda r, j=j: r.rearrange("p (k n) -> p k n", k=KT)[:, :, j * P:(j + 1) * P],
                  cols(w_pw1[0], j * D + i * P, P)) for j in range(2)]
            units.append((("glu", i), UNIT, g))
        for m in range(0, KT, 2):
            units.append((("pw2", m), *full(KT, w_pw2[0], m * P)))
        ffn_units(1)
        U = {u[0]: i for i, u in enumerate(units)}
        landed = []
        count = [0, 0]
        for i, u in enumerate(units):
            count[i % 2] += 16 * len(u[2])
            landed.append(count[i % 2])

        LAST = {"dq": lambda n: ("dq", n[1] + 1), "dkv": lambda n: ("dkv", min(n[1] + 1, KVT)),
                "head": lambda n: ("v", n[1]), "wo": lambda n: ("wo", n[1] + 1),
                "gate": lambda n: ("gate", n[1], n[2] + 1), "up": lambda n: ("up", n[1], n[2] + 1),
                "down": lambda n: ("down", n[1], n[2], n[3] + 1), "glu": lambda n: ("b", n[1]),
                "pw2": lambda n: ("pw2", n[1] + 1)}
        unit_last = [LAST[u[0][0]](u[0]) for u in units]

        NORMS, DIAGS, nsum, ndiag = {}, {}, 0, 0
        for n, adds in (("mix0", KT), ("cq", QLT), ("ck", KVT), ("ffn0", KT), ("mix1", KT), ("mu", KT), ("ln", KT), ("ffn1", KT)):
            nsum += adds - 1
            NORMS[n] = nsum
        for n in ["mix0", "cq", "ck"] + [("rk", h) for h in range(HEADS)] + ["ffn0", "mix1", "ln", "ffn1"]:
            DIAGS[n] = ndiag
            ndiag += NKT if isinstance(n, tuple) else QT
        SQ_BASE, nsq = {}, 0
        for n, tiles in (("mix0", KT), ("cq", QLT), ("ck", KVT), ("ffn0", KT), ("mix1", KT), ("ln", KT), ("ffn1", KT)):
            SQ_BASE[n] = nsq
            nsq += tiles
        APPLY = {"mix0": 0, "ffn0": 1, "mix1": 2, "ln": 3, "ffn1": 4}

        n_vec, n_late = [0], [0]

        block = ctx.enter_context(nc.Block())

        @block.sync
        def _(sp):
            def vec(dst, src):
                sp.dma_start(dst, src).then_inc(sem("vec_landed"), 16)
                n_vec[0] += 16

            def late(dst, src):
                sp.dma_start(dst, src).then_inc(sem("late_landed"), 16)
                n_late[0] += 16

            rows = lambda a: a.rearrange("(r p) -> r p", p=P)
            flat = lambda a: a.rearrange("l n -> (l n)")
            sp.dma_start(EYE[:], const["eye"]).then_inc(sem("eye_landed"), 16)
            vec(ROWS[0:96, :], rows(flat(b_mod)))
            vec(ROWS[96:112, :], rows(flat(norm_mix)))
            vec(ROWS[112:128, :], rows(flat(norm_ffn)))
            for n, a in (("q_norm", q_norm), ("kv_norm", kv_norm), ("b_pw1", b_pw1), ("b_dw", b_dw),
                         ("ln_g", ln_g), ("ln_b", ln_b), ("b_pw2", b_pw2), ("c", c)):
                r = rows(flat(a))
                vec(ROWS2[V2[n]:V2[n] + r.shape[0], :], r)
            vec(ROWS2[V2["c_ctx"]:V2["c_ctx"] + KT, :], rows(c_ctx))
            for n, a in (("gq", q_hn), ("gk", k_hn)):
                vec(ROWS2[V2[n]:V2[n] + 1, :], a[0:1, 0:NOPE])
                for i in range(2):
                    vec(ROWS2[V2[n + "_pe"]:V2[n + "_pe"] + 1, i * ROPE:(i + 1) * ROPE], a[0:1, NOPE:QK])
            late(ROT[:], const["rot"])
            late(TAPROWS[:], w_dw[0])
            late(CROWS[:, 0:KVL], cache_ckv[0, 0])
            for i in range(2):
                late(CROWS[:, KVL + i * ROPE:KVL + (i + 1) * ROPE], cache_kpe[0, 0])

            for i, (name, _, pieces) in enumerate(units):
                if name == ("head", 0):
                    filled(sp, "mods")
                    sp.dma_start(COS[:], const["cos"]).then_inc(sem("rope_landed"), 16)
                    sp.dma_start(SIN[:], const["sin"]).then_inc(sem("rope_landed"), 16)
                if name == ("wo", 0):
                    filled(sp, ("rk", HEADS - 1))
                if i >= 2:
                    sp.wait_ge(lo_done, i - 1)
                for view, src in pieces:
                    sp.dma_start(view(RAW[:, i % 2, :]), src).then_inc(raw_landed[i % 2], 16)
                if name == ("head", 2):
                    was_read(sp, "ctxout")
                    sp.dma_start(new_ckv[0, 0], CKOUT[:, 0:KVL]).then_inc(sem("stored"), 16)
                    sp.dma_start(new_kpe[0, 0], CKOUT[:, KVL:]).then_inc(sem("stored"), 16)
            for t in range(QT):
                was_read(sp, ("y", t))
                dst = y_prompt[0] if t == 0 else y_sample[0, (t - 1) * P:t * P, :]
                sp.dma_start(dst, YROW[t][:]).then_inc(sem("y_stored"), 16)
            sp.wait_ge(sem("stored"), 32)
            sp.wait_ge(sem("y_stored"), 16 * QT)

        @block.gpsimd
        def _(pool):
            for k in range(KT):
                if k >= 5:
                    pool.wait_ge(sem("mods_used"), k - 4)
                pool.dma_start(MODS[:, k % 5], w_mod[0, k * P:(k + 1) * P, 0:2 * D]).then_inc(mods_landed[k % 5], 16)
            filled(pool, ("dkv", 1))
            for i in range(N_ROWS * KT):
                if i >= ROW_SLOTS:
                    row_used(pool, i - ROW_SLOTS)
                j, k = divmod(i, KT)
                pool.dma_start(MODA[i % ROW_SLOTS][:], w_mod[0, k * P:(k + 1) * P, 2 * D + j * 512:2 * D + (j + 1) * 512]).then_inc(moda_landed[i % ROW_SLOTS], 16)
            filled(pool, ("o", HEADS - 1, 2))
            pool.wait_ge(sem("stored"), 32)
            for i in range(N_HALF * KT):
                j, k = divmod(i, KT)
                if i >= BG_SLOTS:
                    pool.wait_ge(sem("bgw_used"), i - BG_SLOTS + 1)
                l, c0 = divmod(FIRST_BG * D + j * 512, 6 * D)
                pool.dma_start(BGW[i % BG_SLOTS][:], w_mod[l, k * P:(k + 1) * P, c0:c0 + 512]).then_inc(bgw_landed[i % BG_SLOTS], 16)
            pool.wait_ge(sem("taps_split"), 1)
            for n in range(KT * PE_TAPS):
                if n >= DIAG_SLOTS:
                    tap_done(pool, n - DIAG_SLOTS)
                i, j = divmod(n, PE_TAPS)
                nc.gpsimd.tensor_scalar(TDL[:, n % DIAG_SLOTS, :], EYE[:], WTL[:, i, j:j + 1], None,
                                        ALU.mult).then_inc(sem("tap_lo"), 1)

        @block.tensor
        def _(pe):
            mm = nc.tensor.matmul
            n_mod = [0]
            n_unit = [0]

            def begin(name):
                n = T[name]
                if n >= 4:
                    pe.wait_ge(tile_read[n % 4], n // 4)
                return tile2(name)

            def split3(outs, wh, wl, xs, first, last):
                for o, (xh, xl) in zip(outs, xs):
                    mm(o, wh, xh, start=first, stop=False)
                for o, (xh, xl) in zip(outs, xs):
                    mm(o, wh, xl, start=False, stop=False)
                ins = None
                for o, (xh, xl) in zip(outs, xs):
                    ins = mm(o, wl, xh, start=False, stop=last)
                return ins

            def halves(ps, n=HALF):
                return [ps[:, 0, 0:n], ps[:, 1, 0:n]]

            def unit_begin(name):
                assert U[name] == n_unit[0], name
                pe.wait_ge(lo_done, n_unit[0] + 1)
                s = n_unit[0] % 2
                n_unit[0] += 1
                return WH[:, s, :], WL[:, s, :]

            def product(name, w, a, kt, step, xh, xl, n=HALF, wait=None, between=None):
                ps = begin(name)
                o = halves(ps, n)
                for k in range(kt):
                    if wait is not None:
                        wait(k)
                    wa = a + k * step
                    ins = split3(o, w[0][:, wa:wa + P], w[1][:, wa:wa + P],
                                 [(xh[:, k, i * n:(i + 1) * n], xl[:, k, i * n:(i + 1) * n]) for i in range(2)],
                                 k == 0, k == kt - 1)
                    if between is not None and k < kt - 1:
                        between(k)
                return ins

            def half_begin(j):
                pe.wait_ge(sem("bgw_used"), KT * (j + 1))
                return begin(("mh", j))

            def half_part(ps, j, i):
                c, s = divmod(i, 2)
                ins = mm(ps[:, 0, i:i + 1], BGACC[j % 2][:, s, c * P:(c + 1) * P], ONES[:, 0:1], start=True, stop=True)
                if i == 7:
                    ins.then_inc(mm_done, 1)

            def stat(n):
                ps = begin(("stat", n))
                pe.wait_ge(sem("sq_added"), NORMS[n])
                for t in range(QT):
                    ins = mm(ps[:, 0, t:t + 1], SUM[:, t * P:(t + 1) * P], ONES[:, 0:1], start=True, stop=True)
                ins.then_inc(mm_done, 1)

            def spread(name, diags, first):
                ps = begin(name)
                for t, d in enumerate(diags):
                    pe.wait_ge(sem("diag_ready"), first + t + 1)
                    ins = mm(ps[:, t // 3, (t % 3) * P:(t % 3 + 1) * P], ONES[:], d, start=True, stop=True)
                ins.then_inc(mm_done, 1)

            diagn = [DIAGN[:, t, :] for t in range(QT)]

            tr = nc.tensor.transpose
            pe.wait_ge(sem("eye_landed"), 16)
            pe.wait_ge(sem("x_landed"), 32)
            for k in range(KT):
                ps = begin(("x", k))
                for t in range(QT):
                    ins = tr(ps[:, t // 3, (t % 3) * P:(t % 3 + 1) * P], XROWS[:, t, k * P:(k + 1) * P], EYE[:])
                ins.then_inc(mm_done, 1)
            pe.wait_ge(sem("vec_landed"), n_vec[0])
            pe.wait_ge(sem("ones_set"), 1)
            ps = begin("vec")
            tr(ps[:, 0, 0:P], ROWS[:], EYE[:])
            tr(ps[:, 0, P:P + NV2], ROWS2[:], EYE[0:NV2, 0:NV2]).then_inc(mm_done, 1)
            stat("mix0")
            pe.wait_ge(sem("late_landed"), n_late[0])
            ps = begin("taps")
            for k in range(KT):
                ins = tr(ps[:, 0, k * TAPS:(k + 1) * TAPS], TAPROWS[:, k * P:(k + 1) * P], EYE[0:TAPS, 0:TAPS])
            ins.then_inc(mm_done, 1)
            ps = begin("cache")
            for j in range(KVT + 1):
                ins = tr(ps[:, 0, j * P:(j + 1) * P], CROWS[:, j * P:(j + 1) * P], EYE[:])
            ins.then_inc(mm_done, 1)
            spread(("rb", "mix0"), diagn, DIAGS["mix0"])
            pe.wait_ge(sem("sc_ready"), 2)
            rows = [begin(("mrow", i)) for i in range(2)]
            for k in range(KT):
                pe.wait_ge(mods_landed[k % 5], 16 * (k // 5 + 1))
                for i in range(4):
                    ins = mm(rows[i // 2][0:2, i % 2, :], SC[:, k, :], MODS[:, k % 5, i * 512:(i + 1) * 512],
                             start=(k == 0), stop=(k == KT - 1))
                    if k == KT - 1 and i % 2:
                        ins.then_inc(mm_done, 1)
                if k < KT - 1:
                    ins.then_inc(sem("mods_used"), 1)
            ps = begin("mods")
            for i in range(2 * KT):
                if i % KT == 0:
                    was_read(pe, ("mrow", i // KT))
                ins = tr(ps[:, 0, 2 * i:2 * i + 2], MROW[:, i * P:(i + 1) * P], EYE[0:2, 0:2])
            ins.then_inc(mm_done, 1)

            h_wait = lambda n: (lambda k: pe.wait_ge(sem("h_ready"), KT * n + k + 1))
            for m in range(0, QLT, 2):
                w = unit_begin(("dq", m))
                for j in range(2):
                    ins = product(("dq", m + j), w, j * P, KT, 256, HH, HL, wait=h_wait(APPLY["mix0"]) if m + j == 0 else None)
                    ins.then_inc(mm_done, 1)
            w = unit_begin(("dkv", 0))
            for j in range(2):
                product(("dkv", j), w, j * P, KT, 256, HH, HL).then_inc(mm_done, 1)
            w = unit_begin(("dkv", 2))
            product(("dkv", 2), w, 0, KT, P, HH, HL).then_inc(mm_done, 1)
            for n in ("cq", "ck"):
                stat(n)
                spread(("rb", n), diagn, DIAGS[n])
            ps = begin("kpstat")
            pe.wait_ge(sem("kpsq_ready"), 1)
            for t in range(NKT):
                ins = mm(ps[:, 0, t:t + 1], KPSQ[0:ROPE, t * P:(t + 1) * P], ONES[0:ROPE, 0:1], start=True, stop=True)
            ins.then_inc(mm_done, 1)
            ps = begin("kprot")
            pe.wait_ge(sem("kpg_ready"), 1)
            mm(ps[:, 0, :], ROT[:], KPSQ[:, KEYS - LAT:KEYS], start=True, stop=True).then_inc(mm_done, 1)
            ps = begin("ctxout")
            pe.wait_ge(sem("ckn_ready"), KVT)
            for j in range(KVT):
                tr(ps[:, 0, j * P:(j + 1) * P], CKN[:, j, :], EYE[:])
            tr(ps[:, 0, KVL:KVL + ROPE], KPRAW[0:ROPE, 0:CTX], EYE[0:ROPE, 0:ROPE]).then_inc(mm_done, 1)

            def queries(h):
                w = unit_begin(("head", h))
                product(("qn", h), w, 0, QLT, P, CQH, CQL).then_inc(mm_done, 1)
                if h % 2 == 0:
                    product(("pe", h), w, 1024, QLT, P, CQH, CQL).then_inc(mm_done, 1)

            def keys(h):
                s = U[("head", h)] % 2
                product(("kn", h), (WH[:, s, :], WL[:, s, :]), 512, KVT, 256, CKH, CKL, n=KEYS // 2).then_inc(mm_done, 1)
                if h % 2 == 0:
                    ps = begin(("rot", h))
                    was_read(pe, ("pe", h))
                    mm(ps[:, 0, :], ROT[:], PEG[:, CTX:TOK], start=True, stop=True).then_inc(mm_done, 1)

            def head_stat(h, half=None):
                lo, hi = (0, ROPE) if h % 2 == 0 else (ROPE, P)
                ps = begin(("hstat", h))
                pe.wait_ge(sem("qn_hi"), h + 1)
                pe.wait_ge(sem("pe_sq"), h // 2 + 1)
                if half is not None:
                    rows = begin(("ma", half))
                for k in range(KT):
                    if half is not None and k < KT - 1:
                        modulate(rows, half, k)
                    for t in ((0,), (1,), (2,), (3, 4), (5, 6), (7, 8), (9, 10), ())[k]:
                        o = ps[:, 0, t:t + 1]
                        if t < QT:
                            mm(o, QSQ[:, t * P:(t + 1) * P], ONES[:, 0:1], start=True, stop=False)
                            mm(o, PESQ[lo:hi, t * P:(t + 1) * P], ONES[lo:hi, 0:1], start=False, stop=True)
                        else:
                            if t == QT:
                                pe.wait_ge(sem("kn_hi"), h + 1)
                            ins = mm(o, KSQ[:, (t - QT) * P:(t - QT + 1) * P], ONES[:, 0:1], start=True, stop=True)
                ins.then_inc(mm_done, 1)
                if half is not None:
                    modulate(rows, half, KT - 1)

            def modulate(ps, j, k):
                i = KT * j + k
                pe.wait_ge(moda_landed[i % ROW_SLOTS], 16 * (i // ROW_SLOTS + 1))
                ins = mm(ps[0:2, 0, :], SC[:, k, :], MODA[i % ROW_SLOTS][:], start=(k == 0), stop=(k == KT - 1))
                ins.then_inc(sem("rows_used") if k < KT - 1 else mm_done, 1)

            def turn_rows(j):
                ps = begin(("mb", j))
                was_read(pe, ("ma", j))
                for i in range(4):
                    ins = tr(ps[:, 0, 2 * i:2 * i + 2], MROWA[:, i * P:(i + 1) * P], EYE[0:2, 0:2])
                ins.then_inc(mm_done, 1)

            def key_spread(h):
                spread(("rk", h), [d[:] for d in DIAGK], DIAGS[("rk", h)])

            def values(h):
                s = U[("head", h)] % 2
                ps = begin(("v", h))
                for t in range(NKT):
                    o = ps[:, t // 3, (t % 3) * P:(t % 3 + 1) * P]
                    for k in range(KVT):
                        wa = 512 + k * 256 + P
                        ks = slice(t * P, (t + 1) * P)
                        mm(o, CKH[:, k, ks], WH[:, s, wa:wa + P], start=(k == 0), stop=False)
                        mm(o, CKH[:, k, ks], WL[:, s, wa:wa + P], start=False, stop=False)
                        ins = mm(o, CKL[:, k, ks], WH[:, s, wa:wa + P], start=False, stop=(k == KVT - 1))
                ins.then_inc(mm_done, 1)

            def scores(h, t):
                ps = begin(("s", h, t))
                lo, hi = (0, ROPE) if h % 2 == 0 else (ROPE, P)
                q = slice(t * P, (t + 1) * P)
                if t == 0:
                    outs, keys = [ps[:, 0, 0:CTX]], [slice(0, CTX)]
                else:
                    outs, keys = halves(ps), [slice(CTX, CTX + 320), slice(CTX + 320, KEYS)]
                split3(outs, QNH[:, q], QNL[:, q], [(KNH[:, k], KNL[:, k]) for k in keys], True, False)
                ins = split3(outs, QPH[lo:hi, q], QPL[lo:hi, q], [(KPH[lo:hi, k], KPL[lo:hi, k]) for k in keys], False, True)
                ins.then_inc(mm_done, 1)

            def turn(h, t):
                ps = begin(("pt", h, t))
                pe.wait_ge(sem("prob_ready"), QT * h + t + 1)
                if t == 0:
                    tr(ps[:, 0, 0:P], PROBC[:], EYE[:]).then_inc(mm_done, 1)
                    return
                for k in range(5):
                    ins = tr(ps[:, k // 3, (k % 3) * P:(k % 3 + 1) * P], PROB[:, t - 1, k * P:(k + 1) * P], EYE[:])
                ins.then_inc(mm_done, 1)

            def weighted(h, g):
                ps = begin(("o", h, g))
                if g == 0:
                    was_read(pe, ("pt", h, 0))
                    split3([ps[:, 0, 0:P]], VH[:, 0, :], VL[:, 0, :], [(PTCH[:], PTCL[:])], True, True).then_inc(mm_done, 1)
                    return
                was_read(pe, ("pt", h, 2 * g - 1))
                was_read(pe, ("pt", h, 2 * g))
                for k in range(5):
                    ins = split3([ps[:, 0, 0:256]], VH[:, k + 1, :], VL[:, k + 1, :],
                                 [(PTH[:, g - 1, k, :], PTL[:, g - 1, k, :])], k == 0, k == 4)
                ins.then_inc(mm_done, 1)

            def head_ready(h):
                was_read(pe, ("qn", h))
                was_read(pe, ("kn", h))
                pe.wait_ge(sem("qp_ready"), h // 2 + 1)

            pe.wait_ge(sem("cq_ready"), QLT)
            queries(0)
            pe.wait_ge(sem("ck_ready"), KVT)
            keys(0)
            head_stat(0)
            values(0)
            key_spread(0)
            for h in range(HEADS):
                head_ready(h)
                if h == 0:
                    pe.wait_ge(sem("kp_ready"), 1)
                for t in range(QT):
                    scores(h, t)
                more = h + 1 < HEADS
                if more:
                    queries(h + 1)
                for t in range(QT):
                    turn(h, t)
                if more:
                    keys(h + 1)
                    head_stat(h + 1, h if h < N_ROWS else None)
                was_read(pe, ("v", h))
                for g in range(3):
                    weighted(h, g)
                if h < N_ROWS:
                    turn_rows(h)
                if more:
                    values(h + 1)
                    key_spread(h + 1)

            for m in range(0, KT, 2):
                w = unit_begin(("wo", m))
                for j in range(2):
                    product(("wo", m + j), w, j * P, KT, 256, OH, OL,
                            wait=(lambda k: pe.wait_ge(sem("o_split"), k + 1)) if m + j == 0 else None).then_inc(mm_done, 1)

            def halves_of(l, pair):
                return [j for j in range(N_HALF) if l == 0 and half_pair(j) == pair]

            def ffn(l):
                n = f"ffn{l}"
                stat(n)
                spread(("rb", n), diagn, DIAGS[n])
                for kind, a, f0 in ffn_steps():
                    if kind == "pair":
                        for g in ("gate", "up"):
                            w = unit_begin((g, l, a))
                            for j in range(2):
                                part = None
                                if g == "up" and j < len(halves_of(l, a // 2)):
                                    jh = halves_of(l, a // 2)[j]
                                    pm = half_begin(jh)
                                    part = lambda k, pm=pm, jh=jh: [half_part(pm, jh, i) for i in ((k,) if k < 6 else (6, 7))]
                                product((g, l, a + j), w, j * P, KT, 256, HH, HL, between=part,
                                        wait=h_wait(APPLY[f"ffn{l}"]) if g == "gate" and a + j == 0 else None).then_inc(mm_done, 1)
                    else:
                        pe.wait_ge(sem("hid_ready"), FT * l + f0 + DOWN_K[a])
                        for m in range(0, KT, 2):
                            w = unit_begin(("down", l, a, m))
                            for j in range(2):
                                ps = begin(("down", l, a, m + j))
                                for k in range(DOWN_K[a]):
                                    hs = (f0 + k) % HID_SLOTS
                                    wa = k * 256 + j * P
                                    ins = split3(halves(ps), w[0][:, wa:wa + P], w[1][:, wa:wa + P],
                                                 [(HIDH[:, hs, i * HALF:(i + 1) * HALF], HIDL[:, hs, i * HALF:(i + 1) * HALF])
                                                  for i in range(2)], k == 0, k == DOWN_K[a] - 1)
                                ins.then_inc(mm_done, 1)

            ffn(0)
            for j in halves_of(0, FT // 2):
                ps = half_begin(j)
                for i in range(8):
                    half_part(ps, j, i)
            stat("mix1")
            spread(("rb", "mix1"), diagn, DIAGS["mix1"])
            def conv(i):
                ps = begin(("cv", i))
                pe.wait_ge(sem("gp_lo"), i + 1)
                for j in range(PE_TAPS):
                    n = i * PE_TAPS + j
                    pe.wait_ge(sem("tap_hi"), n + 1)
                    pe.wait_ge(sem("tap_lo"), n + 1)
                    ins = split3(halves(ps, CHALF), TDH[:, n % DIAG_SLOTS, :], TDL[:, n % DIAG_SLOTS, :],
                                 [(GPH[i % 2][:, j + b * CHALF:j + (b + 1) * CHALF], GPL[i % 2][:, j + b * CHALF:j + (b + 1) * CHALF])
                                  for b in range(2)], j == 0, j == PE_TAPS - 1)
                    if j < PE_TAPS - 1:
                        ins.then_inc(sem("tap_used"), 1)
                ins.then_inc(mm_done, 1)

            for i in range(KT):
                w = unit_begin(("glu", i))
                for j, n in enumerate(("a", "b")):
                    product((n, i), w, j * P, KT, 256, HH, HL, wait=h_wait(APPLY["mix1"]) if i + j == 0 else None).then_inc(mm_done, 1)
                if i:
                    conv(i - 1)
            conv(KT - 1)
            ps = begin("mu")
            pe.wait_ge(sem("sq_added"), NORMS["mu"])
            for i in range(2):
                ins = mm(ps[:, i, 0:HALF], ONES[:], SUM[:, i * HALF:(i + 1) * HALF], start=True, stop=True)
            ins.then_inc(mm_done, 1)
            stat("ln")
            spread(("rb", "ln"), diagn, DIAGS["ln"])
            for m in range(0, KT, 2):
                w = unit_begin(("pw2", m))
                for j in range(2):
                    product(("pw2", m + j), w, j * P, KT, 256, HH, HL,
                            wait=h_wait(APPLY["ln"]) if m + j == 0 else None).then_inc(mm_done, 1)
            ffn(1)
            was_read(pe, ("down", 1, len(DOWN_K) - 1, KT - 2))
            was_read(pe, ("down", 1, len(DOWN_K) - 1, KT - 1))
            for t in range(QT):
                ps = begin(("y", t))
                for k in range(KT):
                    ins = tr(ps[:, k // 4, (k % 4) * P:(k % 4 + 1) * P], X[:, k, t * P:(t + 1) * P], EYE[:])
                ins.then_inc(mm_done, 1)

        @block.scalar
        def _(act):
            A = nc.scalar.activation
            n_hi = [0]
            n_sq = [0]

            def round_units(upto):
                while n_hi[0] <= min(upto, len(units) - 1):
                    u = n_hi[0]
                    act.wait_ge(raw_landed[u % 2], landed[u])
                    if u >= 2:
                        filled(act, unit_last[u - 2])
                    n = units[u][1]
                    A(WH[:, u % 2, 0:n], RAW[:, u % 2, 0:n], ACT.Copy).then_inc(hi_done, 1)
                    n_hi[0] += 1

            def square(norm, m, src, tiles=KT):
                before = NORMS[norm] - (tiles - 1)
                need = before + (max(m - 2, 1) if m >= 2 else 0)
                if need:
                    act.wait_ge(sem("sq_added"), need)
                dst = SQ[m % 2][:] if len(src.shape) == 2 else row2(SQ[m % 2][:])
                A(dst, src, ACT.Square).then_inc(sem("sq_made"), 1)

            def spread_copy(name, dst, n):
                filled(act, name)
                ps = tile2(name)
                A(dst[:, 0:3 * P], ps[:, 0, 0:3 * P], ACT.Copy)
                A(dst[:, 3 * P:n * P], ps[:, 1, 0:(n - 3) * P], ACT.Copy).then_inc(free_of(name), 1)

            def apply(norm, l, half):
                for k in range(KT):
                    act.wait_ge(sem("t_ready"), KT * APPLY[norm] + k + 1)
                    for a, b, s in SEGS:
                        ins = A(HH[:, k, a:b], SCALED[k % 3][:, a:b], ACT.Identity,
                                bias=MODV[:, l, s, 24 * half + k:24 * half + k + 1])
                    ins.then_inc(sem("part_hi"), 1)

            act.dma_start(XROWS[:, 0, :], x_prompt[0]).then_inc(sem("x_landed"), 16)
            act.dma_start(XROWS[:, 1:QT, :], x_sample[0].rearrange("(t p) d -> p t d", p=P)).then_inc(sem("x_landed"), 16)
            for k in range(KT):
                was_read(act, ("x", k))
                square("mix0", k, X[:, k, :])
            was_read(act, "vec")
            A(SC[:, :, 0], VT2[:, V2["c_ctx"]:V2["c_ctx"] + KT], ACT.Silu).then_inc(sem("sc_ready"), 1)
            A(SC[:, :, 1], VT2[:, V2["c"]:V2["c"] + KT], ACT.Silu).then_inc(sem("sc_ready"), 1)
            round_units(1)
            filled(act, "cache")
            ps = tile2("cache")
            A(CKH[:, :, CTX:CTX + PAST], ps[:, 0, 0:KVL].rearrange("p (j t) -> p j t", j=KVT), ACT.Copy).then_inc(sem("cache_hi"), 1)
            spread_copy(("rb", "mix0"), RSTD, QT)
            for i in range(2):
                filled(act, ("mrow", i))
                A(MROW[:, i * D:(i + 1) * D].rearrange("p (b n) -> p b n", b=2), tile2(("mrow", i))[0:2, :, :],
                  ACT.Copy).then_inc(free_of(("mrow", i)), 1)
            apply("mix0", 0, 0)
            for m in range(QLT):
                if m % 2 == 0:
                    round_units(U[("dq", m)] + 1)
                filled(act, ("dq", m))
                square("cq", m, tile2(("dq", m))[:, :, 0:HALF], QLT)
                A(row2(CQRAW[:, m, :]), tile2(("dq", m))[:, :, 0:HALF], ACT.Copy).then_inc(free_of(("dq", m)), 1)
            round_units(U[("dkv", 0)] + 1)
            for m in range(KVT):
                filled(act, ("dkv", m))
                square("ck", m, tile2(("dkv", m))[:, :, 0:HALF], KVT)
                A(row2(CKRAW[:, m, :]), tile2(("dkv", m))[:, :, 0:HALF], ACT.Copy).then_inc(free_of(("dkv", m)), 1)
            round_units(U[("dkv", 2)] + 1)
            n = ("dkv", KVT)
            filled(act, n)
            for bank, a, b, t, s in PSEGS:
                to = t if s == 0 else t + PAST
                ins = A(KPRAW[:, to:to + b - a], tile2(n)[:, bank, a:b], ACT.Copy)
            ins.then_inc(free_of(n), 1)
            was_read(act, n)
            was_read(act, "cache")
            A(KPSQ[:], KPRAW[:], ACT.Square).then_inc(sem("kpsq_ready"), 1)
            spread_copy(("rb", "cq"), RSTD, QT)
            for m in range(QLT):
                act.wait_ge(sem("cq_t"), m + 1)
                A(CQH[:, m, :], TMP[m % 2][:], ACT.Copy).then_inc(sem("cq_hi"), 1)
            spread_copy(("rb", "ck"), RSTD, QT)
            for m in range(KVT):
                act.wait_ge(sem("ck_t"), m + 1)
                A(CKH[:, m, 0:CTX], TMP[m % 2][:, 0:CTX], ACT.Copy)
                A(CKH[:, m, CTX + PAST:KEYS], TMP[m % 2][:, CTX:TOK], ACT.Copy).then_inc(sem("ck_hi"), 1)
            act.wait_ge(sem("kp_rotated"), 1)
            A(KPH[:], KPSQ[:], ACT.Copy).then_inc(sem("kp_hi"), 1)
            filled(act, "ctxout")
            A(CKOUT[:], tile2("ctxout")[:, 0, 0:KVL + ROPE], ACT.Copy).then_inc(free_of("ctxout"), 1)

            def queries(h):
                round_units(U[("head", min(h + 1, HEADS - 1))])
                n = ("qn", h)
                filled(act, n)
                A(row2(QNH[:]), tile2(n)[:, :, 0:HALF], ACT.Copy, scale=GQK[:, 0:1])
                A(row2(QSQ[:]), tile2(n)[:, :, 0:HALF], ACT.Square).then_inc(sem("qn_hi"), 1)
                if h % 2 == 0:
                    n = ("pe", h)
                    filled(act, n)
                    A(row2(PESQ[:]), tile2(n)[:, :, 0:HALF], ACT.Square).then_inc(sem("pe_sq"), 1)

            def keys(h):
                n = ("kn", h)
                filled(act, n)
                k2 = lambda r: r.rearrange("p (b t) -> p b t", b=2)
                A(k2(KSQ[:]), tile2(n)[:, :, 0:KEYS // 2], ACT.Square)
                A(k2(KNH[:]), tile2(n)[:, :, 0:KEYS // 2], ACT.Copy).then_inc(sem("kn_hi"), 1)
                if h % 2 == 0:
                    act.wait_ge(sem("q_rotated"), h // 2 + 1)
                    A(QPH[:], PEG[:], ACT.Copy).then_inc(sem("qp_hi"), 1)

            def values(h):
                n = ("v", h)
                filled(act, n)
                A(VH[:].rearrange("p (b j) v -> p b (j v)", b=2), tile2(n)[:, :, 0:3 * P], ACT.Copy).then_inc(sem("v_hi"), 1)

            queries(0)
            keys(0)
            values(0)
            spread_copy(("rk", 0), RK, NKT)
            for h in range(HEADS):
                for t in range(QT):
                    p = PROBC[:] if t == 0 else PROB[:, t - 1, :]
                    act.wait_ge(sem("nb_ready"), QT * h + t + 1)
                    A(p, p, ACT.Exp, bias=NB8[:, t:t + 1], scale=RQ[h % 2][:, t:t + 1],
                      accum_out=SUM8[:, t:t + 1]).then_inc(sem("exp_done"), 1)
                if h + 1 < HEADS:
                    queries(h + 1)
                for t in range(QT):
                    n = ("pt", h, t)
                    filled(act, n)
                    if t == 0:
                        A(PTCH[:], tile2(n)[:, 0, 0:P], ACT.Copy).then_inc(sem("pt_hi"), 1)
                    else:
                        g, c0 = (t - 1) // 2, (t - 1) % 2 * P
                        for bank, k0, k1 in ((0, 0, 3), (1, 3, 5)):
                            ins = A(PTH[:, g, k0:k1, c0:c0 + P],
                                    tile2(n)[:, bank, 0:(k1 - k0) * P].rearrange("p (k q) -> p k q", q=P), ACT.Copy)
                        ins.then_inc(sem("pt_hi"), 1)
                if h + 1 < HEADS:
                    keys(h + 1)
                if h < N_ROWS:
                    filled(act, ("ma", h))
                    A(MROWA[:], tile2(("ma", h))[0:2, 0, :], ACT.Copy).then_inc(free_of(("ma", h)), 1)
                for g in range(3):
                    n = ("o", h, g)
                    filled(act, n)
                    a, b = ((0, CTX), (CTX, CTX + 256), (CTX + 256, TOK))[g]
                    A(O[:, h, a:b], tile2(n)[:, 0, 0:b - a], ACT.Copy).then_inc(free_of(n), 1)
                if h + 1 < HEADS:
                    values(h + 1)
                    spread_copy(("rk", h + 1), RK, NKT)
            filled(act, ("ma", N_ROWS - 1))
            round_units(U[("wo", 0)])
            for k in range(HEADS):
                was_read(act, ("o", HEADS - 1, 2))
                A(OH[:, k, :], O[:, k, :], ACT.Copy).then_inc(sem("o_hi"), 1)

            for m in range(KT):
                if m % 2 == 0:
                    round_units(U[("wo", m)] + 1)
                was_read(act, ("wo", m))
                square("ffn0", m, X[:, m, :])

            def ffn(l):
                n = f"ffn{l}"
                spread_copy(("rb", n), RSTD, QT)
                apply(n, l, 1)
                nf = 0
                for kind, a, f0 in ffn_steps():
                    if kind == "pair":
                        round_units(U[("gate", l, a)] + 1)
                        for j in range(2):
                            n = ("gate", l, a + j)
                            filled(act, n)
                            if a >= 2:
                                was_read(act, ("up", l, a + j - 2))
                            A(row2(ACTV[j][:]), tile2(n)[:, :, 0:HALF], ACT.Silu).then_inc(free_of(n), 1)
                        round_units(U[("up", l, a)] + 1)
                        for j in range(2):
                            was_read(act, ("up", l, a + j))
                            A(HIDH[:, (a + j) % HID_SLOTS, :], TMP[j][:], ACT.Copy).then_inc(sem("hid_hi"), 1)
                    else:
                        for m in range(KT):
                            if m % 2 == 0:
                                round_units(U[("down", l, a, m)] + 1)
                            if l == 0 and a == len(DOWN_K) - 1:
                                was_read(act, ("down", l, a, m))
                                square("mix1", m, X[:, m, :])

            ffn(0)
            A(WTH[:], WTAP[:], ACT.Copy).then_inc(sem("wth_ready"), 1)
            spread_copy(("rb", "mix1"), RSTD, QT)
            apply("mix1", 1, 0)

            def tap_diagonals(i):
                for j in range(PE_TAPS):
                    n = i * PE_TAPS + j
                    if n >= DIAG_SLOTS:
                        tap_done(act, n - DIAG_SLOTS)
                    A(TDH[:, n % DIAG_SLOTS, :], EYE[:], ACT.Copy, scale=WTH[:, i, j:j + 1].bitcast(F32)).then_inc(sem("tap_hi"), 1)

            def gated(i):
                was_read(act, ("a", i))
                A(GPH[i % 2][:], GP[i % 2][:], ACT.Copy).then_inc(sem("gp_hi"), 1)

            tap_diagonals(0)
            for i in range(KT):
                round_units(U[("glu", i)] + 1)
                n = ("b", i)
                filled(act, n)
                if i >= 2:
                    was_read(act, ("a", i - 2))
                c0 = V2["b_pw1"] + KT + i
                A(row2(ACTV[i % 2][:]), tile2(n)[:, :, 0:HALF], ACT.Sigmoid, bias=VT2[:, c0:c0 + 1]).then_inc(free_of(n), 1)
                gated(i)
                if i + 1 < KT:
                    tap_diagonals(i + 1)
            for i in range(KT):
                act.wait_ge(sem("y_centred"), i + 1)
                square("ln", i, Y[:, i, :])
            spread_copy(("rb", "ln"), RSTD, QT)
            for k in range(KT):
                act.wait_ge(sem("t_ready"), KT * APPLY["ln"] + k + 1)
                if k >= 2:
                    act.wait_ge(sem("h_ready"), KT * APPLY["ln"] + k - 1)
                c0 = V2["ln_b"] + k
                A(ACTV[k % 2][:], SCALED[k % 3][:], ACT.Silu, bias=VT2[:, c0:c0 + 1]).then_inc(sem("swish"), 1)
                act.wait_ge(sem("swish"), k + 1)
                A(HH[:, k, :], ACTV[k % 2][:], ACT.Copy).then_inc(sem("part_hi"), 1)
            for m in range(KT):
                if m % 2 == 0:
                    round_units(U[("pw2", m)] + 1)
                was_read(act, ("pw2", m))
                square("ffn1", m, X[:, m, :])
            ffn(1)
            for t in range(QT):
                n = ("y", t)
                filled(act, n)
                A(YROW[t][:, 0:512], tile2(n)[:, 0, :], ACT.Copy).then_inc(sem("y_half"), 1)

        @block.vector
        def _(dve):
            V = nc.vector
            n_lo, n_add, n_chain, n_t, n_part, n_bg = [0], [0], [0], [0], [0], [0]

            def link(ins):
                n_chain[0] += 1
                ins.then_inc(sem("dve_chain"), 1)
                dve.wait_ge(sem("dve_chain"), n_chain[0])

            def split_units(upto):
                while n_lo[0] <= min(upto, len(units) - 1):
                    u = n_lo[0]
                    dve.wait_ge(hi_done, u + 1)
                    n = units[u][1]
                    V.tensor_tensor(WL[:, u % 2, 0:n], RAW[:, u % 2, 0:n], WH[:, u % 2, 0:n].bitcast(F32),
                                    ALU.subtract).then_inc(lo_done, 1)
                    n_lo[0] += 1

            def add_sum(m, a, b):
                if n_add[0] and m > 1:
                    dve.wait_ge(sem("sq_added"), n_add[0])
                V.tensor_tensor(SUM[:], a if m == 1 else SUM[:], b, ALU.add).then_inc(sem("sq_added"), 1)
                n_add[0] += 1

            def add_square(norm, m, tiles=KT):
                base = SQ_BASE[norm]
                dve.wait_ge(sem("sq_made"), base + m + 1)
                if m >= 1:
                    add_sum(m, SQ[0][:], SQ[m % 2][:])

            def rsqrt(n):
                link(V.tensor_scalar(RSI[:, 0:n], RS[:, 0, 0:n].bitcast(I32), 1, None, ALU.arith_shift_right))
                link(V.tensor_scalar(RS[:, 1, 0:n].bitcast(I32), RSI[:, 0:n], -1.0, 1597463007.0, ALU.mult, ALU.add))
                for _ in range(3):
                    link(V.tensor_tensor(RS[:, 2, 0:n], RS[:, 1, 0:n], RS[:, 1, 0:n], ALU.mult))
                    link(V.scalar_tensor_tensor(out=RS[:, 3, 0:n], in0=RS[:, 2, 0:n], scalar=-0.5, in1=RS[:, 0, 0:n],
                                                op0=ALU.mult, op1=ALU.mult))
                    link(V.scalar_tensor_tensor(out=RS[:, 1, 0:n], in0=RS[:, 3, 0:n], scalar=1.5, in1=RS[:, 1, 0:n],
                                                op0=ALU.add, op1=ALU.mult))

            def norm(n, dim):
                filled(dve, ("stat", n))
                s = ("stat", n)
                V.tensor_scalar(RS[:, 0, 0:QT], tile2(s)[:, 0, 0:QT], 1.0 / dim, EPS, ALU.mult, ALU.add).then_inc(free_of(s), 1)
                was_read(dve, s)
                rsqrt(QT)
                for t in range(QT):
                    V.tensor_scalar(DIAGN[:, t, :], EYE[:], RS[:, 1, t:t + 1], None, ALU.mult).then_inc(sem("diag_ready"), 1)

            def mod_read_chunk(n, ch, t0, tiles, c0=0, give=True):
                l, j = divmod(ch, 6)
                filled(dve, n)
                src = tile2(n)[:, 0, c0:c0 + 2 * tiles].rearrange("p (k s) -> p k s", s=2)
                at = 8 * j + t0
                b = VT1[:, V1["b_mod"] + 48 * l + at:V1["b_mod"] + 48 * l + at + tiles]
                for s in range(2):
                    ins = V.tensor_tensor(MODV[:, l, s, at:at + tiles], src[:, :, s], b, ALU.add)
                if give:
                    ins.then_inc(free_of(n), 1)
                if j in (1, 4) and t0 + tiles == KT:
                    was_read(dve, n)
                    g0 = V1["norm_mix" if j == 1 else "norm_ffn"] + KT * l
                    for s in range(2):
                        ins = V.scalar_tensor_tensor(out=GAIN[:, l, j // 4, s, :], in0=MODV[:, l, s, 8 * j:8 * j + 8], scalar=1.0,
                                                     in1=VT1[:, g0:g0 + KT], op0=ALU.add, op1=ALU.mult)
                    link(ins)

            def background(steps):
                for _ in range(steps):
                    i = n_bg[0]
                    if i == N_HALF * KT:
                        return
                    n_bg[0] += 1
                    j, k = divmod(i, KT)
                    if k == 0 and j >= 2:
                        filled(dve, ("mh", j - 2))
                    dve.wait_ge(bgw_landed[i % BG_SLOTS], 16 * (i // BG_SLOTS + 1))
                    if k:
                        dve.wait_ge(sem("bgw_used"), i)
                    for s in range(2):
                        acc, w, c = BGACC[j % 2][:, s, :], BGW[i % BG_SLOTS][:], SC[:, k, s:s + 1]
                        if k == 0:
                            ins = V.tensor_scalar(acc, w, c, None, ALU.mult)
                        else:
                            ins = V.scalar_tensor_tensor(out=acc, in0=w, scalar=c, in1=acc, op0=ALU.mult, op1=ALU.add)
                    ins.then_inc(sem("bgw_used"), 1)

            def mod_halves(pair):
                for j in range(N_HALF):
                    if half_pair(j) == pair:
                        mod_read_chunk(("mh", j), FIRST_BG + j // 2, 4 * (j % 2), 4)

            def apply(norm_name, l, half):
                was_read(dve, ("rb", norm_name))

                def scale(k):
                    if k >= 3:
                        dve.wait_ge(sem("h_ready"), KT * APPLY[norm_name] + k - 2)
                    for a, b, s in SEGS:
                        ins = V.scalar_tensor_tensor(out=SCALED[k % 3][:, a:b], in0=X[:, k, a:b], scalar=GAIN[:, l, half, s, k:k + 1],
                                                     in1=RSTD[:, a:b], op0=ALU.mult, op1=ALU.mult)
                    ins.then_inc(sem("t_ready"), 1)
                    n_t[0] += 1

                scale(0)
                for k in range(KT):
                    if k + 1 < KT:
                        scale(k + 1)
                    n_part[0] += 1
                    dve.wait_ge(sem("t_ready"), n_t[0] - (k + 1 < KT))
                    dve.wait_ge(sem("part_hi"), n_part[0])
                    for a, b, s in SEGS:
                        ins = V.scalar_tensor_tensor(out=HL[:, k, a:b], in0=SCALED[k % 3][:, a:b],
                                                     scalar=MODV[:, l, s, 24 * half + k:24 * half + k + 1],
                                                     in1=HH[:, k, a:b].bitcast(F32), op0=ALU.add, op1=ALU.subtract)
                    ins.then_inc(sem("h_ready"), 1)

            def residual(n, m, l, which):
                filled(dve, n)
                for bank, a, b, t, s in PSEGS:
                    g = MODV[:, l, s, 8 * which + m:8 * which + m + 1]
                    ins = V.scalar_tensor_tensor(out=X[:, m, t:t + b - a], in0=tile2(n)[:, bank, a:b], scalar=g,
                                                 in1=X[:, m, t:t + b - a], op0=ALU.mult, op1=ALU.add)
                ins.then_inc(free_of(n), 1)

            V.memset(ONES[:], 1.0).then_inc(sem("ones_set"), 1)
            for k in range(KT):
                n = ("x", k)
                filled(dve, n)
                V.tensor_copy(X[:, k, 0:3 * P], tile2(n)[:, 0, 0:3 * P])
                V.tensor_copy(X[:, k, 3 * P:TOK], tile2(n)[:, 1, 0:2 * P]).then_inc(free_of(n), 1)
                if k >= 1:
                    add_square("mix0", k - 1)
            add_square("mix0", KT - 1)
            filled(dve, "vec")
            ps = tile2("vec")
            V.tensor_copy(VT1[:], ps[:, 0, 0:P])
            V.tensor_copy(VT2[:], ps[:, 0, P:P + NV2]).then_inc(free_of("vec"), 1)
            was_read(dve, "vec")
            link(V.tensor_tensor(GQK[:], VT2[:, V2["gq"]:V2["gq"] + 1], VT2[:, V2["gk"]:V2["gk"] + 1], ALU.mult))
            norm("mix0", D)
            filled(dve, "taps")
            V.tensor_copy(WTAP[:].rearrange("p k t -> p (k t)"), tile2("taps")[:, 0, 0:KT * TAPS]).then_inc(free_of("taps"), 1)
            filled(dve, "cache")
            dve.wait_ge(sem("cache_hi"), 1)
            ps = tile2("cache")
            V.tensor_tensor(CKL[:, :, CTX:CTX + PAST], ps[:, 0, 0:KVL].rearrange("p (j t) -> p j t", j=KVT),
                            CKH[:, :, CTX:CTX + PAST].bitcast(F32), ALU.subtract)
            V.tensor_copy(KPRAW[:, CTX:CTX + PAST], ps[:, 0, KVL:KVL + P]).then_inc(free_of("cache"), 1)
            split_units(1)
            for ch in range(2):
                mod_read_chunk("mods", ch, 0, KT, 16 * ch, ch == 1)
            apply("mix0", 0, 0)
            for m in range(QLT):
                if m % 2 == 0:
                    split_units(U[("dq", m)] + 1)
                add_square("cq", m, QLT)
            split_units(U[("dkv", 0)] + 1)
            for m in range(KVT):
                if m == 1:
                    filled(dve, ("stat", "cq"))
                if m == 0:
                    norm("cq", QL)
                add_square("ck", m, KVT)
            split_units(U[("dkv", 2)] + 1)
            was_read(dve, ("rb", "cq"))
            for m in range(QLT):
                g = VT2[:, V2["q_norm"] + m:V2["q_norm"] + m + 1]
                V.scalar_tensor_tensor(out=TMP[m % 2][:], in0=CQRAW[:, m, :], scalar=g, in1=RSTD[:],
                                       op0=ALU.mult, op1=ALU.mult).then_inc(sem("cq_t"), 1)
                dve.wait_ge(sem("cq_t"), m + 1)
                dve.wait_ge(sem("cq_hi"), m + 1)
                V.tensor_tensor(CQL[:, m, :], TMP[m % 2][:], CQH[:, m, :].bitcast(F32), ALU.subtract).then_inc(sem("cq_ready"), 1)
            norm("ck", KVL)
            was_read(dve, ("rb", "ck"))
            for m in range(KVT):
                g = VT2[:, V2["kv_norm"] + m:V2["kv_norm"] + m + 1]
                V.scalar_tensor_tensor(out=TMP[m % 2][:], in0=CKRAW[:, m, :], scalar=g, in1=RSTD[:],
                                       op0=ALU.mult, op1=ALU.mult).then_inc(sem("ck_t"), 1)
                dve.wait_ge(sem("ck_t"), m + 1)
                V.tensor_copy(CKN[:, m, :], TMP[m % 2][:, 0:CTX]).then_inc(sem("ckn_ready"), 1)
                dve.wait_ge(sem("ck_hi"), m + 1)
                V.tensor_tensor(CKL[:, m, 0:CTX], TMP[m % 2][:, 0:CTX], CKH[:, m, 0:CTX].bitcast(F32), ALU.subtract)
                V.tensor_tensor(CKL[:, m, CTX + PAST:KEYS], TMP[m % 2][:, CTX:TOK], CKH[:, m, CTX + PAST:KEYS].bitcast(F32),
                                ALU.subtract).then_inc(sem("ck_ready"), 1)
            filled(dve, "kpstat")
            V.tensor_copy(KPSS[:], tile2("kpstat")[:, 0, 0:NKT]).then_inc(free_of("kpstat"), 1)
            was_read(dve, "kpstat")
            V.tensor_scalar(KPSQ[:], KPRAW[:], VT2[:, V2["gk_pe"]:V2["gk_pe"] + 1], None, ALU.mult).then_inc(sem("kpg_ready"), 1)
            dve.wait_ge(sem("kpg_ready"), 1)
            dve.wait_ge(sem("rope_landed"), 32)
            filled(dve, "kprot")
            V.tensor_tensor(ROPET[:], tile2("kprot")[:, 0, :], SIN[:], ALU.mult).then_inc(free_of("kprot"), 1)
            was_read(dve, "kprot")
            late = KPSQ[:, KEYS - LAT:KEYS]
            link(V.tensor_tensor(late, late, COS[:], ALU.mult))
            V.tensor_tensor(late, late, ROPET[:], ALU.add).then_inc(sem("kp_rotated"), 1)
            dve.wait_ge(sem("kp_rotated"), 1)
            dve.wait_ge(sem("kp_hi"), 1)
            V.tensor_tensor(KPL[:], KPSQ[:], KPH[:].bitcast(F32), ALU.subtract).then_inc(sem("kp_ready"), 1)

            def queries(h):
                split_units(U[("head", min(h + 1, HEADS - 1))])
                n = ("qn", h)
                dve.wait_ge(sem("qn_hi"), h + 1)
                V.scalar_tensor_tensor(out=row2(QNL[:]), in0=tile2(n)[:, :, 0:HALF], scalar=GQK[:, 0:1],
                                       in1=row2(QNH[:]).bitcast(F32), op0=ALU.mult, op1=ALU.subtract).then_inc(free_of(n), 1)
                if h % 2 == 0:
                    n = ("pe", h)
                    dve.wait_ge(sem("pe_sq"), h // 2 + 1)
                    V.tensor_scalar(row2(PEG[:]), tile2(n)[:, :, 0:HALF], VT2[:, V2["gq_pe"]:V2["gq_pe"] + 1], None,
                                    ALU.mult).then_inc(free_of(n), 1)

            def keys(h):
                n = ("kn", h)
                dve.wait_ge(sem("kn_hi"), h + 1)
                k2 = lambda r: r.rearrange("p (b t) -> p b t", b=2)
                V.tensor_tensor(k2(KNL[:]), tile2(n)[:, :, 0:KEYS // 2], k2(KNH[:]).bitcast(F32),
                                ALU.subtract).then_inc(free_of(n), 1)
                if h % 2 == 0:
                    n = ("rot", h)
                    filled(dve, n)
                    V.tensor_tensor(ROPEQ[:], tile2(n)[:, 0, :], SIN[:], ALU.mult).then_inc(free_of(n), 1)
                    was_read(dve, n)
                    was_read(dve, ("pe", h))
                    link(V.tensor_tensor(PEG[:, CTX:TOK], PEG[:, CTX:TOK], COS[:], ALU.mult))
                    V.tensor_tensor(PEG[:, CTX:TOK], PEG[:, CTX:TOK], ROPEQ[:], ALU.add).then_inc(sem("q_rotated"), 1)

            def rotary_low(h):
                if h % 2 == 0:
                    dve.wait_ge(sem("q_rotated"), h // 2 + 1)
                    dve.wait_ge(sem("qp_hi"), h // 2 + 1)
                    V.tensor_tensor(QPL[:], PEG[:], QPH[:].bitcast(F32), ALU.subtract).then_inc(sem("qp_ready"), 1)

            def head_norm(h):
                n = ("hstat", h)
                filled(dve, n)
                V.tensor_copy(HST[:, 0:QT], tile2(n)[:, 0, 0:QT])
                V.tensor_tensor(HST[:, QT:QT + NKT], tile2(n)[:, 0, QT:QT + NKT], KPSS[:], ALU.add).then_inc(free_of(n), 1)
                was_read(dve, n)
                link(V.tensor_scalar(RS[:, 0, 0:QT + NKT], HST[:, 0:QT + NKT], 1.0 / QK, EPS, ALU.mult, ALU.add))
                rsqrt(QT + NKT)
                link(V.tensor_scalar(RQ[h % 2][:], RS[:, 1, 0:QT], QK ** -0.5, None, ALU.mult))
                for t in range(NKT):
                    V.tensor_scalar(DIAGK[t][:], EYE[:], RS[:, 1, QT + t:QT + t + 1], None, ALU.mult).then_inc(sem("diag_ready"), 1)

            def values(h):
                n = ("v", h)
                dve.wait_ge(sem("v_hi"), h + 1)
                v2 = lambda r: r.rearrange("p (b j) v -> p b (j v)", b=2)
                V.tensor_tensor(v2(VL[:]), tile2(n)[:, :, 0:3 * P], v2(VH[:]).bitcast(F32), ALU.subtract).then_inc(free_of(n), 1)

            queries(0)
            keys(0)
            rotary_low(0)
            head_norm(0)
            values(0)
            for h in range(HEADS):
                was_read(dve, ("rk", h))

                def peak(t):
                    n = ("s", h, t)
                    filled(dve, n)
                    if t == 0:
                        o, i0, i1 = PROBC[:], tile2(n)[:, 0, 0:CTX], RK[:, 0:CTX]
                    else:
                        o, i0, i1 = row2(PROB[:, t - 1, :]), tile2(n)[:, :, 0:HALF], row2(RK[:, CTX:KEYS])
                    V.tensor_tensor_reduce(out=o, in0=i0, in1=i1, scale=1.0, scalar=-3.0e38, op0=ALU.mult, op1=ALU.max,
                                           accum_out=MAX8[:, t:t + 1]).then_inc(free_of(n), 1)
                    was_read(dve, n)
                    V.scalar_tensor_tensor(out=NB8[:, t:t + 1], in0=MAX8[:, t:t + 1], scalar=-1.0, in1=RQ[h % 2][:, t:t + 1],
                                           op0=ALU.mult, op1=ALU.mult).then_inc(sem("nb_ready"), 1)

                def normalise(t):
                    dve.wait_ge(sem("exp_done"), QT * h + t + 1)
                    link(V.reciprocal(REC8[:, t:t + 1], SUM8[:, t:t + 1]))
                    p = PROBC[:] if t == 0 else PROB[:, t - 1, :]
                    V.tensor_scalar(p, p, REC8[:, t:t + 1], None, ALU.mult).then_inc(sem("prob_ready"), 1)

                for t in range(QT):
                    peak(t)
                    if t:
                        normalise(t - 1)
                normalise(QT - 1)
                if h + 1 < HEADS:
                    queries(h + 1)
                for t in range(QT):
                    n = ("pt", h, t)
                    dve.wait_ge(sem("pt_hi"), QT * h + t + 1)
                    if t == 0:
                        V.tensor_tensor(PTCL[:], tile2(n)[:, 0, 0:P], PTCH[:].bitcast(F32), ALU.subtract).then_inc(free_of(n), 1)
                    else:
                        g, c0 = (t - 1) // 2, (t - 1) % 2 * P
                        for bank, k0, k1 in ((0, 0, 3), (1, 3, 5)):
                            ins = V.tensor_tensor(PTL[:, g, k0:k1, c0:c0 + P],
                                                  tile2(n)[:, bank, 0:(k1 - k0) * P].rearrange("p (k q) -> p k q", q=P),
                                                  PTH[:, g, k0:k1, c0:c0 + P].bitcast(F32), ALU.subtract)
                        ins.then_inc(free_of(n), 1)
                if h + 1 < HEADS:
                    keys(h + 1)
                    head_norm(h + 1)
                    rotary_low(h + 1)
                if h < N_ROWS:
                    mod_read_chunk(("mb", h), 2 + h // 2, 4 * (h % 2), 4)
                if h + 1 < HEADS:
                    values(h + 1)
            split_units(U[("wo", 0)])
            for k in range(HEADS):
                dve.wait_ge(sem("o_hi"), k + 1)
                V.tensor_tensor(OL[:, k, :], O[:, k, :], OH[:, k, :].bitcast(F32), ALU.subtract).then_inc(sem("o_split"), 1)
            def residuals(name, l, which, norm_name):
                for m in range(KT):
                    if m % 2 == 0:
                        split_units(U[name(m)] + 1)
                    residual(name(m), m, l, which)
                    if norm_name and m:
                        add_square(norm_name, m - 1)
                if norm_name:
                    add_square(norm_name, KT - 1)

            residuals(lambda m: ("wo", m), 0, 2, "ffn0")

            def ffn(l):
                n = f"ffn{l}"
                norm(n, D)
                apply(n, l, 1)
                for kind, a, f0 in ffn_steps():
                    if kind == "pair":
                        split_units(U[("gate", l, a)] + 1)
                        if l == 0:
                            background(BG_STEPS // 2)
                        split_units(U[("up", l, a)] + 1)
                        if l == 0:
                            mod_halves(a // 2)
                        for j in range(2):
                            n = ("up", l, a + j)
                            was_read(dve, ("gate", l, a + j))
                            filled(dve, n)
                            V.tensor_tensor(row2(TMP[j][:]), tile2(n)[:, :, 0:HALF], row2(ACTV[j][:]), ALU.mult).then_inc(free_of(n), 1)
                        for j in range(2):
                            was_read(dve, ("up", l, a + j))
                            dve.wait_ge(sem("hid_hi"), FT * l + a + j + 1)
                            V.tensor_tensor(HIDL[:, (a + j) % HID_SLOTS, :], TMP[j][:], HIDH[:, (a + j) % HID_SLOTS, :].bitcast(F32),
                                            ALU.subtract).then_inc(sem("hid_ready"), 1)
                        if l == 0:
                            background(BG_STEPS - BG_STEPS // 2)
                    else:
                        residuals(lambda m: ("down", l, a, m), l, 5, "mix1" if l == 0 and a == len(DOWN_K) - 1 else None)

            ffn(0)
            mod_halves(FT // 2)
            norm("mix1", D)
            dve.wait_ge(sem("wth_ready"), 1)
            V.tensor_tensor(WTL[:], WTAP[:], WTH[:].bitcast(F32), ALU.subtract).then_inc(sem("taps_split"), 1)
            for i in range(2):
                link(V.memset(GP[i][:], 0.0))
            apply("mix1", 1, 0)

            def gated(i):
                was_read(dve, ("b", i))
                n = ("a", i)
                filled(dve, n)
                for bank, a, b, t, s in PSEGS:
                    to = t + PAD if s == 0 else t + 2 * PAD
                    ins = V.scalar_tensor_tensor(out=GP[i % 2][:, to:to + b - a], in0=tile2(n)[:, bank, a:b],
                                                 scalar=VT2[:, V2["b_pw1"] + i:V2["b_pw1"] + i + 1],
                                                 in1=ACTV[i % 2][:, t:t + b - a], op0=ALU.add, op1=ALU.mult)
                ins.then_inc(free_of(n), 1)
                was_read(dve, n)
                dve.wait_ge(sem("gp_hi"), i + 1)
                V.tensor_tensor(GPL[i % 2][:], GP[i % 2][:], GPH[i % 2][:].bitcast(F32), ALU.subtract).then_inc(sem("gp_lo"), 1)

            def taps(i):
                acc, g = YACC[i % 2], GP[i % 2]
                link(V.tensor_scalar(acc[:], g[:, PE_TAPS:PE_TAPS + RUN], WTAP[:, i, PE_TAPS:PE_TAPS + 1],
                                     VT2[:, V2["b_dw"] + i:V2["b_dw"] + i + 1], ALU.mult, ALU.add))
                for j in range(PE_TAPS + 1, TAPS):
                    link(V.scalar_tensor_tensor(out=acc[:], in0=g[:, j:j + RUN], scalar=WTAP[:, i, j:j + 1],
                                                in1=acc[:], op0=ALU.mult, op1=ALU.add))

            def joined(i):
                n = ("cv", i)
                filled(dve, n)
                for bank, a, b, t in CSEGS:
                    at = a + bank * CHALF
                    ins = V.tensor_tensor(Y[:, i, t:t + b - a], tile2(n)[:, bank, a:b], YACC[i % 2][:, at:at + b - a], ALU.add)
                ins.then_inc(free_of(n), 1)
                was_read(dve, n)
                if i == 1:
                    add_sum(1, Y[:, 0, :], Y[:, 1, :])
                elif i:
                    add_sum(i, None, Y[:, i, :])

            for i in range(KT):
                split_units(U[("glu", i)] + 1)
                gated(i)
                if i:
                    joined(i - 1)
                taps(i)
            joined(KT - 1)
            for s in range(2):
                link(V.tensor_tensor(GB[:, s, :], MODV[:, 1, s, 16:24], VT2[:, V2["b_pw2"]:V2["b_pw2"] + KT], ALU.mult))
            filled(dve, "mu")
            for i in range(KT):
                V.scalar_tensor_tensor(out=row2(Y[:, i, :]), in0=tile2("mu")[:, :, 0:HALF], scalar=-1.0 / D,
                                       in1=row2(Y[:, i, :]), op0=ALU.mult, op1=ALU.add).then_inc(sem("y_centred"), 1)
                if i:
                    add_square("ln", i - 1)
            add_square("ln", KT - 1)
            V.tensor_copy(EPSC[:], tile2("mu")[:, 0, 0:1]).then_inc(free_of("mu"), 1)
            norm("ln", D)
            was_read(dve, ("rb", "ln"))

            def ln_scale(k):
                V.scalar_tensor_tensor(out=SCALED[k % 3][:], in0=Y[:, k, :], scalar=VT2[:, V2["ln_g"] + k:V2["ln_g"] + k + 1],
                                       in1=RSTD[:], op0=ALU.mult, op1=ALU.mult).then_inc(sem("t_ready"), 1)

            ln_scale(0)
            for k in range(KT):
                if k + 1 < KT:
                    if k >= 2:
                        dve.wait_ge(sem("swish"), k - 1)
                    ln_scale(k + 1)
                n_part[0] += 1
                dve.wait_ge(sem("part_hi"), n_part[0])
                V.tensor_tensor(HL[:, k, :], ACTV[k % 2][:], HH[:, k, :].bitcast(F32), ALU.subtract).then_inc(sem("h_ready"), 1)
            n_t[0] += KT
            for k in range(KT):
                for a, b, s in SEGS:
                    ins = V.tensor_scalar(X[:, k, a:b], X[:, k, a:b], GB[:, s, k:k + 1], None, ALU.add)
                link(ins)
            residuals(lambda m: ("pw2", m), 1, 2, "ffn1")
            ffn(1)
            for t in range(QT):
                n = ("y", t)
                filled(dve, n)
                dve.wait_ge(sem("y_half"), t + 1)
                V.tensor_copy(YROW[t][:, 512:1024], tile2(n)[:, 1, :]).then_inc(free_of(n), 1)


_INS = ["x_prompt", "x_sample", "cache_ckv", "cache_kpe", "c", "c_ctx", "w_mod", "b_mod", "norm_mix", "norm_ffn",
        "mla_w_dq", "mla_q_norm", "mla_w_uq", "mla_w_dkv", "mla_kv_norm", "mla_w_ukv", "mla_q_hnorm", "mla_k_hnorm",
        "mla_w_o", "conv_w_pw1", "conv_b_pw1", "conv_w_dw", "conv_b_dw", "conv_ln_g", "conv_ln_b", "conv_w_pw2",
        "conv_b_pw2", "ffn_w_gate", "ffn_w_up", "ffn_w_down"]
_OUTS = [((1, CTX, D), "float32"), ((1, LAT, D), "float32"), ((1, 1, CTX, KVL), "float32"), ((1, 1, CTX, ROPE), "float32")]


def kernel(**inputs):
    import concourse.bacc as bacc
    from concourse.bass_utils import run_bass_kernel_spmd

    nc = bacc.Bacc("TRN2", target_bir_lowering=False, num_devices=1)
    arrays, args = {}, []
    for name in _INS:
        a = np.ascontiguousarray(inputs[name])
        arrays[f"in_{name}"] = a
        args.append(nc.dram_tensor(f"in_{name}", a.shape, mybir.dt.from_np(a.dtype), kind="ExternalInput").ap())
    for i, (shape, dtype) in enumerate(_OUTS):
        args.append(nc.dram_tensor(f"out_{i}", shape, mybir.dt.from_np(np.dtype(dtype)), kind="ExternalOutput").ap())
    program(nc, *args)
    r = run_bass_kernel_spmd(nc, [arrays], core_ids=[0])
    return tuple(r.results[0][f"out_{i}"] for i in range(len(_OUTS)))
```

```python
from contextlib import ExitStack

import numpy as np

import concourse.bass as bass
from concourse import mybir

P = 128
F32 = mybir.dt.float32
F32R = mybir.dt.float32r
I32 = mybir.dt.int32
ALU = mybir.AluOpType
ACT = mybir.ActivationFunctionType

CTX, LAT = 128, 512
TOK = CTX + LAT
PAST = 128
KEYS = CTX + PAST + LAT
D = 1024
KT = D // P
HALF = TOK // 2
HEADS, NOPE, ROPE, VD = 8, 128, 64, 128
QK = NOPE + ROPE
QL, KVL = 512, 256
QLT, KVT = QL // P, KVL // P
FF = 2816
FT = FF // P
TAPS, PAD = 31, 15
GRID_W = 64
THETA = 10000.0
EPS = 1e-6
RUN = CTX + PAD + LAT
GPW = RUN + 2 * PAD + 3
PE_TAPS = 7
POOL_TAPS = 8
CHALF = (RUN + 1) // 2
DIAG_SLOTS = 2 * PE_TAPS
QT = TOK // P
NKT = KEYS // P
DOWN_K = (8, 8, 6)
HID_SLOTS = 10
UNIT = 2048

SEGS = ((0, CTX, 0), (CTX, TOK, 1))
PSEGS = ((0, 0, CTX, 0, 0), (0, CTX, HALF, CTX, 1), (1, 0, HALF, HALF, 1))

CSEGS = ((0, 0, CTX, 0), (0, CTX + PAD, CHALF, CTX), (1, 0, RUN - CHALF, CHALF - PAD))

V1 = {"b_mod": 0, "norm_mix": 96, "norm_ffn": 112}
V2, NV2 = {}, 0
for _n, _w in (("q_norm", 4), ("kv_norm", 2), ("b_pw1", 16), ("b_dw", 8), ("ln_g", 8), ("ln_b", 8),
               ("b_pw2", 8), ("c", 8), ("c_ctx", 8), ("gq", 1), ("gk", 1), ("gq_pe", 1), ("gk_pe", 1)):
    V2[_n] = NV2
    NV2 += _w


def rope_tables():
    t = np.arange(LAT)
    ax = ROPE // 2
    inv = (1.0 / (THETA ** (np.arange(0, ax, 2, dtype=np.float32) / np.float32(ax)))).astype(np.float32)
    ar = (t // GRID_W).astype(np.float32)[:, None] * inv[None, :]
    ac = (t % GRID_W).astype(np.float32)[:, None] * inv[None, :]
    cos = np.concatenate([np.cos(ar), np.cos(ar), np.cos(ac), np.cos(ac)], axis=1).T
    sin = np.concatenate([np.sin(ar), np.sin(ar), np.sin(ac), np.sin(ac)], axis=1).T
    rot = np.zeros((P, P), np.float32)
    q = ROPE // 4
    for b in range(0, P, ROPE // 2):
        for i in range(q):
            rot[b + q + i, b + i] = -1.0
            rot[b + i, b + q + i] = 1.0
    return (np.concatenate([cos, cos]).astype(np.float32), np.concatenate([sin, sin]).astype(np.float32), rot)


MOD_SLOTS = 7
N_ROWS = 6
ROW_SLOTS = 4
FIRST_BG = 5
N_HALF = 2 * (12 - FIRST_BG)
BG_SLOTS = 6

HOLD = 12


def pe_taps(i):
    return PE_TAPS + (DIAG_SLOTS - PE_TAPS if i == KT - 1 else 0)


LAST_DOWN = (1, len(DOWN_K) - 1)
Y_GROUPS = ((0, 4), (4, 7), (7, 8))


def tile_order():
    o = ["vec"] + [("x", k) for k in range(KT)]
    norm = lambda n: [("stat", n), ("rb", n)]
    o += [("stat", "mix0"), ("mrow", 0), ("mrow", 1), ("rb", "mix0"), "taps", "cache", "mods"]
    o += [("dq", m) for m in range(QLT)]
    o += [("dkv", 0), ("stat", "cq"), ("dkv", 1), ("rb", "cq"), ("dkv", 2), ("stat", "ck")]
    even = lambda h, n: [(n, h)] if h % 2 == 0 else []
    o += [("qn", 0), ("rb", "ck"), ("pe", 0), "kpstat", ("kn", 0), "kprot", "ctxout", ("rot", 0), ("hstat", 0), ("v", 0), ("rk", 0)]
    for h in range(HEADS):
        o += [("s", h, t) for t in range(QT)]
        more = h + 1 < HEADS
        if more:
            o += [("qn", h + 1), *even(h + 1, "pe")]
        o += [("pt", h, t) for t in range(QT)]
        if more:
            o += [("kn", h + 1), *even(h + 1, "rot"), ("hstat", h + 1)]
        ma, mb = ([("ma", h)], [("mb", h)]) if h < N_ROWS else ([], [])
        o += ma + [("o", h, g) for g in range(3)] + mb
        if more:
            o += [("v", h + 1), ("rk", h + 1)]
    o += [("wo", m) for m in range(KT)]

    def ffn(l):
        r = norm(f"ffn{l}")
        for step, (kind, a, _) in enumerate(ffn_steps()):
            mh = [("mh", step - 1)] if l == 0 and step else []
            if kind == "pair":
                r += [("gate", l, a), ("gate", l, a + 1), *mh, ("up", l, a), ("up", l, a + 1)]
            else:
                r += [("down", l, a, 0), *mh]
                for m in range(1, KT):
                    r += [("down", l, a, m)] + ([("y", m - 1)] if (l, a) == LAST_DOWN else [])
        return r

    o += ffn(0) + [("stat", "mix1"), ("mh", N_HALF - 1), ("rb", "mix1")]
    for i in range(KT):
        o += [("a", i), ("b", i)] + ([("cv", i - 1)] if i else [])
    o += [("cv", KT - 1)]
    o += ["mu"] + norm("ln") + [("pw2", m) for m in range(KT)] + ffn(1)
    o += [("y", KT - 1)]
    return {n: i for i, n in enumerate(o)}


def ffn_steps():
    steps, f = [], 0
    for c, n in enumerate(DOWN_K):
        end = sum(DOWN_K[:c + 1])
        while f < min(end + 2, FT):
            steps.append(("pair", f, 0))
            f += 2
        steps.append(("down", c, end - n))
    return steps


def program(nc, x_prompt, x_sample, cache_ckv, cache_kpe, c, c_ctx, w_mod, b_mod, norm_mix, norm_ffn,
            w_dq, q_norm, w_uq, w_dkv, kv_norm, w_ukv, q_hn, k_hn, w_o, w_pw1, b_pw1, w_dw, b_dw,
            ln_g, ln_b, w_pw2, b_pw2, w_gate, w_up, w_down, y_prompt, y_sample, new_ckv, new_kpe):
    T = tile_order()
    cos_np, sin_np, rot_np = rope_tables()
    consts = {"eye": np.eye(P, dtype=np.float32), "rot": rot_np, "cos": cos_np, "sin": sin_np}
    const = {n: nc.inline_tensor(a, name=f"const_{n}").ap() for n, a in consts.items()}

    ctx = ExitStack()
    with ctx:
        base = (nc.sbuf_base + 63) // 64 * 64
        top = [base]

        def region(nbytes):
            at = top[0]
            top[0] += nbytes
            return at

        def sb(name, shape, at, dt=F32):
            return nc.alloc_sbuf_tensor_at(name, shape, dt, offset=at)

        R_X, R_HH, R_HL = region(KT * TOK * 4), region(KT * TOK * 4), region(KT * TOK * 4)
        R_HID = region(2 * HID_SLOTS * TOK * 4)
        R_RAW, R_WH, R_WL = region(2 * UNIT * 4), region(2 * UNIT * 4), region(2 * UNIT * 4)
        R_MOD = region(2 * 1024 * 4)
        R_T = [region(TOK * 4) for _ in range(8)]
        R_P, R_PE = region(4 * TOK * 4 + CTX * 4), region(2 * TOK * 4)

        X = sb("X", [P, KT, TOK], R_X)
        HH = sb("HH", [P, KT, TOK], R_HH, F32R)
        HL = sb("HL", [P, KT, TOK], R_HL, F32R)
        HIDH = sb("HIDH", [P, HID_SLOTS, TOK], R_HID, F32R)
        HIDL = sb("HIDL", [P, HID_SLOTS, TOK], R_HID + HID_SLOTS * TOK * 4, F32R)
        RAW = sb("RAW", [P, 2, UNIT], R_RAW)
        WH = sb("WH", [P, 2, UNIT], R_WH, F32R)
        WL = sb("WL", [P, 2, UNIT], R_WL, F32R)
        MODS_A = sb("MODS_A", [P, 5, 2 * D], R_HH)
        MODS_B = sb("MODS_B", [P, 2, 2 * D], R_HID + 32768)
        MODS = [MODS_A[:, i] for i in range(5)] + [MODS_B[:, i] for i in range(2)]
        MROW = sb("MROW", [2, 2 * D], R_MOD)
        MODA = [sb(f"MODA{i}", [P, 512], (R_WH, R_WL)[i // 2] + (i % 2 * UNIT + 1536) * 4) for i in range(ROW_SLOTS)]
        MROWA = sb("MROWA", [2, 512], R_HH + 7 * TOK * 4)
        BGW = [sb(f"BGW{i}", [P, 512], R_MOD + 2048 * i if i < 4 else R_P + 8192 + 2048 * (i - 4)) for i in range(BG_SLOTS)]
        BGACC = [sb(f"BGACC{i}", [P, 2, 512], R_P + 4096 * i) for i in range(2)]
        SQ = [sb(f"SQ{i}", [P, TOK], R_T[i]) for i in range(2)]
        TMP = [sb(f"TMP{i}", [P, TOK], R_T[2 + i]) for i in range(2)]
        ACTV = [sb(f"ACTV{i}", [P, TOK], R_T[4 + i]) for i in range(2)]
        SCALED = [TMP[0], TMP[1], SQ[0]]
        LNSQ = [SQ[0], SQ[1], TMP[0], TMP[1]]
        SUM = sb("SUM", [P, TOK], R_T[6])
        RSTD = sb("RSTD", [P, TOK], R_T[7])
        XROWS = sb("XROWS", [P, QT, D], R_HID)
        CROWS = sb("CROWS", [P, KVL + P], R_P)
        TAPROWS = sb("TAPROWS", [TAPS, D], R_P + 2048)
        CQH = sb("CQH", [P, QLT, TOK], R_HID, F32R)
        CQL = sb("CQL", [P, QLT, TOK], R_HID + 10240, F32R)
        CKH = sb("CKH", [P, KVT, KEYS], R_HID + 20480, F32R)
        CKL = sb("CKL", [P, KVT, KEYS], R_HID + 26624, F32R)
        KPH = sb("KPH", [P, KEYS], R_HID + 32768, F32R)
        KPL = sb("KPL", [P, KEYS], R_HID + 35840, F32R)
        CQRAW = sb("CQRAW", [P, QLT, TOK], R_HID + 38912)
        VH = sb("VH", [P, NKT, VD], R_HID + 38912, F32R)
        VL = sb("VL", [P, NKT, VD], R_HID + 41984, F32R)
        KNH = sb("KNH", [P, KEYS], R_HID + 45056, F32R)
        KNL = sb("KNL", [P, KEYS], R_HID + 48128, F32R)
        CKRAW = sb("CKRAW", [P, KVT, TOK], R_P)
        KPSQ = sb("KPSQ", [P, KEYS], R_P + 5120)
        ROPET = sb("ROPET", [P, LAT], R_P + 8192)
        KPRAW = sb("KPRAW", [P, KEYS], R_PE)
        ROPEQ = sb("ROPEQ", [P, LAT], R_T[6] + KEYS * 4)
        RK = sb("RK", [P, KEYS], R_T[6])
        KSQ = sb("KSQ", [P, KEYS], R_T[0])
        QNH = sb("QNH", [P, TOK], R_T[4], F32R)
        QNL = sb("QNL", [P, TOK], R_T[5], F32R)
        QPH = sb("QPH", [P, TOK], R_PE, F32R)
        QPL = sb("QPL", [P, TOK], R_PE + TOK * 4, F32R)
        PROB = sb("PROB", [P, 4, TOK], R_P)
        PROBC = sb("PROBC", [P, CTX], R_P + 4 * TOK * 4)
        O = sb("O", [P, HEADS, TOK], R_HH)
        PTH = sb("PTH", [P, 2, 5, 256], R_HL, F32R)
        PTL = sb("PTL", [P, 2, 5, 256], R_HL + 10240, F32R)
        OH = sb("OH", [P, HEADS, TOK], R_HID, F32R)
        OL = sb("OL", [P, HEADS, TOK], R_HID + 20480, F32R)
        COS = sb("COS", [P, LAT], R_MOD)
        SIN = sb("SIN", [P, LAT], R_MOD + LAT * 4)
        QSQ, PEG = TMP[1], TMP[0]
        PESQ = sb("PESQ", [P, TOK], R_MOD + 5376)
        CKOUT = sb("CKOUT", [P, KVL + ROPE], R_MOD + 4096)
        PTCH = sb("PTCH", [P, CTX], R_T[0] + 4096, F32R)
        PTCL = sb("PTCL", [P, CTX], R_T[0] + 4608, F32R)
        DIAGN = sb("DIAGN", [P, QT, P], R_T[4])
        DIAGK = [sb(f"DIAGK{t}", [P, P], R_RAW + 1536 * 4 + (t // 4) * UNIT * 4 + (t % 4) * P * 4) for t in range(NKT)]
        ROWS = sb("ROWS", [P, P], R_PE + 3072)
        ROWS2 = sb("ROWS2", [NV2, P], R_PE + 3584)
        GP = [sb(f"GP{i}", [P, GPW], R_HID + 20480 + 2752 * i) for i in range(2)]
        GPH = [sb(f"GPH{i}", [P, GPW], R_HID + 25984 + 2752 * i, F32R) for i in range(2)]
        GPL = [sb(f"GPL{i}", [P, GPW], R_HID + 31488 + 2752 * i, F32R) for i in range(2)]
        YACC = [sb(f"YACC{i}", [P, RUN], R_HID + 36992 + 2688 * i) for i in range(2)]
        WTH = sb("WTH", [P, KT, TAPS], R_HID + 42368, F32R)
        WTL = sb("WTL", [P, KT, TAPS], R_HID + 43392)
        PACC = [sb(f"PACC{i}", [P, RUN], R_HID + 44416 + 2688 * i) for i in range(2)]
        PROD = [sb(f"PROD{i}", [P, RUN], R_T[0] + 2688 * i) for i in range(3)]
        TDH = sb("TDH", [P, DIAG_SLOTS, P], R_P, F32R)
        TDL = sb("TDL", [P, DIAG_SLOTS, P], R_P + DIAG_SLOTS * P * 4, F32R)
        Y = sb("Y", [P, KT, TOK], R_HID)
        YROWS = sb("YROWS", [P, QT, D], R_HH)

        def small(name, shape, dt=F32):
            n = 4
            for s in shape[1:]:
                n *= s
            at = region((n + 31) // 32 * 32)
            return sb(name, shape, at, dt)

        EYE = small("EYE", [P, P])
        ROT = small("ROT", [P, P])
        ONES = small("ONES", [P, P])
        VT1 = small("VT1", [P, P])
        VT2 = small("VT2", [P, NV2])
        WTAP = small("WTAP", [P, KT, TAPS])
        SC = small("SC", [P, KT, 2])
        MODV = small("MODV", [P, 2, 2, 48])
        GAIN = small("GAIN", [P, 2, 2, 2, KT])
        GB = small("GB", [P, 2, KT])
        GQK = small("GQK", [P, 1])
        RS = small("RS", [P, 4, 12])
        RSI = small("RSI", [P, 12], I32)
        KPSS = small("KPSS", [P, NKT])
        RQ = [small(f"RQ{i}", [P, QT]) for i in range(2)]
        LNSS = small("LNSS", [P, QT])
        HST = small("HST", [P, 12])
        MAX8 = small("MAX8", [P, QT])
        NB8 = small("NB8", [P, QT])
        SUM8 = small("SUM8", [P, QT])
        REC8 = small("REC8", [P, QT])
        assert top[0] <= nc.sbuf_usable_end

        PS = ctx.enter_context(nc.psum_tensor("PS", [P, 8, 512], F32))

        sems = {}

        def sem(name):
            if name not in sems:
                sems[name] = ctx.enter_context(nc.semaphore(name))
            return sems[name]

        mm_done = sem("mm_done")
        tile_read = [sem(f"tile_read{i}") for i in range(4)]
        raw_landed = [sem(f"raw_landed{i}") for i in range(2)]
        hi_done, lo_done = sem("hi_done"), sem("lo_done")
        mods_landed = [sem(f"mods_landed{i}") for i in range(MOD_SLOTS)]
        moda_landed = [sem(f"moda_landed{i}") for i in range(ROW_SLOTS)]
        bgw_landed = [sem(f"bgw_landed{i}") for i in range(BG_SLOTS)]

        def tile2(name):
            s = T[name] % 4
            return PS[:, 2 * s:2 * s + 2, :]

        def free_of(name):
            return tile_read[T[name] % 4]

        def filled(eng, name):
            eng.wait_ge(mm_done, T[name] + 1)

        def was_read(eng, name):
            eng.wait_ge(free_of(name), T[name] // 4 + 1)

        def tap_done(eng, n):
            i = min(n // PE_TAPS, KT - 1)
            j = n - PE_TAPS * i
            if j == pe_taps(i) - 1:
                filled(eng, ("cv", i))
            else:
                eng.wait_ge(sem("tap_used"), (PE_TAPS - 1) * i + j + 1)

        def row_used(eng, i):
            j, k = divmod(i, KT)
            if k == KT - 1:
                filled(eng, ("ma", j))
            else:
                eng.wait_ge(sem("rows_used"), (KT - 1) * j + k + 1)

        def row2(ap):
            return ap.rearrange("p (b t) -> p b t", b=2)

        def cols(w, c0, n=256):
            return w[:, c0:c0 + n].rearrange("(k p) n -> p k n", p=P)

        units = []

        def full(kt, w, c0):
            return (kt * 256, [(lambda r, kt=kt: r[:, 0:kt * 256].rearrange("p (k n) -> p k n", k=kt), cols(w, c0))])

        for m in range(0, QLT, 2):
            units.append((("dq", m), *full(KT, w_dq[0], m * P)))
        units.append((("dkv", 0), *full(KT, w_dkv[0], 0)))
        dup = [(lambda r, i=i: r[:, 0:KT * P].rearrange("p (k n) -> p k n", k=KT)[:, :, i * ROPE:(i + 1) * ROPE],
                cols(w_dkv[0], KVL, ROPE)) for i in range(2)]
        units.append((("dkv", 2), KT * P, dup))
        for h in range(HEADS):
            v = lambda r, a, k, n: r[:, a:a + k * n].rearrange("p (k n) -> p k n", k=k)
            d = [(lambda r, v=v: v(r, 0, QLT, NOPE), cols(w_uq[0], h * QK, NOPE)),
                 (lambda r, v=v: v(r, 512, KVT, 256), cols(w_ukv[0], h * 256))]
            if h % 2 == 0:
                d += [(lambda r, v=v, i=i: v(r, 1024, QLT, P)[:, :, i * ROPE:(i + 1) * ROPE],
                       cols(w_uq[0], (h + i) * QK + NOPE, ROPE)) for i in range(2)]
            units.append((("head", h), 1536 if h % 2 == 0 else 1024, d))
        for m in range(0, KT, 2):
            units.append((("wo", m), *full(KT, w_o[0], m * P)))

        def ffn_units(l):
            for kind, a, f0 in ffn_steps():
                if kind == "pair":
                    units.append((("gate", l, a), *full(KT, w_gate[l], a * P)))
                    units.append((("up", l, a), *full(KT, w_up[l], a * P)))
                else:
                    n = DOWN_K[a]
                    for m in range(0, KT, 2):
                        units.append((("down", l, a, m), *full(n, w_down[l][f0 * P:(f0 + n) * P], m * P)))

        ffn_units(0)
        for i in range(KT):
            g = [(lambda r, j=j: r.rearrange("p (k n) -> p k n", k=KT)[:, :, j * P:(j + 1) * P],
                  cols(w_pw1[0], j * D + i * P, P)) for j in range(2)]
            units.append((("glu", i), UNIT, g))
        for m in range(0, KT, 2):
            units.append((("pw2", m), *full(KT, w_pw2[0], m * P)))
        ffn_units(1)
        U = {u[0]: i for i, u in enumerate(units)}
        landed = []
        count = [0, 0]
        for i, u in enumerate(units):
            count[i % 2] += 16 * len(u[2])
            landed.append(count[i % 2])

        LAST = {"dq": lambda n: ("dq", n[1] + 1), "dkv": lambda n: ("dkv", min(n[1] + 1, KVT)),
                "head": lambda n: ("v", n[1]), "wo": lambda n: ("wo", n[1] + 1),
                "gate": lambda n: ("gate", n[1], n[2] + 1), "up": lambda n: ("up", n[1], n[2] + 1),
                "down": lambda n: ("down", n[1], n[2], n[3] + 1), "glu": lambda n: ("b", n[1]),
                "pw2": lambda n: ("pw2", n[1] + 1)}
        unit_last = [LAST[u[0][0]](u[0]) for u in units]

        NORMS, DIAGS, nsum, ndiag = {}, {}, 0, 0
        for n, adds in (("mix0", KT), ("cq", QLT), ("ck", KVT), ("ffn0", KT), ("mix1", KT), ("mu", KT), ("ffn1", KT)):
            nsum += adds - 1
            NORMS[n] = nsum
        for n in ["mix0", "cq", "ck"] + [("rk", h) for h in range(HEADS)] + ["ffn0", "mix1", "ln", "ffn1"]:
            DIAGS[n] = ndiag
            ndiag += NKT if isinstance(n, tuple) else QT
        SQ_BASE, nsq = {}, 0
        for n, tiles in (("mix0", KT), ("cq", QLT), ("ck", KVT), ("ffn0", KT), ("mix1", KT), ("ln", KT), ("ffn1", KT)):
            SQ_BASE[n] = nsq
            nsq += tiles
        APPLY = {"mix0": 0, "ffn0": 1, "mix1": 2, "ln": 3, "ffn1": 4}

        n_vec, n_late = [0], [0]

        block = ctx.enter_context(nc.Block())

        @block.sync
        def _(sp):
            def vec(dst, src):
                sp.dma_start(dst, src).then_inc(sem("vec_landed"), 16)
                n_vec[0] += 16

            def late(dst, src):
                sp.dma_start(dst, src).then_inc(sem("late_landed"), 16)
                n_late[0] += 16

            rows = lambda a: a.rearrange("(r p) -> r p", p=P)
            flat = lambda a: a.rearrange("l n -> (l n)")
            sp.dma_start(EYE[:], const["eye"]).then_inc(sem("eye_landed"), 16)
            vec(ROWS[0:96, :], rows(flat(b_mod)))
            vec(ROWS[96:112, :], rows(flat(norm_mix)))
            vec(ROWS[112:128, :], rows(flat(norm_ffn)))
            for n, a in (("q_norm", q_norm), ("kv_norm", kv_norm), ("b_pw1", b_pw1), ("b_dw", b_dw),
                         ("ln_g", ln_g), ("ln_b", ln_b), ("b_pw2", b_pw2), ("c", c)):
                r = rows(flat(a))
                vec(ROWS2[V2[n]:V2[n] + r.shape[0], :], r)
            vec(ROWS2[V2["c_ctx"]:V2["c_ctx"] + KT, :], rows(c_ctx))
            for n, a in (("gq", q_hn), ("gk", k_hn)):
                vec(ROWS2[V2[n]:V2[n] + 1, :], a[0:1, 0:NOPE])
                for i in range(2):
                    vec(ROWS2[V2[n + "_pe"]:V2[n + "_pe"] + 1, i * ROPE:(i + 1) * ROPE], a[0:1, NOPE:QK])
            late(ROT[:], const["rot"])
            late(TAPROWS[:], w_dw[0])
            late(CROWS[:, 0:KVL], cache_ckv[0, 0])
            for i in range(2):
                late(CROWS[:, KVL + i * ROPE:KVL + (i + 1) * ROPE], cache_kpe[0, 0])

            for i, (name, _, pieces) in enumerate(units):
                if name == ("head", 0):
                    filled(sp, "mods")
                    sp.dma_start(COS[:], const["cos"]).then_inc(sem("rope_landed"), 16)
                    sp.dma_start(SIN[:], const["sin"]).then_inc(sem("rope_landed"), 16)
                if name == ("wo", 0):
                    filled(sp, ("rk", HEADS - 1))
                if i >= 2:
                    sp.wait_ge(lo_done, i - 1)
                for view, src in pieces:
                    sp.dma_start(view(RAW[:, i % 2, :]), src).then_inc(raw_landed[i % 2], 16)
                if name == ("head", 2):
                    was_read(sp, "ctxout")
                    sp.dma_start(new_ckv[0, 0], CKOUT[:, 0:KVL]).then_inc(sem("stored"), 16)
                    sp.dma_start(new_kpe[0, 0], CKOUT[:, KVL:]).then_inc(sem("stored"), 16)
            for a, b in Y_GROUPS:
                was_read(sp, ("y", b - 1))
                ys = slice(a * P, b * P)
                sp.dma_start(y_prompt[0][:, ys], YROWS[:, 0, ys]).then_inc(sem("y_stored"), 16)
                sp.dma_start(y_sample[0].rearrange("(t p) d -> p t d", p=P)[:, :, ys], YROWS[:, 1:QT, ys]).then_inc(sem("y_stored"), 16)
            sp.wait_ge(sem("stored"), 32)
            sp.wait_ge(sem("y_stored"), 32 * len(Y_GROUPS))

        @block.gpsimd
        def _(pool):
            pool.wait_ge(sem("vec_landed"), n_vec[0])
            for k in range(KT):
                if k >= MOD_SLOTS:
                    pool.wait_ge(sem("mods_used"), k - MOD_SLOTS + 1)
                pool.dma_start(MODS[k % MOD_SLOTS], w_mod[0, k * P:(k + 1) * P, 0:2 * D]).then_inc(mods_landed[k % MOD_SLOTS], 16)
            filled(pool, ("dkv", 1))
            for i in range(N_ROWS * KT):
                if i >= ROW_SLOTS:
                    row_used(pool, i - ROW_SLOTS)
                j, k = divmod(i, KT)
                c0 = 2 * D + j * 512
                pool.dma_start(MODA[i % ROW_SLOTS][:], w_mod[0, k * P:(k + 1) * P, c0:c0 + 512]).then_inc(moda_landed[i % ROW_SLOTS], 16)
            filled(pool, ("o", HEADS - 1, 2))
            pool.wait_ge(sem("stored"), 32)
            def half_rows(i):
                j, k = divmod(i, KT)
                l, c0 = divmod(FIRST_BG * D + j * 512, 6 * D)
                pool.dma_start(BGW[i % BG_SLOTS][:], w_mod[l, k * P:(k + 1) * P, c0:c0 + 512]).then_inc(bgw_landed[i % BG_SLOTS], 16)

            for i in range(BG_SLOTS - 1):
                half_rows(i)
            for i in range(N_HALF * KT):
                j, k = divmod(i, KT)
                if i:
                    pool.wait_ge(sem("bgw_used"), i)
                if i + BG_SLOTS - 1 < N_HALF * KT:
                    half_rows(i + BG_SLOTS - 1)
                if k == 0 and j >= 2:
                    filled(pool, ("mh", j - 2))
                pool.wait_ge(sem("bgw_scaled"), i + 1)
                acc, w = BGACC[j % 2][:, 1, :], BGW[i % BG_SLOTS][:]
                if k == 0:
                    ins = nc.gpsimd.tensor_copy(acc, w)
                else:
                    ins = nc.gpsimd.tensor_tensor(acc, acc, w, ALU.add)
                ins.then_inc(sem("bgw_used"), 1)
            pool.wait_ge(sem("taps_split"), 1)

            def tap_diagonals(i, first=0, end=PE_TAPS):
                for j in range(first, end):
                    n = i * PE_TAPS + j
                    if n >= DIAG_SLOTS:
                        tap_done(pool, n - DIAG_SLOTS)
                    nc.gpsimd.tensor_scalar(TDL[:, n % DIAG_SLOTS, :], EYE[:], WTL[:, i, j:j + 1], None,
                                            ALU.mult).then_inc(sem("tap_lo"), 1)

            def joined(i):
                was_read(pool, ("cv", i))
                pool.wait_ge(sem("pool_added"), (POOL_TAPS - 1) * (i + 1))
                for bank, a, b, t in CSEGS:
                    at = a + bank * CHALF
                    y = Y[:, i, t:t + b - a]
                    ins = nc.gpsimd.tensor_tensor(y, y, PACC[i % 2][:, at:at + b - a], ALU.add)
                ins.then_inc(sem("pool_joined"), 1)
                pool.wait_ge(sem("pool_joined"), i + 1)
                if i:
                    if i > 1:
                        pool.wait_ge(sem("sq_added"), NORMS["mu"] - (KT - 1) + i - 1)
                    nc.gpsimd.tensor_tensor(SUM[:], Y[:, 0, :] if i == 1 else SUM[:], Y[:, i, :], ALU.add).then_inc(sem("sq_added"), 1)

            tap_diagonals(0)
            for i in range(KT):
                if i + 1 < KT:
                    tap_diagonals(i + 1)
                else:
                    tap_diagonals(i, PE_TAPS, pe_taps(i))
                for q in range(1, POOL_TAPS):
                    n = (POOL_TAPS - 1) * i + q - 1
                    if n:
                        pool.wait_ge(sem("pool_added"), n)
                    pool.wait_ge(sem("tap_scaled"), POOL_TAPS * i + q + 1)
                    nc.gpsimd.tensor_tensor(PACC[i % 2][:], PACC[i % 2][:], PROD[n % 3][:], ALU.add).then_inc(sem("pool_added"), 1)
                if i:
                    joined(i - 1)
            for k in range(KT // 2):
                pool.wait_ge(sem("sq_made"), SQ_BASE["ln"] + 2 * k + 2)
                a, b = LNSQ[2 * k % 4][:], LNSQ[2 * k % 4 + 1][:]
                nc.gpsimd.tensor_tensor(a, a, b, ALU.add).then_inc(sem("ln_pair"), 1)

        @block.tensor
        def _(pe):
            mm = nc.tensor.matmul
            n_unit = [0]

            def begin(name):
                n = T[name]
                if n >= 4:
                    pe.wait_ge(tile_read[n % 4], n // 4)
                return tile2(name)

            def split3(outs, wh, wl, xs, first, last):
                for o, (xh, xl) in zip(outs, xs):
                    mm(o, wh, xh, start=first, stop=False)
                for o, (xh, xl) in zip(outs, xs):
                    mm(o, wh, xl, start=False, stop=False)
                ins = None
                for o, (xh, xl) in zip(outs, xs):
                    ins = mm(o, wl, xh, start=False, stop=last)
                return ins

            def halves(ps, n=HALF):
                return [ps[:, 0, 0:n], ps[:, 1, 0:n]]

            def unit_begin(name):
                assert U[name] == n_unit[0], name
                pe.wait_ge(lo_done, n_unit[0] + 1)
                s = n_unit[0] % 2
                n_unit[0] += 1
                return WH[:, s, :], WL[:, s, :]

            def product(name, w, a, kt, step, xh, xl, n=HALF, between=None):
                ps = begin(name)
                o = halves(ps, n)
                for k in range(kt):
                    wa = a + k * step
                    ins = split3(o, w[0][:, wa:wa + P], w[1][:, wa:wa + P],
                                 [(xh[:, k, i * n:(i + 1) * n], xl[:, k, i * n:(i + 1) * n]) for i in range(2)],
                                 k == 0, k == kt - 1)
                    if between is not None and k < kt - 1:
                        between(k)
                return ins

            def pair(names, w, xh, xl, wait):
                ps = [begin(n) for n in names]
                for k in range(KT):
                    wait(k)
                    for j in range(2):
                        wa = k * 256 + j * P
                        ins = split3(halves(ps[j]), w[0][:, wa:wa + P], w[1][:, wa:wa + P],
                                     [(xh[:, k, i * HALF:(i + 1) * HALF], xl[:, k, i * HALF:(i + 1) * HALF]) for i in range(2)],
                                     k == 0, k == KT - 1)
                        if k == KT - 1:
                            ins.then_inc(mm_done, 1)

            def half_begin(j):
                pe.wait_ge(sem("bgw_used"), KT * (j + 1))
                return begin(("mh", j))

            def half_sum(ps, j, c):
                if c < 4:
                    for s in range(2):
                        ins = mm(ps[:, 0, 2 * c + s:2 * c + s + 1], BGACC[j % 2][:, s, c * P:(c + 1) * P], ONES[:, 0:1],
                                 start=True, stop=True)
                    if c == 3:
                        ins.then_inc(mm_done, 1)

            def hold_clock(ps, steps):
                for _ in range(steps):
                    mm(ps[:, 1, 384:512], EYE[:], ONES[:], start=True, stop=True)

            def stat(n, before=0, after=0):
                ps = begin(("stat", n))
                hold_clock(ps, before)
                pe.wait_ge(sem("sq_added"), NORMS[n])
                for t in range(QT):
                    ins = mm(ps[:, 0, t:t + 1], SUM[:, t * P:(t + 1) * P], ONES[:, 0:1], start=True, stop=True)
                ins.then_inc(mm_done, 1)
                hold_clock(ps, after)
                return ps

            def spread(name, diags, first):
                ps = begin(name)
                for t, d in enumerate(diags):
                    pe.wait_ge(sem("diag_ready"), first + t + 1)
                    ins = mm(ps[:, t // 3, (t % 3) * P:(t % 3 + 1) * P], ONES[:], d, start=True, stop=True)
                ins.then_inc(mm_done, 1)

            diagn = [DIAGN[:, t, :] for t in range(QT)]

            tr = nc.tensor.transpose
            pe.wait_ge(sem("eye_landed"), 16)
            pe.wait_ge(sem("vec_landed"), n_vec[0])
            pe.wait_ge(sem("ones_set"), 1)
            ps = begin("vec")
            tr(ps[:, 0, 0:P], ROWS[:], EYE[:])
            tr(ps[:, 0, P:P + NV2], ROWS2[:], EYE[0:NV2, 0:NV2]).then_inc(mm_done, 1)
            pe.wait_ge(sem("x_landed"), 32)
            for k in range(KT):
                ps = begin(("x", k))
                for t in range(QT):
                    ins = tr(ps[:, t // 3, (t % 3) * P:(t % 3 + 1) * P], XROWS[:, t, k * P:(k + 1) * P], EYE[:])
                ins.then_inc(mm_done, 1)
            pe.wait_ge(sem("sc_ready"), 2)
            rows = [begin(("mrow", i)) for i in range(2)]
            for k in range(KT):
                if k == KT // 2:
                    stat("mix0")
                pe.wait_ge(mods_landed[k % MOD_SLOTS], 16 * (k // MOD_SLOTS + 1))
                for i in range(4):
                    ins = mm(rows[i // 2][0:2, i % 2, :], SC[:, k, :], MODS[k % MOD_SLOTS][:, i * 512:(i + 1) * 512],
                             start=(k == 0), stop=(k == KT - 1))
                    if k == KT - 1 and i % 2:
                        ins.then_inc(mm_done, 1)
                if k < KT - 1:
                    ins.then_inc(sem("mods_used"), 1)
            spread(("rb", "mix0"), diagn, DIAGS["mix0"])
            pe.wait_ge(sem("late_landed"), n_late[0])
            ps = begin("taps")
            for k in range(KT):
                ins = tr(ps[:, 0, k * TAPS:(k + 1) * TAPS], TAPROWS[:, k * P:(k + 1) * P], EYE[0:TAPS, 0:TAPS])
            ins.then_inc(mm_done, 1)
            ps = begin("cache")
            for j in range(KVT + 1):
                ins = tr(ps[:, 0, j * P:(j + 1) * P], CROWS[:, j * P:(j + 1) * P], EYE[:])
            ins.then_inc(mm_done, 1)
            ps = begin("mods")
            for i in range(2 * KT):
                if i % KT == 0:
                    was_read(pe, ("mrow", i // KT))
                ins = tr(ps[:, 0, 2 * i:2 * i + 2], MROW[:, i * P:(i + 1) * P], EYE[0:2, 0:2])
            ins.then_inc(mm_done, 1)

            h_wait = lambda n: (lambda k: pe.wait_ge(sem("h_ready"), KT * n + k + 1))
            for m in range(0, QLT, 2):
                w = unit_begin(("dq", m))
                if m == 0:
                    pair([("dq", 0), ("dq", 1)], w, HH, HL, h_wait(APPLY["mix0"]))
                    continue
                for j in range(2):
                    product(("dq", m + j), w, j * P, KT, 256, HH, HL).then_inc(mm_done, 1)
            w = unit_begin(("dkv", 0))
            product(("dkv", 0), w, 0, KT, 256, HH, HL).then_inc(mm_done, 1)
            stat("cq")
            product(("dkv", 1), w, P, KT, 256, HH, HL).then_inc(mm_done, 1)
            spread(("rb", "cq"), diagn, DIAGS["cq"])
            w = unit_begin(("dkv", 2))
            product(("dkv", 2), w, 0, KT, P, HH, HL).then_inc(mm_done, 1)
            stat("ck")

            def key_squares():
                ps = begin("kpstat")
                pe.wait_ge(sem("kpsq_ready"), 1)
                for t in range(NKT):
                    ins = mm(ps[:, 0, t:t + 1], KPSQ[0:ROPE, t * P:(t + 1) * P], ONES[0:ROPE, 0:1], start=True, stop=True)
                ins.then_inc(mm_done, 1)

            def rotate_keys():
                ps = begin("kprot")
                pe.wait_ge(sem("kpg_ready"), 1)
                mm(ps[:, 0, :], ROT[:], KPSQ[:, KEYS - LAT:KEYS], start=True, stop=True).then_inc(mm_done, 1)

            def cache_rows():
                ps = begin("ctxout")
                for j in range(KVT):
                    tr(ps[:, 0, j * P:(j + 1) * P], CKRAW[:, j, 0:CTX], EYE[:])
                tr(ps[:, 0, KVL:KVL + ROPE], KPRAW[0:ROPE, 0:CTX], EYE[0:ROPE, 0:ROPE]).then_inc(mm_done, 1)

            def queries(h):
                w = unit_begin(("head", h))
                product(("qn", h), w, 0, QLT, P, CQH, CQL).then_inc(mm_done, 1)
                if h == 0:
                    spread(("rb", "ck"), diagn, DIAGS["ck"])
                if h % 2 == 0:
                    product(("pe", h), w, 1024, QLT, P, CQH, CQL).then_inc(mm_done, 1)

            def keys(h):
                s = U[("head", h)] % 2
                product(("kn", h), (WH[:, s, :], WL[:, s, :]), 512, KVT, 256, CKH, CKL, n=KEYS // 2).then_inc(mm_done, 1)

            def rotate_queries(h):
                if h % 2 == 0:
                    ps = begin(("rot", h))
                    was_read(pe, ("pe", h))
                    mm(ps[:, 0, :], ROT[:], PEG[:, CTX:TOK], start=True, stop=True).then_inc(mm_done, 1)

            def head_stat(h, half=None):
                lo, hi = (0, ROPE) if h % 2 == 0 else (ROPE, P)
                ps = begin(("hstat", h))
                pe.wait_ge(sem("qn_hi"), h + 1)
                pe.wait_ge(sem("pe_sq"), h // 2 + 1)
                if half is not None:
                    rows = begin(("ma", half))
                for k in range(KT):
                    if half is not None and k < KT - 1:
                        modulate(rows, half, k)
                    for t in ((0,), (1,), (2,), (3, 4), (5, 6), (7, 8), (9, 10), ())[k]:
                        o = ps[:, 0, t:t + 1]
                        if t < QT:
                            mm(o, QSQ[:, t * P:(t + 1) * P], ONES[:, 0:1], start=True, stop=False)
                            mm(o, PESQ[lo:hi, t * P:(t + 1) * P], ONES[lo:hi, 0:1], start=False, stop=True)
                        else:
                            if t == QT:
                                pe.wait_ge(sem("kn_hi"), h + 1)
                            ins = mm(o, KSQ[:, (t - QT) * P:(t - QT + 1) * P], ONES[:, 0:1], start=True, stop=True)
                ins.then_inc(mm_done, 1)
                if half is not None:
                    modulate(rows, half, KT - 1)

            def modulate(ps, j, k):
                i = KT * j + k
                pe.wait_ge(moda_landed[i % ROW_SLOTS], 16 * (i // ROW_SLOTS + 1))
                ins = mm(ps[0:2, 0, :], SC[:, k, :], MODA[i % ROW_SLOTS][:], start=(k == 0), stop=(k == KT - 1))
                ins.then_inc(sem("rows_used") if k < KT - 1 else mm_done, 1)

            def turn_rows(j):
                ps = begin(("mb", j))
                was_read(pe, ("ma", j))
                for i in range(4):
                    ins = tr(ps[:, 0, 2 * i:2 * i + 2], MROWA[:, i * P:(i + 1) * P], EYE[0:2, 0:2])
                ins.then_inc(mm_done, 1)

            def key_spread(h):
                spread(("rk", h), [d[:] for d in DIAGK], DIAGS[("rk", h)])

            def values(h):
                s = U[("head", h)] % 2
                ps = begin(("v", h))
                for t in range(NKT):
                    o = ps[:, t // 3, (t % 3) * P:(t % 3 + 1) * P]
                    for k in range(KVT):
                        wa = 512 + k * 256 + P
                        ks = slice(t * P, (t + 1) * P)
                        mm(o, CKH[:, k, ks], WH[:, s, wa:wa + P], start=(k == 0), stop=False)
                        mm(o, CKH[:, k, ks], WL[:, s, wa:wa + P], start=False, stop=False)
                        ins = mm(o, CKL[:, k, ks], WH[:, s, wa:wa + P], start=False, stop=(k == KVT - 1))
                ins.then_inc(mm_done, 1)

            def scores(h, t):
                ps = begin(("s", h, t))
                lo, hi = (0, ROPE) if h % 2 == 0 else (ROPE, P)
                q = slice(t * P, (t + 1) * P)
                if t == 0:
                    outs, keys = [ps[:, 0, 0:CTX]], [slice(0, CTX)]
                else:
                    outs, keys = halves(ps), [slice(CTX, CTX + 320), slice(CTX + 320, KEYS)]
                split3(outs, QNH[:, q], QNL[:, q], [(KNH[:, k], KNL[:, k]) for k in keys], True, False)
                ins = split3(outs, QPH[lo:hi, q], QPL[lo:hi, q], [(KPH[lo:hi, k], KPL[lo:hi, k]) for k in keys], False, True)
                ins.then_inc(mm_done, 1)

            def turn(h, t):
                ps = begin(("pt", h, t))
                pe.wait_ge(sem("prob_ready"), QT * h + t + 1)
                if t == 0:
                    tr(ps[:, 0, 0:P], PROBC[:], EYE[:]).then_inc(mm_done, 1)
                    return
                for k in range(5):
                    ins = tr(ps[:, k // 3, (k % 3) * P:(k % 3 + 1) * P], PROB[:, t - 1, k * P:(k + 1) * P], EYE[:])
                ins.then_inc(mm_done, 1)

            def weighted(h, g):
                ps = begin(("o", h, g))
                if g == 0:
                    was_read(pe, ("pt", h, 0))
                    split3([ps[:, 0, 0:P]], VH[:, 0, :], VL[:, 0, :], [(PTCH[:], PTCL[:])], True, True).then_inc(mm_done, 1)
                    return
                was_read(pe, ("pt", h, 2 * g - 1))
                was_read(pe, ("pt", h, 2 * g))
                for k in range(5):
                    ins = split3([ps[:, 0, 0:256]], VH[:, k + 1, :], VL[:, k + 1, :],
                                 [(PTH[:, g - 1, k, :], PTL[:, g - 1, k, :])], k == 0, k == 4)
                ins.then_inc(mm_done, 1)

            def head_ready(h):
                was_read(pe, ("qn", h))
                was_read(pe, ("kn", h))
                pe.wait_ge(sem("qp_ready"), h // 2 + 1)

            pe.wait_ge(sem("cq_ready"), QLT)
            queries(0)
            key_squares()
            pe.wait_ge(sem("ck_ready"), KVT)
            keys(0)
            rotate_keys()
            cache_rows()
            rotate_queries(0)
            head_stat(0)
            values(0)
            key_spread(0)
            for h in range(HEADS):
                head_ready(h)
                if h == 0:
                    pe.wait_ge(sem("kp_ready"), 1)
                for t in range(QT):
                    scores(h, t)
                more = h + 1 < HEADS
                if more:
                    queries(h + 1)
                for t in range(QT):
                    turn(h, t)
                if more:
                    keys(h + 1)
                    rotate_queries(h + 1)
                    head_stat(h + 1, h if h < N_ROWS else None)
                was_read(pe, ("v", h))
                for g in range(3):
                    weighted(h, g)
                if h < N_ROWS:
                    turn_rows(h)
                if more:
                    values(h + 1)
                    key_spread(h + 1)

            for m in range(0, KT, 2):
                w = unit_begin(("wo", m))
                if m == 0:
                    pair([("wo", 0), ("wo", 1)], w, OH, OL, lambda k: pe.wait_ge(sem("o_split"), k + 1))
                    continue
                for j in range(2):
                    product(("wo", m + j), w, j * P, KT, 256, OH, OL).then_inc(mm_done, 1)

            def ffn(l):
                n = f"ffn{l}"
                ps = stat(n, HOLD, HOLD)
                spread(("rb", n), diagn, DIAGS[n])
                hold_clock(ps, HOLD + HOLD // 2)
                for step, (kind, a, f0) in enumerate(ffn_steps()):
                    part = None
                    if kind == "pair":
                        for g in ("gate", "up"):
                            w = unit_begin((g, l, a))
                            if g == "gate" and a == 0:
                                pair([(g, l, 0), (g, l, 1)], w, HH, HL, h_wait(APPLY[f"ffn{l}"]))
                                continue
                            for j in range(2):
                                if l == 0 and step and g == "up" and j == 0:
                                    pm = half_begin(step - 1)
                                    part = lambda k: half_sum(pm, step - 1, k)
                                product((g, l, a + j), w, j * P, KT, 256, HH, HL, between=part if g == "up" and j == 0 else None).then_inc(mm_done, 1)
                    else:
                        pe.wait_ge(sem("hid_ready"), FT * l + f0 + DOWN_K[a])
                        for m in range(0, KT, 2):
                            w = unit_begin(("down", l, a, m))
                            for j in range(2):
                                summing = l == 0 and m + j == 1
                                if summing:
                                    pm = half_begin(step - 1)
                                ps = begin(("down", l, a, m + j))
                                for k in range(DOWN_K[a]):
                                    hs = (f0 + k) % HID_SLOTS
                                    wa = k * 256 + j * P
                                    ins = split3(halves(ps), w[0][:, wa:wa + P], w[1][:, wa:wa + P],
                                                 [(HIDH[:, hs, i * HALF:(i + 1) * HALF], HIDL[:, hs, i * HALF:(i + 1) * HALF])
                                                  for i in range(2)], k == 0, k == DOWN_K[a] - 1)
                                    if summing and k < DOWN_K[a] - 1:
                                        half_sum(pm, step - 1, k)
                                ins.then_inc(mm_done, 1)
                                if (l, a) == LAST_DOWN and m + j:
                                    output_rows(m + j - 1)

            def output_rows(k):
                ps = begin(("y", k))
                was_read(pe, ("down", *LAST_DOWN, k))
                for t in range(QT):
                    ins = tr(ps[:, t // 3, (t % 3) * P:(t % 3 + 1) * P], X[:, k, t * P:(t + 1) * P], EYE[:])
                ins.then_inc(mm_done, 1)

            ffn(0)
            ps = stat("mix1", HOLD)
            last_half = half_begin(N_HALF - 1)
            for k in range(4):
                half_sum(last_half, N_HALF - 1, k)
            hold_clock(ps, HOLD // 2)
            spread(("rb", "mix1"), diagn, DIAGS["mix1"])
            hold_clock(ps, HOLD + HOLD // 2)
            def conv(i):
                ps = begin(("cv", i))
                pe.wait_ge(sem("gp_lo"), i + 1)
                for j in range(pe_taps(i)):
                    n = i * PE_TAPS + j
                    pe.wait_ge(sem("tap_hi"), n + 1)
                    pe.wait_ge(sem("tap_lo"), n + 1)
                    ins = split3(halves(ps, CHALF), TDH[:, n % DIAG_SLOTS, :], TDL[:, n % DIAG_SLOTS, :],
                                 [(GPH[i % 2][:, j + b * CHALF:j + (b + 1) * CHALF], GPL[i % 2][:, j + b * CHALF:j + (b + 1) * CHALF])
                                  for b in range(2)], j == 0, j == pe_taps(i) - 1)
                    if j < pe_taps(i) - 1:
                        ins.then_inc(sem("tap_used"), 1)
                ins.then_inc(mm_done, 1)

            for i in range(KT):
                w = unit_begin(("glu", i))
                if i == 0:
                    pair([("a", 0), ("b", 0)], w, HH, HL, h_wait(APPLY["mix1"]))
                    continue
                for j, n in enumerate(("a", "b")):
                    product((n, i), w, j * P, KT, 256, HH, HL).then_inc(mm_done, 1)
                if i:
                    conv(i - 1)
            conv(KT - 1)
            ps = begin("mu")
            hold_clock(ps, HOLD)
            pe.wait_ge(sem("sq_added"), NORMS["mu"])
            for i in range(2):
                ins = mm(ps[:, i, 0:HALF], ONES[:], SUM[:, i * HALF:(i + 1) * HALF], start=True, stop=True)
            ins.then_inc(mm_done, 1)
            ps = begin(("stat", "ln"))
            hold_clock(ps, HOLD)
            for k in range(KT // 2):
                hold_clock(ps, HOLD // 4)
                pe.wait_ge(sem("ln_pair"), k + 1)
                for t in range(QT):
                    c = KT // 2 * t + k
                    ins = mm(ps[:, 0, c:c + 1], LNSQ[2 * k % 4][:, t * P:(t + 1) * P], ONES[:, 0:1], start=True, stop=True)
                ins.then_inc(sem("ln_summed") if k < KT // 2 - 1 else mm_done, 1)
            hold_clock(ps, HOLD)
            spread(("rb", "ln"), diagn, DIAGS["ln"])
            hold_clock(ps, HOLD)
            for m in range(0, KT, 2):
                w = unit_begin(("pw2", m))
                if m == 0:
                    pair([("pw2", 0), ("pw2", 1)], w, HH, HL, h_wait(APPLY["ln"]))
                    continue
                for j in range(2):
                    product(("pw2", m + j), w, j * P, KT, 256, HH, HL).then_inc(mm_done, 1)
            ffn(1)
            output_rows(KT - 1)

        @block.scalar
        def _(act):
            A = nc.scalar.activation
            n_hi = [0]
            n_bg = [0]

            def round_units(upto):
                while n_hi[0] <= min(upto, len(units) - 1):
                    u = n_hi[0]
                    act.wait_ge(raw_landed[u % 2], landed[u])
                    if u >= 2:
                        filled(act, unit_last[u - 2])
                    n = units[u][1]
                    A(WH[:, u % 2, 0:n], RAW[:, u % 2, 0:n], ACT.Copy).then_inc(hi_done, 1)
                    n_hi[0] += 1

            def square(norm, m, src, tiles=KT):
                before = NORMS[norm] - (tiles - 1)
                need = before + (max(m - 2, 1) if m >= 2 else 0)
                if need:
                    act.wait_ge(sem("sq_added"), need)
                dst = SQ[m % 2][:] if len(src.shape) == 2 else row2(SQ[m % 2][:])
                A(dst, src, ACT.Square).then_inc(sem("sq_made"), 1)

            def spread_copy(name, dst, n):
                filled(act, name)
                ps = tile2(name)
                A(dst[:, 0:3 * P], ps[:, 0, 0:3 * P], ACT.Copy)
                A(dst[:, 3 * P:n * P], ps[:, 1, 0:(n - 3) * P], ACT.Copy).then_inc(free_of(name), 1)

            def apply(norm, l, half):
                for k in range(KT):
                    act.wait_ge(sem("t_ready"), KT * APPLY[norm] + k + 1)
                    for a, b, s in SEGS:
                        ins = A(HH[:, k, a:b], SCALED[k % 3][:, a:b], ACT.Identity,
                                bias=MODV[:, l, s, 24 * half + k:24 * half + k + 1])
                    ins.then_inc(sem("part_hi"), 1)

            act.dma_start(XROWS[:, 0, :], x_prompt[0]).then_inc(sem("x_landed"), 16)
            act.dma_start(XROWS[:, 1:QT, :], x_sample[0].rearrange("(t p) d -> p t d", p=P)).then_inc(sem("x_landed"), 16)
            was_read(act, "vec")
            A(SC[:, :, 0], VT2[:, V2["c_ctx"]:V2["c_ctx"] + KT], ACT.Silu).then_inc(sem("sc_ready"), 1)
            A(SC[:, :, 1], VT2[:, V2["c"]:V2["c"] + KT], ACT.Silu).then_inc(sem("sc_ready"), 1)
            for k in range(KT):
                was_read(act, ("x", k))
                square("mix0", k, X[:, k, :])
            round_units(1)
            for i in range(2):
                filled(act, ("mrow", i))
                A(MROW[:, i * D:(i + 1) * D].rearrange("p (b n) -> p b n", b=2), tile2(("mrow", i))[0:2, :, :],
                  ACT.Copy).then_inc(free_of(("mrow", i)), 1)
            spread_copy(("rb", "mix0"), RSTD, QT)
            filled(act, "cache")
            ps = tile2("cache")
            A(CKH[:, :, CTX:CTX + PAST], ps[:, 0, 0:KVL].rearrange("p (j t) -> p j t", j=KVT), ACT.Copy).then_inc(sem("cache_hi"), 1)
            apply("mix0", 0, 0)
            for m in range(QLT):
                if m % 2 == 0:
                    round_units(U[("dq", m)] + 1)
                filled(act, ("dq", m))
                square("cq", m, tile2(("dq", m))[:, :, 0:HALF], QLT)
                A(row2(CQRAW[:, m, :]), tile2(("dq", m))[:, :, 0:HALF], ACT.Copy).then_inc(free_of(("dq", m)), 1)
            round_units(U[("dkv", 0)] + 1)
            for m in range(KVT):
                filled(act, ("dkv", m))
                square("ck", m, tile2(("dkv", m))[:, :, 0:HALF], KVT)
                A(row2(CKRAW[:, m, :]), tile2(("dkv", m))[:, :, 0:HALF], ACT.Copy).then_inc(free_of(("dkv", m)), 1)
            spread_copy(("rb", "cq"), RSTD, QT)
            round_units(U[("dkv", 2)] + 1)
            for m in range(QLT):
                act.wait_ge(sem("cq_t"), m + 1)
                A(CQH[:, m, :], TMP[m % 2][:], ACT.Copy).then_inc(sem("cq_hi"), 1)
            n = ("dkv", KVT)
            filled(act, n)
            for bank, a, b, t, s in PSEGS:
                to = t if s == 0 else t + PAST
                ins = A(KPRAW[:, to:to + b - a], tile2(n)[:, bank, a:b], ACT.Copy)
            ins.then_inc(free_of(n), 1)
            was_read(act, n)
            was_read(act, "cache")
            A(KPSQ[:], KPRAW[:], ACT.Square).then_inc(sem("kpsq_ready"), 1)

            def queries(h):
                round_units(U[("head", min(h + 1, HEADS - 1))])
                n = ("qn", h)
                filled(act, n)
                if h == 0:
                    filled(act, ("rb", "ck"))
                A(row2(QNH[:]), tile2(n)[:, :, 0:HALF], ACT.Copy, scale=GQK[:, 0:1])
                A(row2(QSQ[:]), tile2(n)[:, :, 0:HALF], ACT.Square).then_inc(sem("qn_hi"), 1)
                if h % 2 == 0:
                    n = ("pe", h)
                    filled(act, n)
                    A(row2(PESQ[:]), tile2(n)[:, :, 0:HALF], ACT.Square).then_inc(sem("pe_sq"), 1)

            def keys(h):
                n = ("kn", h)
                filled(act, n)
                k2 = lambda r: r.rearrange("p (b t) -> p b t", b=2)
                A(k2(KSQ[:]), tile2(n)[:, :, 0:KEYS // 2], ACT.Square)
                A(k2(KNH[:]), tile2(n)[:, :, 0:KEYS // 2], ACT.Copy).then_inc(sem("kn_hi"), 1)
                if h % 2 == 0:
                    act.wait_ge(sem("q_rotated"), h // 2 + 1)
                    A(QPH[:], PEG[:], ACT.Copy).then_inc(sem("qp_hi"), 1)

            def values(h):
                n = ("v", h)
                filled(act, n)
                A(VH[:].rearrange("p (b j) v -> p b (j v)", b=2), tile2(n)[:, :, 0:3 * P], ACT.Copy).then_inc(sem("v_hi"), 1)

            def round_output(k):
                was_read(act, ("o", k, 2))
                A(OH[:, k, :], O[:, k, :], ACT.Copy).then_inc(sem("o_hi"), 1)

            queries(0)
            spread_copy(("rb", "ck"), RSTD, QT)
            for m in range(KVT):
                act.wait_ge(sem("ck_t"), m + 1)
                A(CKH[:, m, 0:CTX], CKRAW[:, m, 0:CTX], ACT.Copy)
                A(CKH[:, m, CTX + PAST:KEYS], CKRAW[:, m, CTX:TOK], ACT.Copy).then_inc(sem("ck_hi"), 1)
            act.wait_ge(sem("kp_rotated"), 1)
            A(KPH[:], KPSQ[:], ACT.Copy).then_inc(sem("kp_hi"), 1)
            keys(0)
            filled(act, "ctxout")
            A(CKOUT[:], tile2("ctxout")[:, 0, 0:KVL + ROPE], ACT.Copy).then_inc(free_of("ctxout"), 1)
            values(0)
            spread_copy(("rk", 0), RK, NKT)
            for h in range(HEADS):
                for t in range(QT):
                    p = PROBC[:] if t == 0 else PROB[:, t - 1, :]
                    act.wait_ge(sem("nb_ready"), QT * h + t + 1)
                    A(p, p, ACT.Exp, bias=NB8[:, t:t + 1], scale=RQ[h % 2][:, t:t + 1],
                      accum_out=SUM8[:, t:t + 1]).then_inc(sem("exp_done"), 1)
                if h + 1 < HEADS:
                    queries(h + 1)
                else:
                    round_units(U[("wo", 0)])
                for t in range(QT):
                    n = ("pt", h, t)
                    filled(act, n)
                    if t == 0:
                        A(PTCH[:], tile2(n)[:, 0, 0:P], ACT.Copy).then_inc(sem("pt_hi"), 1)
                    else:
                        g, c0 = (t - 1) // 2, (t - 1) % 2 * P
                        for bank, k0, k1 in ((0, 0, 3), (1, 3, 5)):
                            ins = A(PTH[:, g, k0:k1, c0:c0 + P],
                                    tile2(n)[:, bank, 0:(k1 - k0) * P].rearrange("p (k q) -> p k q", q=P), ACT.Copy)
                        ins.then_inc(sem("pt_hi"), 1)
                if h + 1 < HEADS:
                    keys(h + 1)
                else:
                    for k in range(HEADS - 1):
                        round_output(k)
                if h < N_ROWS:
                    filled(act, ("ma", h))
                    A(MROWA[:], tile2(("ma", h))[0:2, 0, :], ACT.Copy).then_inc(free_of(("ma", h)), 1)
                for g in range(3):
                    n = ("o", h, g)
                    filled(act, n)
                    a, b = ((0, CTX), (CTX, CTX + 256), (CTX + 256, TOK))[g]
                    A(O[:, h, a:b], tile2(n)[:, 0, 0:b - a], ACT.Copy).then_inc(free_of(n), 1)
                if h + 1 < HEADS:
                    values(h + 1)
                    spread_copy(("rk", h + 1), RK, NKT)
            was_read(act, ("o", HEADS - 1, 2))
            round_output(HEADS - 1)

            for m in range(KT):
                if m % 2 == 0:
                    round_units(U[("wo", m)] + 1)
                was_read(act, ("wo", m))
                square("ffn0", m, X[:, m, :])

            def half_scale(l, steps):
                for i in range(n_bg[0], n_bg[0] + steps * (l == 0)):
                    act.wait_ge(sem("bgw_first"), i + 1)
                    w = BGW[i % BG_SLOTS][:]
                    A(w, w, ACT.Copy, scale=SC[:, i % KT, 1:2]).then_inc(sem("bgw_scaled"), 1)
                n_bg[0] += steps * (l == 0)

            def ffn(l):
                n = f"ffn{l}"
                spread_copy(("rb", n), RSTD, QT)
                apply(n, l, 1)
                for kind, a, f0 in ffn_steps():
                    if kind == "pair":
                        round_units(U[("gate", l, a)] + 1)
                        half_scale(l, 2)
                        for j in range(2):
                            n = ("gate", l, a + j)
                            filled(act, n)
                            if a >= 2:
                                was_read(act, ("up", l, a + j - 2))
                            A(row2(ACTV[j][:]), tile2(n)[:, :, 0:HALF], ACT.Silu).then_inc(free_of(n), 1)
                        round_units(U[("up", l, a)] + 1)
                        half_scale(l, 2)
                        for j in range(2):
                            was_read(act, ("up", l, a + j))
                            A(HIDH[:, (a + j) % HID_SLOTS, :], TMP[j][:], ACT.Copy).then_inc(sem("hid_hi"), 1)
                            half_scale(l, 2)
                    else:
                        for m in range(KT):
                            if m % 2 == 0:
                                round_units(U[("down", l, a, m)] + 1)
                            if l == 0 and a == len(DOWN_K) - 1:
                                was_read(act, ("down", l, a, m))
                                square("mix1", m, X[:, m, :])
                            half_scale(l, 1)
                            if (l, a) == LAST_DOWN and m:
                                output_copy(m - 1)

            def output_copy(k):
                n = ("y", k)
                filled(act, n)
                for bank, t, e in ((0, 0, 3), (1, 3, QT)):
                    ins = A(YROWS[:, t:e, k * P:(k + 1) * P], tile2(n)[:, bank, 0:(e - t) * P].rearrange("p (t c) -> p t c", c=P), ACT.Copy)
                ins.then_inc(free_of(n), 1)

            ffn(0)
            A(WTH[:], WTAP[:], ACT.Copy).then_inc(sem("wth_ready"), 1)
            spread_copy(("rb", "mix1"), RSTD, QT)
            apply("mix1", 1, 0)

            def tap_diagonals(i, first=0, end=PE_TAPS):
                for j in range(first, end):
                    n = i * PE_TAPS + j
                    if n >= DIAG_SLOTS:
                        tap_done(act, n - DIAG_SLOTS)
                    A(TDH[:, n % DIAG_SLOTS, :], EYE[:], ACT.Copy, scale=WTH[:, i, j:j + 1].bitcast(F32)).then_inc(sem("tap_hi"), 1)

            def gated(i):
                was_read(act, ("a", i))
                A(GPH[i % 2][:], GP[i % 2][:], ACT.Copy).then_inc(sem("gp_hi"), 1)

            def tap_products(i):
                for q in range(POOL_TAPS):
                    j = pe_taps(i) + q
                    n = (POOL_TAPS - 1) * i + q - 1
                    if q == 0:
                        if i >= 2:
                            act.wait_ge(sem("pool_joined"), i - 1)
                    elif n >= 3:
                        act.wait_ge(sem("pool_added"), n - 2)
                    dst = PACC[i % 2] if q == 0 else PROD[n % 3]
                    A(dst[:], GP[i % 2][:, j:j + RUN], ACT.Copy, scale=WTAP[:, i, j:j + 1]).then_inc(sem("tap_scaled"), 1)

            tap_diagonals(0)
            round_units(U[("glu", 1)])
            for i in range(KT):
                n = ("b", i)
                filled(act, n)
                if i >= 2:
                    was_read(act, ("a", i - 2))
                c0 = V2["b_pw1"] + KT + i
                A(row2(ACTV[i % 2][:]), tile2(n)[:, :, 0:HALF], ACT.Sigmoid, bias=VT2[:, c0:c0 + 1]).then_inc(free_of(n), 1)
                gated(i)
                round_units(U[("glu", i)] + 2)
                if i + 1 < KT:
                    tap_diagonals(i + 1)
                else:
                    tap_diagonals(i, PE_TAPS, pe_taps(i))
                tap_products(i)
            A(HST[:, 0:1], ONES[:, 0:1], ACT.Silu)
            for i in range(KT):
                act.wait_ge(sem("y_centred"), i + 1)
                if i >= 4:
                    act.wait_ge(sem("ln_summed"), i // 2 - 1)
                A(LNSQ[i % 4][:], Y[:, i, :], ACT.Square).then_inc(sem("sq_made"), 1)
            spread_copy(("rb", "ln"), RSTD, QT)
            for k in range(KT):
                act.wait_ge(sem("t_ready"), KT * APPLY["ln"] + k + 1)
                if k >= 2:
                    act.wait_ge(sem("h_ready"), KT * APPLY["ln"] + k - 1)
                c0 = V2["ln_b"] + k
                A(ACTV[k % 2][:], SCALED[k % 3][:], ACT.Silu, bias=VT2[:, c0:c0 + 1]).then_inc(sem("swish"), 1)
                act.wait_ge(sem("swish"), k + 1)
                A(HH[:, k, :], ACTV[k % 2][:], ACT.Copy).then_inc(sem("part_hi"), 1)
            for m in range(KT):
                if m % 2 == 0:
                    round_units(U[("pw2", m)] + 1)
                was_read(act, ("pw2", m))
                square("ffn1", m, X[:, m, :])
            ffn(1)
            output_copy(KT - 1)

        @block.vector
        def _(dve):
            V = nc.vector
            n_lo, n_add, n_chain, n_t, n_part, n_bg = [0], [0], [0], [0], [0], [0]

            def link(ins):
                n_chain[0] += 1
                ins.then_inc(sem("dve_chain"), 1)
                dve.wait_ge(sem("dve_chain"), n_chain[0])

            def split_units(upto):
                while n_lo[0] <= min(upto, len(units) - 1):
                    u = n_lo[0]
                    dve.wait_ge(hi_done, u + 1)
                    n = units[u][1]
                    V.tensor_tensor(WL[:, u % 2, 0:n], RAW[:, u % 2, 0:n], WH[:, u % 2, 0:n].bitcast(F32),
                                    ALU.subtract).then_inc(lo_done, 1)
                    n_lo[0] += 1

            def add_sum(m, a, b):
                if n_add[0] and m > 1:
                    dve.wait_ge(sem("sq_added"), n_add[0])
                V.tensor_tensor(SUM[:], a if m == 1 else SUM[:], b, ALU.add).then_inc(sem("sq_added"), 1)
                n_add[0] += 1

            def add_square(norm, m, tiles=KT):
                base = SQ_BASE[norm]
                dve.wait_ge(sem("sq_made"), base + m + 1)
                if m >= 1:
                    add_sum(m, SQ[0][:], SQ[m % 2][:])

            def rsqrt(n):
                link(V.tensor_scalar(RSI[:, 0:n], RS[:, 0, 0:n].bitcast(I32), 1, None, ALU.arith_shift_right))
                link(V.tensor_scalar(RS[:, 1, 0:n].bitcast(I32), RSI[:, 0:n], -1.0, 1597463007.0, ALU.mult, ALU.add))
                for _ in range(3):
                    link(V.tensor_tensor(RS[:, 2, 0:n], RS[:, 1, 0:n], RS[:, 1, 0:n], ALU.mult))
                    link(V.scalar_tensor_tensor(out=RS[:, 3, 0:n], in0=RS[:, 2, 0:n], scalar=-0.5, in1=RS[:, 0, 0:n],
                                                op0=ALU.mult, op1=ALU.mult))
                    link(V.scalar_tensor_tensor(out=RS[:, 1, 0:n], in0=RS[:, 3, 0:n], scalar=1.5, in1=RS[:, 1, 0:n],
                                                op0=ALU.add, op1=ALU.mult))

            def norm(n, dim):
                filled(dve, ("stat", n))
                s = ("stat", n)
                V.tensor_scalar(RS[:, 0, 0:QT], tile2(s)[:, 0, 0:QT], 1.0 / dim, EPS, ALU.mult, ALU.add).then_inc(free_of(s), 1)
                was_read(dve, s)
                inverse_root()

            def inverse_root():
                rsqrt(QT)
                for t in range(QT):
                    V.tensor_scalar(DIAGN[:, t, :], EYE[:], RS[:, 1, t:t + 1], None, ALU.mult).then_inc(sem("diag_ready"), 1)

            def mod_read_chunk(n, ch, t0, tiles, c0=0, give=True):
                l, j = divmod(ch, 6)
                filled(dve, n)
                src = tile2(n)[:, 0, c0:c0 + 2 * tiles].rearrange("p (k s) -> p k s", s=2)
                at = 8 * j + t0
                b = VT1[:, V1["b_mod"] + 48 * l + at:V1["b_mod"] + 48 * l + at + tiles]
                for s in range(2):
                    ins = V.tensor_tensor(MODV[:, l, s, at:at + tiles], src[:, :, s], b, ALU.add)
                if give:
                    ins.then_inc(free_of(n), 1)
                if j in (1, 4) and t0 + tiles == KT:
                    was_read(dve, n)
                    g0 = V1["norm_mix" if j == 1 else "norm_ffn"] + KT * l
                    for s in range(2):
                        ins = V.scalar_tensor_tensor(out=GAIN[:, l, j // 4, s, :], in0=MODV[:, l, s, 8 * j:8 * j + 8], scalar=1.0,
                                                     in1=VT1[:, g0:g0 + KT], op0=ALU.add, op1=ALU.mult)
                    link(ins)

            def half_steps(l, steps):
                for i in range(n_bg[0], n_bg[0] + steps * (l == 0)):
                    j, k = divmod(i, KT)
                    if k == 0 and j >= 2:
                        filled(dve, ("mh", j - 2))
                    dve.wait_ge(bgw_landed[i % BG_SLOTS], 16 * (i // BG_SLOTS + 1))
                    if k:
                        dve.wait_ge(sem("bgw_first"), i)
                    acc, w, c = BGACC[j % 2][:, 0, :], BGW[i % BG_SLOTS][:], SC[:, k, 0:1]
                    if k == 0:
                        ins = V.tensor_scalar(acc, w, c, None, ALU.mult)
                    else:
                        ins = V.scalar_tensor_tensor(out=acc, in0=w, scalar=c, in1=acc, op0=ALU.mult, op1=ALU.add)
                    ins.then_inc(sem("bgw_first"), 1)
                n_bg[0] += steps * (l == 0)

            def mod_half(j):
                mod_read_chunk(("mh", j), FIRST_BG + j // 2, 4 * (j % 2), 4)

            def apply(norm_name, l, half):
                was_read(dve, ("rb", norm_name))

                def scale(k):
                    if k >= 3:
                        dve.wait_ge(sem("h_ready"), KT * APPLY[norm_name] + k - 2)
                    for a, b, s in SEGS:
                        ins = V.scalar_tensor_tensor(out=SCALED[k % 3][:, a:b], in0=X[:, k, a:b], scalar=GAIN[:, l, half, s, k:k + 1],
                                                     in1=RSTD[:, a:b], op0=ALU.mult, op1=ALU.mult)
                    ins.then_inc(sem("t_ready"), 1)
                    n_t[0] += 1

                scale(0)
                for k in range(KT):
                    if k + 1 < KT:
                        scale(k + 1)
                    n_part[0] += 1
                    dve.wait_ge(sem("t_ready"), n_t[0] - (k + 1 < KT))
                    dve.wait_ge(sem("part_hi"), n_part[0])
                    for a, b, s in SEGS:
                        ins = V.scalar_tensor_tensor(out=HL[:, k, a:b], in0=SCALED[k % 3][:, a:b],
                                                     scalar=MODV[:, l, s, 24 * half + k:24 * half + k + 1],
                                                     in1=HH[:, k, a:b].bitcast(F32), op0=ALU.add, op1=ALU.subtract)
                    ins.then_inc(sem("h_ready"), 1)

            def residual(n, m, l, which):
                filled(dve, n)
                for bank, a, b, t, s in PSEGS:
                    g = MODV[:, l, s, 8 * which + m:8 * which + m + 1]
                    ins = V.scalar_tensor_tensor(out=X[:, m, t:t + b - a], in0=tile2(n)[:, bank, a:b], scalar=g,
                                                 in1=X[:, m, t:t + b - a], op0=ALU.mult, op1=ALU.add)
                ins.then_inc(free_of(n), 1)

            V.memset(ONES[:], 1.0).then_inc(sem("ones_set"), 1)
            filled(dve, "vec")
            ps = tile2("vec")
            V.tensor_copy(VT1[:], ps[:, 0, 0:P])
            V.tensor_copy(VT2[:], ps[:, 0, P:P + NV2]).then_inc(free_of("vec"), 1)
            for k in range(KT):
                n = ("x", k)
                filled(dve, n)
                V.tensor_copy(X[:, k, 0:3 * P], tile2(n)[:, 0, 0:3 * P])
                V.tensor_copy(X[:, k, 3 * P:TOK], tile2(n)[:, 1, 0:2 * P]).then_inc(free_of(n), 1)
                if k >= 1:
                    add_square("mix0", k - 1)
            add_square("mix0", KT - 1)
            was_read(dve, "vec")
            link(V.tensor_tensor(GQK[:], VT2[:, V2["gq"]:V2["gq"] + 1], VT2[:, V2["gk"]:V2["gk"] + 1], ALU.mult))
            norm("mix0", D)
            split_units(1)
            filled(dve, "taps")
            V.tensor_copy(WTAP[:].rearrange("p k t -> p (k t)"), tile2("taps")[:, 0, 0:KT * TAPS]).then_inc(free_of("taps"), 1)
            filled(dve, "cache")
            dve.wait_ge(sem("cache_hi"), 1)
            ps = tile2("cache")
            V.tensor_tensor(CKL[:, :, CTX:CTX + PAST], ps[:, 0, 0:KVL].rearrange("p (j t) -> p j t", j=KVT),
                            CKH[:, :, CTX:CTX + PAST].bitcast(F32), ALU.subtract)
            V.tensor_copy(KPRAW[:, CTX:CTX + PAST], ps[:, 0, KVL:KVL + P]).then_inc(free_of("cache"), 1)
            for ch in range(2):
                mod_read_chunk("mods", ch, 0, KT, 16 * ch, ch == 1)
            apply("mix0", 0, 0)
            for m in range(QLT):
                if m % 2 == 0:
                    split_units(U[("dq", m)] + 1)
                add_square("cq", m, QLT)
            split_units(U[("dkv", 0)] + 1)
            for m in range(KVT):
                if m == 1:
                    filled(dve, ("stat", "cq"))
                if m == 0:
                    norm("cq", QL)
                add_square("ck", m, KVT)
            split_units(U[("dkv", 2)] + 1)
            was_read(dve, ("rb", "cq"))

            def query_scale(m):
                if m >= 2:
                    dve.wait_ge(sem("cq_ready"), m - 1)
                g = VT2[:, V2["q_norm"] + m:V2["q_norm"] + m + 1]
                V.scalar_tensor_tensor(out=TMP[m % 2][:], in0=CQRAW[:, m, :], scalar=g, in1=RSTD[:],
                                       op0=ALU.mult, op1=ALU.mult).then_inc(sem("cq_t"), 1)

            query_scale(0)
            for m in range(QLT):
                if m + 1 < QLT:
                    query_scale(m + 1)
                dve.wait_ge(sem("cq_t"), m + 1)
                dve.wait_ge(sem("cq_hi"), m + 1)
                V.tensor_tensor(CQL[:, m, :], TMP[m % 2][:], CQH[:, m, :].bitcast(F32), ALU.subtract).then_inc(sem("cq_ready"), 1)
            dve.wait_ge(sem("cq_ready"), QLT)
            norm("ck", KVL)

            def queries(h):
                split_units(U[("head", min(h + 1, HEADS - 1))])
                n = ("qn", h)
                dve.wait_ge(sem("qn_hi"), h + 1)
                V.scalar_tensor_tensor(out=row2(QNL[:]), in0=tile2(n)[:, :, 0:HALF], scalar=GQK[:, 0:1],
                                       in1=row2(QNH[:]).bitcast(F32), op0=ALU.mult, op1=ALU.subtract).then_inc(free_of(n), 1)
                if h % 2 == 0:
                    n = ("pe", h)
                    dve.wait_ge(sem("pe_sq"), h // 2 + 1)
                    V.tensor_scalar(row2(PEG[:]), tile2(n)[:, :, 0:HALF], VT2[:, V2["gq_pe"]:V2["gq_pe"] + 1], None,
                                    ALU.mult).then_inc(free_of(n), 1)

            def keys(h):
                n = ("kn", h)
                dve.wait_ge(sem("kn_hi"), h + 1)
                k2 = lambda r: r.rearrange("p (b t) -> p b t", b=2)
                V.tensor_tensor(k2(KNL[:]), tile2(n)[:, :, 0:KEYS // 2], k2(KNH[:]).bitcast(F32),
                                ALU.subtract).then_inc(free_of(n), 1)
                if h % 2 == 0:
                    n = ("rot", h)
                    filled(dve, n)
                    V.tensor_tensor(ROPEQ[:], tile2(n)[:, 0, :], SIN[:], ALU.mult).then_inc(free_of(n), 1)
                    was_read(dve, n)
                    was_read(dve, ("pe", h))
                    link(V.tensor_tensor(PEG[:, CTX:TOK], PEG[:, CTX:TOK], COS[:], ALU.mult))
                    V.tensor_tensor(PEG[:, CTX:TOK], PEG[:, CTX:TOK], ROPEQ[:], ALU.add).then_inc(sem("q_rotated"), 1)

            def rotary_low(h):
                if h % 2 == 0:
                    dve.wait_ge(sem("q_rotated"), h // 2 + 1)
                    dve.wait_ge(sem("qp_hi"), h // 2 + 1)
                    V.tensor_tensor(QPL[:], PEG[:], QPH[:].bitcast(F32), ALU.subtract).then_inc(sem("qp_ready"), 1)

            def head_norm(h):
                n = ("hstat", h)
                filled(dve, n)
                V.tensor_copy(HST[:, 0:QT], tile2(n)[:, 0, 0:QT])
                V.tensor_tensor(HST[:, QT:QT + NKT], tile2(n)[:, 0, QT:QT + NKT], KPSS[:], ALU.add).then_inc(free_of(n), 1)
                was_read(dve, n)
                link(V.tensor_scalar(RS[:, 0, 0:QT + NKT], HST[:, 0:QT + NKT], 1.0 / QK, EPS, ALU.mult, ALU.add))
                rsqrt(QT + NKT)
                link(V.tensor_scalar(RQ[h % 2][:], RS[:, 1, 0:QT], QK ** -0.5, None, ALU.mult))
                for t in range(NKT):
                    V.tensor_scalar(DIAGK[t][:], EYE[:], RS[:, 1, QT + t:QT + t + 1], None, ALU.mult).then_inc(sem("diag_ready"), 1)

            def values(h):
                n = ("v", h)
                dve.wait_ge(sem("v_hi"), h + 1)
                v2 = lambda r: r.rearrange("p (b j) v -> p b (j v)", b=2)
                V.tensor_tensor(v2(VL[:]), tile2(n)[:, :, 0:3 * P], v2(VH[:]).bitcast(F32), ALU.subtract).then_inc(free_of(n), 1)

            def split_output(k):
                dve.wait_ge(sem("o_hi"), k + 1)
                V.tensor_tensor(OL[:, k, :], O[:, k, :], OH[:, k, :].bitcast(F32), ALU.subtract).then_inc(sem("o_split"), 1)

            queries(0)
            was_read(dve, ("rb", "ck"))
            for m in range(KVT):
                g = VT2[:, V2["kv_norm"] + m:V2["kv_norm"] + m + 1]
                V.scalar_tensor_tensor(out=CKRAW[:, m, :], in0=CKRAW[:, m, :], scalar=g, in1=RSTD[:],
                                       op0=ALU.mult, op1=ALU.mult).then_inc(sem("ck_t"), 1)
            for m in range(KVT):
                dve.wait_ge(sem("ck_t"), m + 1)
                dve.wait_ge(sem("ck_hi"), m + 1)
                V.tensor_tensor(CKL[:, m, 0:CTX], CKRAW[:, m, 0:CTX], CKH[:, m, 0:CTX].bitcast(F32), ALU.subtract)
                V.tensor_tensor(CKL[:, m, CTX + PAST:KEYS], CKRAW[:, m, CTX:TOK], CKH[:, m, CTX + PAST:KEYS].bitcast(F32),
                                ALU.subtract).then_inc(sem("ck_ready"), 1)
            filled(dve, "kpstat")
            V.tensor_copy(KPSS[:], tile2("kpstat")[:, 0, 0:NKT]).then_inc(free_of("kpstat"), 1)
            was_read(dve, "kpstat")
            V.tensor_scalar(KPSQ[:], KPRAW[:], VT2[:, V2["gk_pe"]:V2["gk_pe"] + 1], None, ALU.mult).then_inc(sem("kpg_ready"), 1)
            dve.wait_ge(sem("kpg_ready"), 1)
            dve.wait_ge(sem("rope_landed"), 32)
            filled(dve, "kprot")
            V.tensor_tensor(ROPET[:], tile2("kprot")[:, 0, :], SIN[:], ALU.mult).then_inc(free_of("kprot"), 1)
            was_read(dve, "kprot")
            late = KPSQ[:, KEYS - LAT:KEYS]
            link(V.tensor_tensor(late, late, COS[:], ALU.mult))
            V.tensor_tensor(late, late, ROPET[:], ALU.add).then_inc(sem("kp_rotated"), 1)
            dve.wait_ge(sem("kp_rotated"), 1)
            dve.wait_ge(sem("kp_hi"), 1)
            V.tensor_tensor(KPL[:], KPSQ[:], KPH[:].bitcast(F32), ALU.subtract).then_inc(sem("kp_ready"), 1)

            keys(0)
            rotary_low(0)
            head_norm(0)
            values(0)
            for h in range(HEADS):
                was_read(dve, ("rk", h))

                def peak(t):
                    n = ("s", h, t)
                    filled(dve, n)
                    if t == 0:
                        o, i0, i1 = PROBC[:], tile2(n)[:, 0, 0:CTX], RK[:, 0:CTX]
                    else:
                        o, i0, i1 = row2(PROB[:, t - 1, :]), tile2(n)[:, :, 0:HALF], row2(RK[:, CTX:KEYS])
                    V.tensor_tensor_reduce(out=o, in0=i0, in1=i1, scale=1.0, scalar=-3.0e38, op0=ALU.mult, op1=ALU.max,
                                           accum_out=MAX8[:, t:t + 1]).then_inc(free_of(n), 1)
                    was_read(dve, n)
                    V.scalar_tensor_tensor(out=NB8[:, t:t + 1], in0=MAX8[:, t:t + 1], scalar=-1.0, in1=RQ[h % 2][:, t:t + 1],
                                           op0=ALU.mult, op1=ALU.mult).then_inc(sem("nb_ready"), 1)

                def normalise(t):
                    dve.wait_ge(sem("exp_done"), QT * h + t + 1)
                    link(V.reciprocal(REC8[:, t:t + 1], SUM8[:, t:t + 1]))
                    p = PROBC[:] if t == 0 else PROB[:, t - 1, :]
                    V.tensor_scalar(p, p, REC8[:, t:t + 1], None, ALU.mult).then_inc(sem("prob_ready"), 1)

                for t in range(QT):
                    peak(t)
                    if t:
                        normalise(t - 1)
                normalise(QT - 1)
                if h + 1 < HEADS:
                    queries(h + 1)
                for t in range(QT):
                    n = ("pt", h, t)
                    dve.wait_ge(sem("pt_hi"), QT * h + t + 1)
                    if t == 0:
                        V.tensor_tensor(PTCL[:], tile2(n)[:, 0, 0:P], PTCH[:].bitcast(F32), ALU.subtract).then_inc(free_of(n), 1)
                    else:
                        g, c0 = (t - 1) // 2, (t - 1) % 2 * P
                        for bank, k0, k1 in ((0, 0, 3), (1, 3, 5)):
                            ins = V.tensor_tensor(PTL[:, g, k0:k1, c0:c0 + P],
                                                  tile2(n)[:, bank, 0:(k1 - k0) * P].rearrange("p (k q) -> p k q", q=P),
                                                  PTH[:, g, k0:k1, c0:c0 + P].bitcast(F32), ALU.subtract)
                        ins.then_inc(free_of(n), 1)
                if h + 1 < HEADS:
                    keys(h + 1)
                    head_norm(h + 1)
                    rotary_low(h + 1)
                else:
                    split_units(U[("wo", 0)])
                    for k in range(HEADS - 1):
                        split_output(k)
                if h < N_ROWS:
                    mod_read_chunk(("mb", h), 2 + h // 2, 4 * (h % 2), 4)
                if h + 1 < HEADS:
                    values(h + 1)
            filled(dve, ("o", HEADS - 1, 2))
            split_output(HEADS - 1)

            def residuals(name, l, which, norm_name, step=None):
                for m in range(KT):
                    if m % 2 == 0:
                        split_units(U[name(m)] + 1)
                    residual(name(m), m, l, which)
                    if step is not None:
                        half_steps(l, 1)
                        if l == 0 and m == 0:
                            mod_half(step - 1)
                    if norm_name and m:
                        add_square(norm_name, m - 1)
                if norm_name:
                    add_square(norm_name, KT - 1)

            residuals(lambda m: ("wo", m), 0, 2, "ffn0")

            def ffn(l):
                n = f"ffn{l}"
                norm(n, D)
                apply(n, l, 1)
                for step, (kind, a, f0) in enumerate(ffn_steps()):
                    if kind == "pair":
                        split_units(U[("gate", l, a)] + 1)
                        half_steps(l, 2)
                        split_units(U[("up", l, a)] + 1)
                        half_steps(l, 2)
                        if l == 0 and step:
                            mod_half(step - 1)
                        for j in range(2):
                            n = ("up", l, a + j)
                            was_read(dve, ("gate", l, a + j))
                            filled(dve, n)
                            V.tensor_tensor(row2(TMP[j][:]), tile2(n)[:, :, 0:HALF], row2(ACTV[j][:]), ALU.mult).then_inc(free_of(n), 1)
                            half_steps(l, 2)
                        for j in range(2):
                            was_read(dve, ("up", l, a + j))
                            dve.wait_ge(sem("hid_hi"), FT * l + a + j + 1)
                            V.tensor_tensor(HIDL[:, (a + j) % HID_SLOTS, :], TMP[j][:], HIDH[:, (a + j) % HID_SLOTS, :].bitcast(F32),
                                            ALU.subtract).then_inc(sem("hid_ready"), 1)
                    else:
                        residuals(lambda m: ("down", l, a, m), l, 5, "mix1" if l == 0 and a == len(DOWN_K) - 1 else None, step)

            ffn(0)
            norm("mix1", D)
            mod_half(N_HALF - 1)
            dve.wait_ge(sem("wth_ready"), 1)
            V.tensor_tensor(WTL[:], WTAP[:], WTH[:].bitcast(F32), ALU.subtract).then_inc(sem("taps_split"), 1)
            for i in range(2):
                link(V.memset(GP[i][:], 0.0))
            apply("mix1", 1, 0)

            def gated(i):
                was_read(dve, ("b", i))
                n = ("a", i)
                filled(dve, n)
                if i >= 2:
                    dve.wait_ge(sem("tap_scaled"), POOL_TAPS * (i - 1))
                for bank, a, b, t, s in PSEGS:
                    to = t + PAD if s == 0 else t + 2 * PAD
                    ins = V.scalar_tensor_tensor(out=GP[i % 2][:, to:to + b - a], in0=tile2(n)[:, bank, a:b],
                                                 scalar=VT2[:, V2["b_pw1"] + i:V2["b_pw1"] + i + 1],
                                                 in1=ACTV[i % 2][:, t:t + b - a], op0=ALU.add, op1=ALU.mult)
                ins.then_inc(free_of(n), 1)
                was_read(dve, n)
                first_tap(i)
                taps(i, 1, 2)
                dve.wait_ge(sem("gp_hi"), i + 1)
                V.tensor_tensor(GPL[i % 2][:], GP[i % 2][:], GPH[i % 2][:].bitcast(F32), ALU.subtract).then_inc(sem("gp_lo"), 1)

            def first_tap(i):
                j = pe_taps(i) + POOL_TAPS
                link(V.tensor_scalar(YACC[i % 2][:], GP[i % 2][:, j:j + RUN], WTAP[:, i, j:j + 1],
                                     VT2[:, V2["b_dw"] + i:V2["b_dw"] + i + 1], ALU.mult, ALU.add))

            def taps(i, first, end):
                acc, g = YACC[i % 2], GP[i % 2]
                j0 = pe_taps(i) + POOL_TAPS
                for j in range(j0 + first, min(j0 + end, TAPS)):
                    link(V.scalar_tensor_tensor(out=acc[:], in0=g[:, j:j + RUN], scalar=WTAP[:, i, j:j + 1],
                                                in1=acc[:], op0=ALU.mult, op1=ALU.add))

            def joined(i):
                n = ("cv", i)
                filled(dve, n)
                for bank, a, b, t in CSEGS:
                    at = a + bank * CHALF
                    ins = V.tensor_tensor(Y[:, i, t:t + b - a], tile2(n)[:, bank, a:b], YACC[i % 2][:, at:at + b - a], ALU.add)
                ins.then_inc(free_of(n), 1)

            split_units(U[("glu", 1)])
            gated(0)
            for i in range(KT):
                split_units(U[("glu", i)] + 2)
                if i:
                    joined(i - 1)
                cut = 8 if i == KT - 2 else TAPS
                taps(i, 2, cut)
                if i + 1 < KT:
                    gated(i + 1)
                taps(i, cut, TAPS)
            joined(KT - 1)
            was_read(dve, ("cv", KT - 1))
            dve.wait_ge(sem("pool_added"), (POOL_TAPS - 1) * KT)
            for bank, a, b, t in CSEGS:
                at = a + bank * CHALF
                y = Y[:, KT - 1, t:t + b - a]
                ins = V.tensor_tensor(y, y, PACC[(KT - 1) % 2][:, at:at + b - a], ALU.add)
            link(ins)
            n_add[0] += KT - 2
            add_sum(KT - 1, None, Y[:, KT - 1, :])
            for s in range(2):
                link(V.tensor_tensor(GB[:, s, :], MODV[:, 1, s, 16:24], VT2[:, V2["b_pw2"]:V2["b_pw2"] + KT], ALU.mult))
            filled(dve, "mu")
            for i in range(KT):
                V.scalar_tensor_tensor(out=row2(Y[:, i, :]), in0=tile2("mu")[:, :, 0:HALF], scalar=-1.0 / D,
                                       in1=row2(Y[:, i, :]), op0=ALU.mult, op1=ALU.add).then_inc(sem("y_centred"), 1)
            V.tensor_copy(MAX8[:, 0:1], tile2("mu")[:, 0, 0:1]).then_inc(free_of("mu"), 1)
            filled(dve, ("stat", "ln"))
            V.tensor_reduce(out=LNSS[:], in_=tile2(("stat", "ln"))[:, 0, 0:QT * KT // 2].rearrange("p (t k) -> p t k", k=KT // 2),
                            op=ALU.add, axis=mybir.AxisListType.X).then_inc(free_of(("stat", "ln")), 1)
            was_read(dve, ("stat", "ln"))
            link(V.tensor_scalar(RS[:, 0, 0:QT], LNSS[:], 1.0 / D, EPS, ALU.mult, ALU.add))
            inverse_root()
            was_read(dve, ("rb", "ln"))

            def ln_scale(k):
                V.scalar_tensor_tensor(out=SCALED[k % 3][:], in0=Y[:, k, :], scalar=VT2[:, V2["ln_g"] + k:V2["ln_g"] + k + 1],
                                       in1=RSTD[:], op0=ALU.mult, op1=ALU.mult).then_inc(sem("t_ready"), 1)

            ln_scale(0)
            for k in range(KT):
                if k + 1 < KT:
                    if k >= 2:
                        dve.wait_ge(sem("swish"), k - 1)
                    ln_scale(k + 1)
                n_part[0] += 1
                dve.wait_ge(sem("part_hi"), n_part[0])
                V.tensor_tensor(HL[:, k, :], ACTV[k % 2][:], HH[:, k, :].bitcast(F32), ALU.subtract).then_inc(sem("h_ready"), 1)
            n_t[0] += KT
            for k in range(KT):
                for a, b, s in SEGS:
                    ins = V.tensor_scalar(X[:, k, a:b], X[:, k, a:b], GB[:, s, k:k + 1], None, ALU.add)
                link(ins)
            residuals(lambda m: ("pw2", m), 1, 2, "ffn1")
            ffn(1)


_INS = ["x_prompt", "x_sample", "cache_ckv", "cache_kpe", "c", "c_ctx", "w_mod", "b_mod", "norm_mix", "norm_ffn",
        "mla_w_dq", "mla_q_norm", "mla_w_uq", "mla_w_dkv", "mla_kv_norm", "mla_w_ukv", "mla_q_hnorm", "mla_k_hnorm",
        "mla_w_o", "conv_w_pw1", "conv_b_pw1", "conv_w_dw", "conv_b_dw", "conv_ln_g", "conv_ln_b", "conv_w_pw2",
        "conv_b_pw2", "ffn_w_gate", "ffn_w_up", "ffn_w_down"]
_OUTS = [((1, CTX, D), "float32"), ((1, LAT, D), "float32"), ((1, 1, CTX, KVL), "float32"), ((1, 1, CTX, ROPE), "float32")]


def kernel(**inputs):
    import concourse.bacc as bacc
    from concourse.bass_utils import run_bass_kernel_spmd

    nc = bacc.Bacc("TRN2", target_bir_lowering=False, num_devices=1)
    arrays, args = {}, []
    for name in _INS:
        a = np.ascontiguousarray(inputs[name])
        arrays[f"in_{name}"] = a
        args.append(nc.dram_tensor(f"in_{name}", a.shape, mybir.dt.from_np(a.dtype), kind="ExternalInput").ap())
    for i, (shape, dtype) in enumerate(_OUTS):
        args.append(nc.dram_tensor(f"out_{i}", shape, mybir.dt.from_np(np.dtype(dtype)), kind="ExternalOutput").ap())
    program(nc, *args)
    r = run_bass_kernel_spmd(nc, [arrays], core_ids=[0])
    return tuple(r.results[0][f"out_{i}"] for i in range(len(_OUTS)))
```
